# Optimizing a Trainium2 kernel written in Bass

```python
import math
import jax
import jax.numpy as jnp
from jax import lax
import numpy as np

D_MODEL = 1024
BATCH = 1
SEQ = 128
DEPTH = 2
DEC_BATCH = 1
DEC_SEQ = 128
PAST_LEN = 128

GRID_W = 64
N_EVEN = (DEPTH + 1) // 2
N_ODD = DEPTH // 2
EPS = 1e-6
A_WIDTH = D_MODEL // 2
A_HEADS = 4
A_DK = A_WIDTH // A_HEADS
A_DV = A_WIDTH // A_HEADS
CHUNK = 64
B_HEAD_DIM = 64
B_HEADS = (D_MODEL // 2) // B_HEAD_DIM
B_KV_HEADS = 2
Q_BLOCK = 128
ROPE_THETA = 10000.0
ROPE_PAIRS = B_HEAD_DIM // 4
AB_IN = 5 * A_WIDTH + (B_HEADS + 2 * B_KV_HEADS) * B_HEAD_DIM
AB_OUT = A_WIDTH + B_HEADS * B_HEAD_DIM
HY_BANDS = 16
HY_EMB = 1 + 2 * HY_BANDS
HY_FFN = 64
HY_SHORT = 3
HY_DECAY_TARGET = 1e-2
HY_FAST_PCT = 0.3
HY_SLOW_PCT = 1.5
N_EXPERTS = 16
N_GROUPS = 4
EXPERTS_PER_GROUP = N_EXPERTS // N_GROUPS
TOP_K = 2
D_EXPERT = 512

kernel_name = 'hybrid_diffusion_hgrn2_gqa_hyena_moe_step'

def _rms(x, g):
    xf = x.astype(jnp.float32)
    y = xf * lax.rsqrt(jnp.mean(xf * xf, axis=-1, keepdims=True) + EPS)
    return (y * g.astype(jnp.float32)).astype(x.dtype)

def _heads(a, n):
    b_, l_, _ = a.shape
    return a.reshape(b_, l_, n, -1).transpose(0, 2, 1, 3)

def hgrn_scan(q, log_f, inp, s0):
    bn, hn, L, dk = q.shape
    dv = inp.shape[-1]
    n = L // CHUNK
    k = -jnp.expm1(log_f)
    ch = lambda a: a.reshape(bn, hn, n, CHUNK, a.shape[-1])
    qc, kc, vc = ch(q), ch(k), ch(inp)
    b = jnp.cumsum(ch(log_f), axis=3)
    b_mid = b[:, :, :, CHUNK // 2:CHUNK // 2 + 1]
    att = jnp.einsum('bhnik,bhnjk->bhnij', qc * jnp.exp(b - b_mid), kc * jnp.exp(b_mid - b))
    causal = jnp.tril(jnp.ones((CHUNK, CHUNK), dtype=bool))
    o_intra = jnp.einsum('bhnij,bhnjv->bhniv', jnp.where(causal, att, 0.0), vc)
    b_last = b[:, :, :, -1:]
    chunk_state = jnp.einsum('bhnjk,bhnjv->bhnkv', kc * jnp.exp(b_last - b), vc)
    chunk_decay = jnp.exp(b_last[:, :, :, 0])

    def step(s, xs):
        dec, upd = xs
        return dec[..., None] * s + upd, s

    s_fin, s_prev = lax.scan(step, s0, (jnp.moveaxis(chunk_decay, 2, 0), jnp.moveaxis(chunk_state, 2, 0)))
    o_inter = jnp.einsum('bhnik,bhnkv->bhniv', qc * jnp.exp(b), jnp.moveaxis(s_prev, 0, 2))
    return (o_intra + o_inter).reshape(bn, hn, L, dv), s_fin

def rope_2d(x, row, col):
    inv = ROPE_THETA ** (-jnp.arange(ROPE_PAIRS, dtype=jnp.float32) / ROPE_PAIRS)

    def rot(xa, p):
        ang = p.astype(jnp.float32)[:, None] * inv
        cos = jnp.cos(ang)[None, :, None, :]
        sin = jnp.sin(ang)[None, :, None, :]
        x1, x2 = jnp.split(xa.astype(jnp.float32), 2, axis=-1)
        return jnp.concatenate([x1 * cos - x2 * sin, x2 * cos + x1 * sin], axis=-1)

    xr, xc = jnp.split(x, 2, axis=-1)
    return jnp.concatenate([rot(xr, row), rot(xc, col)], axis=-1).astype(x.dtype)

def attend(q, k, v):
    bn, hq, s, hd = q.shape
    hkv = k.shape[1]
    g = hq // hkv
    nb = s // Q_BLOCK
    qb = jnp.moveaxis(q.reshape(bn, hkv, g, nb, Q_BLOCK, hd), 3, 0)
    scale = hd ** -0.5

    def block(qi):
        sc = jnp.einsum('bhgqd,bhkd->bhgqk', qi, k).astype(jnp.float32) * scale
        p = jax.nn.softmax(sc, axis=-1).astype(v.dtype)
        return jnp.einsum('bhgqk,bhkd->bhgqd', p, v)

    o = lax.map(block, qb)
    return jnp.moveaxis(o, 0, 3).reshape(bn, hq, s, hd)

def ab_mixer(h, w_in, lb, onorm_g, qn_g, kn_g, w_out, s0, ctx_k, ctx_v, pos):
    f32 = jnp.float32
    bn, L, _ = h.shape
    sizes = [A_WIDTH] * 5 + [B_HEADS * B_HEAD_DIM, B_KV_HEADS * B_HEAD_DIM, B_KV_HEADS * B_HEAD_DIM]
    z = h @ w_in
    qa, zf, zb, ia, ga, qb, kb, vb = jnp.split(z, np.cumsum(sizes)[:-1].tolist(), axis=-1)
    q_h = _heads(qa.astype(f32), A_HEADS)
    i_h = _heads(ia.astype(f32), A_HEADS)
    lf_f = _heads(jnp.log(lb[0] + (1.0 - lb[0]) * jax.nn.sigmoid(zf.astype(f32))), A_HEADS)
    lf_b = _heads(jnp.log(lb[1] + (1.0 - lb[1]) * jax.nn.sigmoid(zb.astype(f32))), A_HEADS)
    s0 = s0.astype(f32)
    o_f, s_f = hgrn_scan(q_h, lf_f, i_h, s0[:, 0])
    o_r, s_b = hgrn_scan(q_h[:, :, ::-1], lf_b[:, :, ::-1], i_h[:, :, ::-1], s0[:, 1])
    o_a = (o_f + o_r[:, :, ::-1]).transpose(0, 2, 1, 3)
    o_a = o_a * lax.rsqrt(jnp.mean(o_a * o_a, axis=-1, keepdims=True) + EPS)
    o_a = (o_a * onorm_g.astype(f32).reshape(A_HEADS, A_DV)).reshape(bn, L, A_WIDTH)
    o_a = o_a.astype(h.dtype) * jax.nn.silu(ga)
    q = _rms(qb.reshape(bn, L, B_HEADS, B_HEAD_DIM), qn_g)
    k = _rms(kb.reshape(bn, L, B_KV_HEADS, B_HEAD_DIM), kn_g)
    v = vb.reshape(bn, L, B_KV_HEADS, B_HEAD_DIM)
    if pos is not None:
        q = rope_2d(q, pos[0], pos[1])
        k = rope_2d(k, pos[0], pos[1])
    q = q.transpose(0, 2, 1, 3)
    k = k.transpose(0, 2, 1, 3)
    v = v.transpose(0, 2, 1, 3)
    if ctx_k is None:
        keys, vals = k, v
    else:
        keys = jnp.concatenate([k, ctx_k.astype(k.dtype)], axis=2)
        vals = jnp.concatenate([v, ctx_v.astype(v.dtype)], axis=2)
    o_attn = attend(q, keys, vals).transpose(0, 2, 1, 3).reshape(bn, L, B_HEADS * B_HEAD_DIM)
    out = jnp.concatenate([o_a, o_attn], axis=-1) @ w_out
    return out, jnp.stack([s_f, s_b], axis=1), k, v

def hyena_filter(L, w1, b1, w2, b2, w3, freq):
    f32 = jnp.float32
    t = jnp.linspace(0.0, 1.0, L, dtype=f32)[:, None]
    w = 2.0 * np.pi * jnp.arange(L, dtype=f32)[:, None] / L
    fb = jnp.linspace(1e-4, HY_BANDS - 1, HY_BANDS, dtype=f32)[None, :]
    z = jnp.concatenate([t, jnp.cos(fb * w), -jnp.sin(fb * w)], axis=-1)
    fr = freq.astype(f32)
    hd = jnp.sin(fr * (z @ w1.astype(f32) + b1.astype(f32)))
    hd = jnp.sin(fr * (hd @ w2.astype(f32) + b2.astype(f32)))
    filt = (hd @ w3.astype(f32)).reshape(L, 2, D_MODEL)
    lo = math.log(HY_DECAY_TARGET) / HY_SLOW_PCT
    hi = math.log(HY_DECAY_TARGET) / HY_FAST_PCT
    deltas = jnp.abs(jnp.linspace(lo, hi, D_MODEL, dtype=f32))
    decay = jnp.exp(-t * deltas)
    return filt * decay[:, None, :]

def bidir_long_conv(u, filt):
    L = u.shape[1]
    k2 = jnp.concatenate([filt[:, 0], jnp.zeros((1, D_MODEL), jnp.float32), filt[:0:-1, 1]], axis=0)
    uf = jnp.fft.rfft(u.astype(jnp.float32), n=2 * L, axis=1)
    kf = jnp.fft.rfft(k2, n=2 * L, axis=0)
    return jnp.fft.irfft(uf * kf[None], n=2 * L, axis=1)[:, :L]

def hyena(h, in_w, in_b, conv_w, conv_b, w1, b1, w2, b2, w3, freq, dskip, out_w):
    bn, L, _ = h.shape
    u = h @ in_w + in_b
    up = jnp.pad(u, ((0, 0), (1, 1), (0, 0)))
    u = up[:, :-2] * conv_w[0] + up[:, 1:-1] * conv_w[1] + up[:, 2:] * conv_w[2] + conv_b
    x0, x1, v = jnp.split(u, 3, axis=-1)
    zz = v * x1
    filt = hyena_filter(L, w1, b1, w2, b2, w3, freq)
    y = bidir_long_conv(zz, filt).astype(h.dtype) + zz * dskip
    return (x0 * y) @ out_w

def moe(h, router_w, router_b, w_gate, w_up, w_down):
    f32 = jnp.float32
    bn, L, d = h.shape
    t = h.reshape(bn * L, d)
    scores = jax.nn.softmax((t @ router_w).astype(f32), axis=-1)
    biased = (scores + router_b.astype(f32)).reshape(-1, N_GROUPS, EXPERTS_PER_GROUP)
    group_score = lax.top_k(biased, TOP_K)[0].sum(-1)
    grp = jnp.argmax(group_score, axis=-1)
    in_grp = jnp.take_along_axis(biased, grp[:, None, None], axis=1)[:, 0]
    _, local = lax.top_k(in_grp, TOP_K)
    idx = grp[:, None] * EXPERTS_PER_GROUP + local
    wsel = jnp.take_along_axis(scores, idx, axis=-1)
    wsel = wsel / jnp.sum(wsel, axis=-1, keepdims=True)
    gates = jnp.sum(jax.nn.one_hot(idx, N_EXPERTS, dtype=f32) * wsel[..., None], axis=1)
    a = jnp.einsum('td,edf->etf', t, w_gate)
    b = jnp.einsum('td,edf->etf', t, w_up)
    hid = jax.nn.silu(a) * b * gates.T[:, :, None].astype(t.dtype)
    out = jnp.einsum('etf,efd->td', hid, w_down)
    return out.reshape(bn, L, d)

def setup_inputs(seed: int = 0) -> dict:
    key = jax.random.key(seed)
    keys = iter(jax.random.split(key, 48))
    nrm = lambda shape, scale: jax.random.normal(next(keys), shape, jnp.float32) * scale
    D = D_MODEL
    return {
        'x_prompt': nrm((BATCH, SEQ, D), 1.0),
        'x_sample': nrm((DEC_BATCH, DEC_SEQ, D), 1.0),
        'cache_k': nrm((DEC_BATCH, N_EVEN, B_KV_HEADS, PAST_LEN, B_HEAD_DIM), 1.0),
        'cache_v': nrm((DEC_BATCH, N_EVEN, B_KV_HEADS, PAST_LEN, B_HEAD_DIM), 1.0),
        'state_hgrn': nrm((DEC_BATCH, N_EVEN, 2, A_HEADS, A_DK, A_DV), 0.5),
        'c': nrm((DEC_BATCH, D), 1.0),
        'c_ctx': nrm((D,), 1.0),
        'norm_g': 1.0 + nrm((DEPTH, 2, D), 0.02),
        'mod_w': nrm((DEPTH, D, 6 * D), 0.5 * D ** -0.5),
        'mod_b': nrm((DEPTH, 6 * D), 0.02),
        'ab_in_w': nrm((N_EVEN, D, AB_IN), D ** -0.5),
        'hgrn_lb': nrm((N_EVEN + 1, 2, A_WIDTH), 0.1),
        'hgrn_onorm_g': 1.0 + nrm((N_EVEN, A_WIDTH), 0.02),
        'attn_qnorm_g': 1.0 + nrm((N_EVEN, B_HEAD_DIM), 0.02),
        'attn_knorm_g': 1.0 + nrm((N_EVEN, B_HEAD_DIM), 0.02),
        'ab_out_w': nrm((N_EVEN, AB_OUT, D), AB_OUT ** -0.5),
        'hy_in_w': nrm((N_ODD, D, 3 * D), D ** -0.5),
        'hy_in_b': nrm((N_ODD, 3 * D), 0.02),
        'hy_conv_w': nrm((N_ODD, HY_SHORT, 3 * D), HY_SHORT ** -0.5),
        'hy_conv_b': nrm((N_ODD, 3 * D), 0.02),
        'hy_f_w1': nrm((N_ODD, HY_EMB, HY_FFN), HY_EMB ** -0.5),
        'hy_f_b1': nrm((N_ODD, HY_FFN), 0.02),
        'hy_f_w2': nrm((N_ODD, HY_FFN, HY_FFN), HY_FFN ** -0.5),
        'hy_f_b2': nrm((N_ODD, HY_FFN), 0.02),
        'hy_f_w3': nrm((N_ODD, HY_FFN, 2 * D), 0.01),
        'hy_f_freq': 1.0 + nrm((N_ODD, HY_FFN), 0.02),
        'hy_dskip': nrm((N_ODD, D), 0.5),
        'hy_out_w': nrm((N_ODD, D, D), D ** -0.5),
        'router_w': nrm((D, N_EXPERTS), D ** -0.5),
        'router_b': nrm((N_EXPERTS,), 0.01),
        'moe_w_gate': nrm((DEPTH, N_EXPERTS, D, D_EXPERT), D ** -0.5),
        'moe_w_up': nrm((DEPTH, N_EXPERTS, D, D_EXPERT), D ** -0.5),
        'moe_w_down': nrm((DEPTH, N_EXPERTS, D_EXPERT, D), D_EXPERT ** -0.5),
    }

def reference(x_prompt, x_sample, cache_k, cache_v, state_hgrn, c, c_ctx, norm_g, mod_w, mod_b,
              ab_in_w, hgrn_lb, hgrn_onorm_g, attn_qnorm_g, attn_knorm_g, ab_out_w,
              hy_in_w, hy_in_b, hy_conv_w, hy_conv_b, hy_f_w1, hy_f_b1, hy_f_w2, hy_f_b2,
              hy_f_w3, hy_f_freq, hy_dskip, hy_out_w, router_w, router_b,
              moe_w_gate, moe_w_up, moe_w_down):
    f32 = jnp.float32
    lb_all = jnp.cumsum(jax.nn.softmax(hgrn_lb.astype(f32), axis=0), axis=0)

    def trunk(x, cond, latent):
        bn, L, _ = x.shape
        if latent:
            rows = L // GRID_W
            pos = (jnp.repeat(jnp.arange(rows), GRID_W), jnp.tile(jnp.arange(GRID_W), rows))
        else:
            pos = None
        ks, vs, ss = [], [], []
        for l in range(DEPTH):
            j = l // 2
            mod = (jax.nn.silu(cond) @ mod_w[l] + mod_b[l])[:, None, :]
            sh1, sc1, g1, sh2, sc2, g2 = jnp.split(mod, 6, axis=-1)
            h = _rms(x, norm_g[l, 0]) * (1.0 + sc1) + sh1
            if l % 2 == 0:
                if latent:
                    s0, ck, cv = state_hgrn[:, j], cache_k[:, j], cache_v[:, j]
                else:
                    s0, ck, cv = jnp.zeros((bn, 2, A_HEADS, A_DK, A_DV), f32), None, None
                out, s_fin, k_c, v_c = ab_mixer(h, ab_in_w[j], lb_all[j], hgrn_onorm_g[j],
                                                attn_qnorm_g[j], attn_knorm_g[j], ab_out_w[j],
                                                s0, ck, cv, pos)
                if not latent:
                    ks.append(k_c)
                    vs.append(v_c)
                    ss.append(s_fin)
            else:
                out = hyena(h, hy_in_w[j], hy_in_b[j], hy_conv_w[j], hy_conv_b[j], hy_f_w1[j],
                            hy_f_b1[j], hy_f_w2[j], hy_f_b2[j], hy_f_w3[j], hy_f_freq[j],
                            hy_dskip[j], hy_out_w[j])
            x = x + g1 * out
            h = _rms(x, norm_g[l, 1]) * (1.0 + sc2) + sh2
            x = x + g2 * moe(h, router_w, router_b, moe_w_gate[l], moe_w_up[l], moe_w_down[l])
        return x, ks, vs, ss

    y_prompt, ks, vs, ss = trunk(x_prompt, c_ctx[None, :], False)
    y_sample, _, _, _ = trunk(x_sample, c, True)
    new_cache_k = jnp.stack(ks, axis=1)
    new_cache_v = jnp.stack(vs, axis=1)
    new_state_hgrn = jnp.stack(ss, axis=1).astype(x_prompt.dtype)
    return (y_prompt, y_sample, new_cache_k, new_cache_v, new_state_hgrn)


_drawn_inputs = setup_inputs


def setup_inputs(seed=0):
    import zlib

    import numpy as np

    out = dict(_drawn_inputs(seed))
    spreads = {}
    factors = {'state_hgrn': 3.006,
     'hgrn_onorm_g': 8.0,
     'attn_qnorm_g': 8.0,
     'attn_knorm_g': 2.88,
     'hy_in_b': 3.507,
     'hy_conv_b': 8.0,
     'hy_f_b1': 3.897,
     'hy_f_b2': 8.0,
     'hy_f_freq': 8.0,
     'cache_k': 8.0,
     'cache_v': 8.0}
    for name, (base, spread) in spreads.items():
        noise = np.random.default_rng([zlib.crc32(name.encode()), seed]).standard_normal(out[name].shape)
        drawn = base * np.exp(spread * noise) if base else spread * noise
        out[name] = jnp.asarray(drawn.astype(out[name].dtype))
    for name, factor in factors.items():
        out[name] = (out[name] * factor).astype(out[name].dtype)
    return out
```

```python
from contextlib import ExitStack

import numpy as np

import concourse.bass as bass
from concourse import mybir

F32 = mybir.dt.float32
BF16 = mybir.dt.bfloat16
U32 = mybir.dt.uint32
I32 = mybir.dt.int32
ALU = mybir.AluOpType
ACT = mybir.ActivationFunctionType
AX = mybir.AxisListType

P = 128
D = 1024
KD = D // P
T = 128
NS = 2
CHUNK = 64
HA = 4
HB = 8
KV = 2
HD = 64
NE = 16
NG = 4
F = 512
KF = F // P
CAP = 64
NPAIR = NE // 2
RING = 6
UNIT = KD * 512
EPS = 1e-6
HY = 64
EMB = 33
ARENA = 17920

CST = {}
CST_N = 0
for _name, _n in [("ident", 128), ("tri", 128), ("mask_f", 64), ("mask_r", 64), ("cos", 64), ("sin", 64),
                  ("slot", CAP), ("tie", 16)]:
    CST[_name] = (CST_N, _n)
    CST_N += _n
HYC = {}
HYC_N = 0
for _name, _n in [("zT", 128), ("fa", 128), ("fb", 128), ("ka0", 128), ("kb0", 128), ("kc0", 128), ("ka1", 128),
                  ("kb1", 128), ("kc1", 128), ("ga", 128), ("gb", 128), ("decay", D)]:
    HYC[_name] = (HYC_N, _n)
    HYC_N += _n


def shape_constants():
    f32 = np.float32
    a = np.zeros((P, CST_N), f32)

    def put(arr, table, name, val):
        o, n = table[name]
        arr[:val.shape[0], o:o + n] = val

    i = np.arange(P)
    put(a, CST, "ident", np.eye(P, dtype=f32))
    put(a, CST, "tri", (i[:, None] < i[None, :]).astype(f32))
    j = i[:, None] % CHUNK
    put(a, CST, "mask_f", (j <= np.arange(CHUNK)[None]).astype(f32))
    put(a, CST, "mask_r", (j >= np.arange(CHUNK)[None]).astype(f32))
    inv = (f32(10000.0) ** (-np.arange(16, dtype=f32) / f32(16))).astype(f32)
    row, col = (i // 64).astype(f32), (i % 64).astype(f32)
    ang = np.stack([row[:, None] * inv, col[:, None] * inv], 1).astype(f32)
    cos, sin = np.cos(ang.astype(np.float64)), np.sin(ang.astype(np.float64))
    put(a, CST, "cos", np.stack([cos, cos], 2).reshape(P, 64).astype(f32))
    put(a, CST, "sin", np.stack([-sin, sin], 2).reshape(P, 64).astype(f32))
    put(a, CST, "slot", np.tile(np.arange(CAP, dtype=f32), (P, 1)))
    tie = (np.arange(4)[None] < np.arange(4)[:, None]).astype(f32).reshape(1, 16)
    put(a, CST, "tie", np.tile(tie, (P, 1)))

    b = np.zeros((P, HYC_N), f32)
    L, N = T, 2 * T
    t = np.linspace(0.0, 1.0, L, dtype=f32)
    w = (2.0 * np.pi * np.arange(L) / L)
    fb = np.linspace(1e-4, 15, 16, dtype=f32).astype(np.float64)
    z = np.concatenate([t[:, None], np.cos(w[:, None] * fb), -np.sin(w[:, None] * fb)], 1)
    put(b, HYC, "zT", z.T.astype(f32))
    n = np.arange(L)[:, None]
    f = np.arange(L)[None]
    ang = 2 * np.pi * n * f / N
    alt = (-1.0) ** n
    fa, fbm = np.cos(ang), np.sin(ang)
    fbm = np.where(f == 0, alt, fbm)
    late = n >= 1
    put(b, HYC, "fa", fa)
    put(b, HYC, "fb", fbm)
    put(b, HYC, "ka0", fa)
    put(b, HYC, "kb0", np.sin(ang))
    put(b, HYC, "kc0", np.where(f == 0, alt, fa))
    put(b, HYC, "ka1", fa * late)
    put(b, HYC, "kb1", -np.sin(ang) * late)
    put(b, HYC, "kc1", np.where(f == 0, alt, fa) * late)
    wgt = np.where(np.arange(L) == 0, 1.0, 2.0)[:, None] / N
    ang = ang.T
    put(b, HYC, "ga", np.cos(ang) * wgt)
    put(b, HYC, "gb", np.where(np.arange(L)[:, None] == 0, alt.T / N, np.sin(ang) * wgt))
    lo, hi = np.log(1e-2) / 1.5, np.log(1e-2) / 0.3
    deltas = np.abs(np.linspace(lo, hi, D, dtype=f32)).astype(np.float64)
    put(b, HYC, "decay", np.exp(-t.astype(np.float64)[:, None] * deltas).astype(f32))
    return a, b


ROWS = {"norm_g": (0, 0, 32), "hgrn_lb": (0, 32, 16), "onorm": (0, 48, 4), "c": (0, 52, 8), "c_ctx": (0, 60, 8),
        "dskip": (0, 68, 8), "hy_in_b": (0, 76, 24), "hy_conv_b": (0, 100, 24), "mod_b": (1, 0, 96),
        "hy_conv_w": (2, 0, 72)}
ROWS_IN_TILE = [124, 96, 72]

AB_UNITS = [("ab", 512), ("ab", 1024), ("ab", 0), ("ab", 1536), ("ab", 2560), ("ab", 3072), ("ab", 2048)]
MODS = [("mod", n // 12, n % 12) for n in range(24)]
UNITS = list(MODS[0:4])
AB_AT, MOD_AFTER = [], []
_m = 4
for _u in AB_UNITS:
    AB_AT.append(len(UNITS))
    UNITS.append(_u)
    MOD_AFTER.append((_m, _m + 2))
    UNITS += MODS[_m:_m + 2]
    _m += 2
MOD_REST = _m
UNITS += MODS[_m:]
OUT0_AT = len(UNITS)
UNITS += [("about", 0), ("about", 1)]
MOE_AT = [len(UNITS)]
UNITS += [("moe", 0)] * 48
HYIN_AT = len(UNITS)
UNITS += [("hyin", c) for c in (2, 3, 4, 5, 0, 1)]
OUT1_AT = len(UNITS)
UNITS += [("hyout", 0), ("hyout", 1)]
MOE_AT.append(len(UNITS))
UNITS += [("moe", 1)] * 48
MOD_AT = {u[1] * 12 + u[2]: n for n, u in enumerate(UNITS) if u[0] == "mod"}


def build(nc, I, O):
    ctx = ExitStack()
    with ctx:
        def sb(name, shape, dt=F32):
            return ctx.enter_context(nc.sbuf_tensor(name, shape, dt))

        def sem(name):
            return ctx.enter_context(nc.semaphore(name))

        ps = ctx.enter_context(nc.psum_tensor("ps", [P, 8, 512], F32))

        def bank(b, n=1):
            return ps[:, b:b + n, :].rearrange("p b c -> p (b c)")

        ring = sb("ring", [P, RING, UNIT])
        xT = sb("xT", [P, KD, NS, T])
        hT = sb("hT", [P, KD, NS, T])
        sqs = sb("sqs", [P, 2304])
        sq = sqs[:, 0:2048].rearrange("p (k s t) -> p k s t", k=KD, s=NS)
        rstd = sb("rstd", [P, NS, T])
        cst = sb("cst", [P, CST_N])
        ones = sb("ones", [P, P])
        VT = sb("VT", [P, 3, 128])
        modT = sb("modT", [P, 2, 48, NS])
        scl = sb("scl", [P, 4, KD, NS])
        csil = sb("csil", [P, KD, NS])
        eps = sb("eps", [P, 1])
        rw = sb("rw", [P, KD, NE])
        rb = sb("rb", [P, NE])
        fcol = sb("fcol", [P, 8])
        zero16 = sb("zero16", [P, 128], BF16)
        arena = sb("arena", [P, ARENA])

        def carve(sizes):
            out, at = {}, 0
            for name, n in sizes:
                out[name] = arena[:, at:at + n]
                at += n
            assert at <= ARENA, at
            return out

        def C(name):
            o, n = CST[name]
            return cst[:, o:o + n]

        ident = C("ident")

        def V(name):
            t, r, n = ROWS[name]
            return VT[:, t, r:r + n]

        A = carve([("E0", 1024), ("E1", 1024), ("K0", 1024), ("K1", 1024), ("B0", 1024), ("B1", 1024),
                   ("X0", 1024), ("X1", 1024), ("tmp", 1024),
                   ("kcT", 1024), ("att0", 1024), ("att1", 1024), ("q", 1024), ("v", 1024), ("S1", 2048),
                   ("qk", 1280), ("vb", 256)])
        E, K, B, X = ([A[n + d] for d in "01"] for n in "EKBX")
        att = [A["att0"], A["att1"]]
        probs_s = arena[:, 0:2048]
        probs_p = arena[:, 3072:4096]
        pT_s = arena[:, 4096:6144]
        pT_p = arena[:, 6144:7168]
        otm = arena[:, 7168:8192]
        sqk = sqs[:, 0:1280]
        S0 = sqs[:, 1280:2304].rearrange("p (d h c) -> p d h c", d=2, h=HA)
        qn = sqs[:, 0:1024].rearrange("p (s n c) -> p s n c", s=NS, c=HD)
        osd = sqs[:, 1280:2304]
        seg = sb("seg", [P, 1024])
        qT = seg[:].rearrange("p (s c t) -> p s c t", s=NS, c=4)
        Sfin = A["tmp"].rearrange("p (d h c) -> p d h c", d=2, h=HA)
        S1 = A["S1"].rearrange("p (d s h c) -> p d s h c", d=2, s=NS, h=HA)
        decs = sb("decs", [P, 2, 16])
        kT = sb("kT", [P, 3, 128])
        ckv = sb("ckv", [P, 2, 128])
        gqk = sb("gqk", [P, 2, HD])
        sga = A["K0"].rearrange("p (h s t) -> p h s t", h=HA, s=NS)
        lbt = sb("lbt", [P, 6, 8])
        small = sb("small", [P, 96])
        catT = hT

        M = carve([("htm", 2048), ("S", 2048), ("ST", 2048), ("xg", 1024), ("sg", 512), ("hid", 512),
                   ("yT", 1024), ("y", 1024), ("r", 1024), ("fhT", 512), ("fh", 512)])
        htm = M["htm"].rearrange("p (s d) -> p s d", s=NS)
        S = M["S"].rearrange("p (s c) -> p s c", s=NS)
        ST = M["ST"].rearrange("p (g c) -> p g c", g=NPAIR)
        xg = M["xg"].rearrange("p (k c) -> p k c", k=KD)
        sg = M["sg"].rearrange("p (e c) -> p e c", e=2)
        hid = M["hid"].rearrange("p (e f c) -> p e f c", e=2, f=KF)
        yT = M["yT"].rearrange("p (k c) -> p k c", k=KD)
        y = M["y"]
        R = {}
        _at = 0
        for name, n in [("lg", 32), ("e", 32), ("score", 32), ("bi", 32), ("gt", 128), ("eq", 128), ("rank", 32),
                        ("selE", 32), ("bs", 32), ("gs", 8), ("grank", 8), ("selG", 8), ("mask", 32), ("w", 32),
                        ("gate", 32), ("pos", 32), ("over", 32), ("c1", 2), ("c2", 2), ("c3", 2), ("cnt", 16),
                        ("mxc", 1), ("gcol", 2)]:
            R[name] = M["r"][:, _at:_at + n]
            _at += n
        flag = sb("flag", [P, 2], I32)

        H = carve([("zz", 2048), ("x1", 2048), ("x0", 2048), ("zt", 2048), ("KA", 1024), ("KB", 1024), ("KC", 1024),
                   ("ub", 4 * 264), ("uc", 4 * 256), ("ya", 1024), ("yb", 1024), ("t1", 1024), ("hyc", HYC_N - D)])
        w3s = arena[:, 0:2048]
        filt = arena[:, 6144:8192]
        decay = H["ya"]
        fw = H["t1"][:, 0:128].rearrange("p (n c) -> p n c", n=2)
        hid1 = H["t1"][0:HY, 128:640].rearrange("p (n c) -> p n c", n=4)
        YS = [(H["ya"], H["yb"]), (H["x1"][:, 0:1024], H["x1"][:, 1024:2048])]
        HY_ORDER = list(range(8, 16)) + list(range(16, 24)) + list(range(0, 8))

        def HC(name):
            o, n = HYC[name]
            return H["hyc"][:, o:o + n]

        ring_full = [sem(f"ring_full{i}") for i in range(RING)]
        ring_free = [sem(f"ring_free{i}") for i in range(RING)]
        names = """fw_in rows_in cst_in x_in small_in state_in cache_in hyc_in w3_in decay_in out_done cache_out
            g_const t_rows d_rows t_xT a_xT d_xT a_cs a_sq t_ss a_sqrt d_mod d_h
            a_proj d_ef d_kk a_lf d_x1 a_ea a_eb d_kd d_x2 a_e2 d_q2 d_kc a_e3 a_e4
            t_att d_att t_kcT a_kcT t_U d_state t_o a_osq t_oss a_osqrt d_oA
            a_qksq d_var a_qksd d_qk t_qkT a_qkT t_sc d_max a_exp t_pT a_pT t_pv d_o t_oT a_cat d_x
            t_log a_htm d_lg a_re d_mask t_pos d_sg t_ST a_ST t_htm
            m_xg a_xg d_xg a_sg d_hid a_yT d_yT m_y a_y d_y m_sc
            d_flag t_sg d_vs
            hy_l1 hy_r1 hy_s1 hy_l2 hy_r2 hy_s2 hy_f hy_fd hy_k a_k t_u a_u d_uc d_zz t_zt a_zt t_spec d_spec t_y d_r
            t_fin a_fin d_chain a_chain g_chain""".split()
        q = {n: sem(n) for n in names}
        fb = {n: [sem(f"{n}{l}") for l in range(2)] for n in
              ["fb_in", "fb_gate", "fb_silu", "fb_hid", "fb_tr", "fb_hidT", "fb_down", "fb_done", "fb_col"]}

        chain = {"d_chain": 0, "a_chain": 0, "g_chain": 0}

        def link(eng, name, ins):
            chain[name] += 1
            ins.then_inc(q[name], 1)
            eng.wait_ge(q[name], chain[name])

        def unit(n):
            return ring[:, n % RING, :].rearrange("p (k c) -> p k c", k=KD)

        def down_unit(n):
            return ring[:, n % RING, :].rearrange("p (k c) -> p k c", k=KF)

        def arrived(eng, n, more=0):
            eng.wait_ge(ring_full[n % RING], (more + (n // RING + 1)) * 16)

        def products_of(eng, n, more=0):
            eng.wait_ge(ring_free[n % RING], more + (n // RING + 1))

        block = ctx.enter_context(nc.Block())

        @block.sync
        def _(sp):
            def rows_of(name, ap):
                t, r, n = ROWS[name]
                sp.dma_start(rows[r:r + n, t, :], ap).then_inc(q["rows_in"], 16)

            rows = ring[:, RING - 1, 0:384].rearrange("p (t c) -> p t c", t=3)
            rows_of("norm_g", I["norm_g"].rearrange("l i (k p) -> (l i k) p", p=P))
            rows_of("hgrn_lb", I["hgrn_lb"].rearrange("n d (k p) -> (n d k) p", p=P))
            rows_of("onorm", I["hgrn_onorm_g"].rearrange("n (k p) -> (n k) p", p=P))
            rows_of("c", I["c"].rearrange("n (k p) -> (n k) p", p=P))
            rows_of("c_ctx", I["c_ctx"].rearrange("(k p) -> k p", p=P))
            rows_of("dskip", I["hy_dskip"].rearrange("n (k p) -> (n k) p", p=P))
            rows_of("hy_in_b", I["hy_in_b"].rearrange("n (k p) -> (n k) p", p=P))
            rows_of("hy_conv_b", I["hy_conv_b"].rearrange("n (k p) -> (n k) p", p=P))
            rows_of("mod_b", I["mod_b"].rearrange("l (k p) -> (l k) p", p=P))
            rows_of("hy_conv_w", I["hy_conv_w"].rearrange("n w (k p) -> (n w k) p", p=P))

            w_dram = {
                "mod": lambda u: I["mod_w"][u[1]].rearrange("(k p) c -> p k c", p=P)[:, :, u[2] * 512:u[2] * 512 + 512],
                "ab": lambda u: I["ab_in_w"][0].rearrange("(k p) c -> p k c", p=P)[:, :, u[1]:min(u[1] + 512, 3328)],
                "about": lambda u: I["ab_out_w"][0].rearrange("(k p) c -> p k c", p=P)[:, :, u[1] * 512:u[1] * 512 + 512],
                "hyin": lambda u: I["hy_in_w"][0].rearrange("(k p) c -> p k c", p=P)[:, :, u[1] * 512:u[1] * 512 + 512],
                "hyout": lambda u: I["hy_out_w"][0].rearrange("(k p) c -> p k c", p=P)[:, :, u[1] * 512:u[1] * 512 + 512],
            }
            n = 0
            while n < len(UNITS):
                u = UNITS[n]
                if u[0] != "moe":
                    src = w_dram[u[0]](u)
                    if n == RING - 1:
                        sp.wait_ge(q["t_rows"], 1)
                    if n >= RING:
                        sp.wait_ge(ring_free[n % RING], n // RING)
                    sp.dma_start(unit(n)[:, :, 0:src.shape[2]], src).then_inc(ring_full[n % RING], 16)
                    n += 1
                    continue
                l = u[1]
                with sp.Fori(0, NPAIR) as i:
                    for j, (e, w) in enumerate([(0, "gate"), (0, "up"), (1, "gate"), (1, "up"), (0, "down"), (1, "down")]):
                        m = n + j
                        sp.wait_ge(ring_free[m % RING], i + m // RING)
                        src = I["moe_w_" + w][l, bass.ds(i * 2 + e, 1)].rearrange("o (k p) c -> p (o k) c", p=P)
                        dst = down_unit(m) if w == "down" else unit(m)
                        sp.dma_start(dst, src).then_inc(ring_full[m % RING], 16)
                n += 6 * NPAIR
                sp.wait_ge(q["d_flag"], l + 1)
                more = sp.value_load(flag[0:1, l:l + 1])
                with sp.If(more > 0):
                    for m in range(n - 6, n):
                        sp.wait_ge(ring_free[m % RING], m // RING + 1)
                    with sp.Fori(0, NE) as e:
                        sp.wait_ge(fb["fb_done"][l], e * 2 + 1)
                        for j, w in enumerate(["gate", "up", "down"]):
                            src = I["moe_w_" + w][l, bass.ds(e, 1)].rearrange("o (k p) c -> p (o k) c", p=P)
                            dst = down_unit(n + j) if w == "down" else unit(n + j)
                            sp.dma_start(dst, src).then_inc(fb["fb_in"][l], 16)
                    sp.wait_ge(fb["fb_done"][l], 2 * NE + 1)
            sp.wait_ge(q["cache_out"], 16 * 6)
            sp.wait_ge(q["out_done"], 16 * 4)

        @block.gpsimd
        def _(pool):
            nc.gpsimd.memset(ones[:], 1.0).then_inc(q["g_const"], 1)
            nc.gpsimd.memset(eps[:], EPS).then_inc(q["g_const"], 1)
            nc.gpsimd.memset(zero16[:], 0.0).then_inc(q["g_const"], 1)
            link(pool, "g_chain", nc.gpsimd.memset(seg[:], 1.0))
            nc.gpsimd.memset(seg[:].rearrange("p (c t) -> p c t", t=CHUNK)[:, :, 0:1], 0.0).then_inc(q["g_const"], 1)
            nc.gpsimd.memset(att[0], 0.0).then_inc(q["g_const"], 1)
            nc.gpsimd.memset(att[1], 0.0).then_inc(q["g_const"], 1)
            pool.wait_ge(q["d_qk"], 1)
            qkt = A["qk"].rearrange("p (s c) -> p s c", s=NS)
            for g in range(KV):
                pool.dma_start(O["new_cache_k"][0, 0, g], qkt[:, 0, 512 + 64 * g:576 + 64 * g]).then_inc(q["cache_out"], 16)
                pool.dma_start(O["new_cache_v"][0, 0, g], A["vb"][:, 64 * g:64 * g + 64]).then_inc(q["cache_out"], 16)
            pool.wait_ge(q["d_state"], 2)
            for d in range(2):
                pool.dma_start(O["new_state"][0, 0, d].rearrange("h k v -> k h v"), Sfin[:, d]).then_inc(q["cache_out"], 16)

        def recur(act, act_fn, d):
            act.wait_ge(q["d_kk"], d + 1)
            act_fn(E[d], E[d], ACT.Ln).then_inc(q["a_lf"], 1)
            act.wait_ge(q["d_x1"], d + 1)
            act_fn(E[d], X[d], ACT.Exp).then_inc(q["a_ea"], 1)
            act.wait_ge(q["a_ea"], d + 1)
            act_fn(X[d], X[d], ACT.Exp, scale=-1.0).then_inc(q["a_eb"], 1)
            act.wait_ge(q["d_x2"], d + 1)
            act_fn(A["tmp"], A["tmp"], ACT.Exp).then_inc(q["a_e2"], 1)
            act_fn(B[d], B[d], ACT.Exp).then_inc(q["a_e3"], 1)

        @block.scalar
        def _(act):
            def dma(dst, src, s):
                act.dma_start(dst, src).then_inc(q[s], 16)

            xin = arena[:, 0:2048].rearrange("p (s d) -> p s d", s=NS)
            dma(cst[:], I["cst"], "cst_in")
            dma(xin[:, 0], I["x_prompt"][0], "x_in")
            dma(xin[:, 1], I["x_sample"][0], "x_in")
            dma(rw[:], I["router_w"].rearrange("(k p) e -> p k e", p=P), "small_in")
            dma(rb[:], I["router_b"].rearrange("(a e) -> a e", a=1).broadcast_to([P, NE]), "small_in")
            dma(gqk[:, 0], I["attn_qnorm_g"].broadcast_to([P, HD]), "small_in")
            dma(gqk[:, 1], I["attn_knorm_g"].broadcast_to([P, HD]), "small_in")
            for c, n in enumerate(["hy_f_b1", "hy_f_b2", "hy_f_freq"]):
                dma(fcol[0:HY, c:c + 1], I[n].rearrange("n (c a) -> (n c) a", a=1), "small_in")
            for g in range(KV):
                dma(ckv[:, 0, 64 * g:64 * g + 64], I["cache_k"][0, 0, g], "cache_in")
                dma(ckv[:, 1, 64 * g:64 * g + 64], I["cache_v"][0, 0, g], "cache_in")

            def act_fn(out, in_, f, **k):
                return nc.scalar.activation(out, in_, f, **k)

            xf = xT[:].rearrange("p k s t -> p (k s t)")
            sqf = sqs[:, 0:2048]
            act.wait_ge(q["d_rows"], 1)
            for s, n in enumerate(["c_ctx", "c"]):
                ins = act_fn(csil[:, :, s], V(n), ACT.Silu)
            ins.then_inc(q["a_cs"], 1)
            act.wait_ge(q["t_xT"], 1)
            nc.scalar.copy(xf[:, 1024:2048], bank(2, 2)).then_inc(q["a_xT"], 1)

            def norm(n):
                if n == 0:
                    act.wait_ge(q["a_xT"], 1)
                    act.wait_ge(q["d_xT"], 1)
                else:
                    act.wait_ge(q["d_x"], n)
                for half in range(2):
                    sl = slice(half * 1024, half * 1024 + 1024)
                    act_fn(sqf[:, sl], xf[:, sl], ACT.Square).then_inc(q["a_sq"], 1)
                act.wait_ge(q["t_ss"], n + 1)
                act.wait_ge(q["g_const"], 6)
                act_fn(rstd[:].rearrange("p s t -> p (s t)"), bank(7)[:, 0:256], ACT.Sqrt, bias=eps[:],
                       scale=1.0 / D).then_inc(q["a_sqrt"], 1)

            def turned_keys(d):
                for s in range(NS):
                    act.wait_ge(q["t_kcT"], d * 2 + s + 1)
                    if d == 1 and s == 0:
                        act.wait_ge(q["t_U"], 1)
                    nc.scalar.copy(A["kcT"][:, s * 512:s * 512 + 512], bank(7)).then_inc(q["a_kcT"], 1)

            norm(0)
            act.wait_ge(q["d_ef"], 1)
            act_fn(lbt[:, 3:5], lbt[:, 1:3], ACT.Exp).then_inc(q["a_e4"], 1)
            act.wait_ge(q["d_h"], KD)
            for d in range(2):
                dma(S0[:, d], I["state_hgrn"][0, 0, d].rearrange("h k v -> k h v"), "state_in")
            pairs = [bank(0, 2), bank(2, 2)]
            dst = [E[0], E[1], A["q"], A["v"]]
            for j in range(7):
                products_of(act, AB_AT[j])
                src = pairs[j % 2]
                if j < 2:
                    act_fn(dst[j], src, ACT.Exp, scale=-1.0).then_inc(q["a_proj"], 1)
                elif j < 4:
                    nc.scalar.copy(dst[j], src).then_inc(q["a_proj"], 1)
                elif j == 4:
                    qkt = A["qk"].rearrange("p (s c) -> p s c", s=NS)
                    nc.scalar.copy(qkt[:, :, 0:512], src.rearrange("p (s c) -> p s c", s=NS)).then_inc(q["a_proj"], 1)
                elif j == 5:
                    sv = src.rearrange("p (s c) -> p s c", s=NS)
                    link(act, "a_chain", nc.scalar.copy(qkt[:, :, 512:640], sv[:, :, 0:128]))
                    nc.scalar.copy(A["vb"].rearrange("p (s c) -> p s c", s=NS), sv[:, :, 128:256]).then_inc(q["a_proj"], 1)
                    act.wait_ge(q["a_proj"], 6)
                    act.wait_ge(q["d_h"], KD)
                    act_fn(sqk, A["qk"], ACT.Square).then_inc(q["a_qksq"], 1)
                else:
                    act_fn(A["K0"], src, ACT.Silu).then_inc(q["a_proj"], 1)
                if j == 2:
                    recur(act, act_fn, 0)
                if j == 3:
                    recur(act, act_fn, 1)
                if j == 5:
                    turned_keys(0)
            act.wait_ge(q["d_var"], 1)
            act_fn(small[:, 20:40], small[:, 0:20], ACT.Sqrt, bias=eps[:], scale=1.0 / HD).then_inc(q["a_qksd"], 1)
            turned_keys(1)
            act.wait_ge(q["t_qkT"], 1)
            link(act, "a_chain", nc.scalar.copy(qT[:, 0].rearrange("p c t -> p (c t)"), bank(0)))
            link(act, "a_chain", nc.scalar.copy(kT[:, 0], bank(1)[:, 0:128]))
            link(act, "a_chain", nc.scalar.copy(qT[:, 1].rearrange("p c t -> p (c t)"), bank(2)))
            nc.scalar.copy(kT[:, 1:3].rearrange("p c t -> p (c t)"), bank(3)[:, 0:256]).then_inc(q["a_qkT"], 1)
            act.wait_ge(q["t_o"], 1)
            act.wait_ge(q["d_qk"], 1)
            for half in range(2):
                act_fn(sqs[:, half * 512:half * 512 + 512], bank(4 + half), ACT.Square).then_inc(q["a_osq"], 1)
            act.wait_ge(q["d_max"], 1)
            for h in range(HB):
                ins = act_fn(probs_s[:, h * 256:h * 256 + 256], bank(0, 4)[:, h * 256:h * 256 + 256], ACT.Exp,
                             bias=small[:, 48 + h:49 + h], scale=HD ** -0.5, accum_out=small[:, 64 + h:65 + h])
            ins.then_inc(q["a_exp"], 1)
            for half in range(2):
                act.wait_ge(q["t_oss"], half + 1)
                act_fn(osd[:, half * 512:half * 512 + 512], bank(7), ACT.Sqrt, bias=eps[:],
                       scale=1.0 / 128).then_inc(q["a_osqrt"], 1)
            act.wait_ge(q["t_pT"], 1)
            nc.scalar.copy(pT_s, bank(0, 4)).then_inc(q["a_pT"], 1)
            act.wait_ge(q["d_max"], 2)
            for h in range(HB):
                ins = act_fn(probs_p[:, h * 128:h * 128 + 128], bank(4, 2)[:, h * 128:h * 128 + 128], ACT.Exp,
                             bias=small[:, 56 + h:57 + h], scale=HD ** -0.5, accum_out=small[:, 72 + h:73 + h])
            ins.then_inc(q["a_exp"], 1)
            act.wait_ge(q["t_pT"], 2)
            nc.scalar.copy(pT_p, bank(4, 2)).then_inc(q["a_pT"], 1)
            for s, b in [(1, 1), (0, 2)]:
                act.wait_ge(q["t_oT"], 2 - s)
                nc.scalar.copy(catT[:, 4:8, s, :], bank(b).rearrange("p (c t) -> p c t", c=4)).then_inc(q["a_cat"], 1)

            def moe(l):
                norm(2 * l + 1)
                if l == 0:
                    act.wait_ge(q["cache_out"], 16 * 6)
                act.wait_ge(q["t_htm"], l + 1)
                nc.scalar.copy(M["htm"], bank(0, 4)).then_inc(q["a_htm"], 1)
                act.wait_ge(q["d_lg"], l + 1)
                act_fn(R["e"], R["lg"], ACT.Exp).then_inc(q["a_re"], 1)
                act.wait_ge(q["t_ST"], l + 1)
                nc.scalar.copy(M["ST"], bank(0, 4)).then_inc(q["a_ST"], 1)
                n0, n2 = l * NPAIR, 2 * l * NPAIR
                with act.Fori(0, NPAIR) as i:
                    act.wait_ge(q["m_xg"], i + (n0 + 1))
                    nc.scalar.copy(xg[:, 0:4, :].rearrange("p k c -> p (k c)"), bank(6)).then_inc(q["a_xg"], 1)
                    for e in range(2):
                        products_of(act, MOE_AT[l] + 2 * e + 1, i)
                        act_fn(sg[:, e, :], bank(6 + e)[:, 0:256], ACT.Silu).then_inc(q["a_sg"], 1)
                    products_of(act, MOE_AT[l] + 5, i)
                    nc.scalar.copy(yT[:, 0:4, :].rearrange("p k c -> p (k c)"), bank(4)).then_inc(q["a_yT"], 1)
                    act.wait_ge(q["m_y"], i + (n0 + 1))
                    nc.scalar.copy(y[:, 0:512], bank(4)).then_inc(q["a_y"], 1)
                act.wait_ge(q["d_flag"], l + 1)
                more = act.value_load(flag[0:1, l:l + 1])
                with act.If(more > 0):
                    with act.Fori(0, NE) as e:
                        for s in range(NS):
                            act.wait_ge(fb["fb_gate"][l], e * 2 + (s + 1))
                            act_fn(M["fh"], bank(4), ACT.Silu).then_inc(fb["fb_silu"][l], 1)

            moe(0)
            act.wait_ge(q["d_x"], 2)
            act.dma_start(fw[0:EMB, 0], I["hy_f_w1"][0]).then_inc(q["fw_in"], 16)
            act.dma_start(fw[0:HY, 1], I["hy_f_w2"][0]).then_inc(q["fw_in"], 16)
            act.dma_start(H["hyc"], I["hyc"][:, 0:HYC_N - D]).then_inc(q["hyc_in"], 16)
            act.dma_start(decay, I["hyc"][:, HYC_N - D:]).then_inc(q["decay_in"], 16)
            act.dma_start(w3s[0:HY, :], I["hy_f_w3"][0]).then_inc(q["w3_in"], 16)
            for i, nm in enumerate(["hy_r1", "hy_r2"]):
                act.wait_ge(q[nm], 1)
                act_fn(hid1[:, 1 + 2 * i, :], hid1[:, 2 * i, :], ACT.Sin).then_inc(q[["hy_s1", "hy_s2"][i]], 1)
            for i, nm in enumerate(["KA", "KB", "KC"]):
                act.wait_ge(q["hy_k"], i + 1)
                nc.scalar.copy(H[nm], bank(4, 2)).then_inc(q["a_k"], 1)
            norm(2)
            for j in range(24):
                if j % 4 == 3:
                    products_of(act, HYIN_AT + j // 4)
                else:
                    act.wait_ge(q["t_u"], j // 4 * 3 + j % 4 + 1)
                ch = HY_ORDER[j]
                b = j % 4
                if j >= 4:
                    act.wait_ge(q["d_uc"], j - 3)
                ub = H["ub"].rearrange("p (b s t) -> p b s t", b=4, s=NS)[:, b, :, 1:T + 1]
                act_fn(ub, bank(4 + b)[:, 0:256].rearrange("p (s t) -> p s t", s=NS), ACT.Identity,
                       bias=V("hy_in_b")[:, ch:ch + 1]).then_inc(q["a_u"], 1)
                if j == 17:
                    for s in range(NS):
                        act.wait_ge(q["t_zt"], s + 1)
                        nc.scalar.copy(H["zt"][:, s * 1024:s * 1024 + 1024], bank(0, 2)).then_inc(q["a_zt"], 1)
            moe(1)
            act.wait_ge(q["t_fin"], 1)
            fin = arena[:, 0:2048].rearrange("p (s d) -> p s d", s=NS)
            nc.scalar.copy(arena[:, 0:2048], bank(0, 4)).then_inc(q["a_fin"], 1)
            act.wait_ge(q["a_fin"], 1)
            for s, o in enumerate(["y_prompt", "y_sample"]):
                act.dma_start(O[o][0, 0:64], fin[0:64, s]).then_inc(q["out_done"], 16)
                act.dma_start(O[o][0, 64:128], fin[64:128, s]).then_inc(q["out_done"], 16)

        @block.vector
        def _(dve):
            v = nc.vector

            def L(ins):
                link(dve, "d_chain", ins)

            dve.wait_ge(q["t_rows"], 1)
            L(v.tensor_copy(VT[:, 0, 0:124], bank(7)[:, 0:124]))
            L(v.tensor_copy(VT[:, 1, 0:96], bank(7)[:, 128:224]))
            v.tensor_copy(VT[:, 2, 0:72], bank(7)[:, 256:328]).then_inc(q["d_rows"], 1)
            dve.wait_ge(q["t_xT"], 1)
            xf = xT[:].rearrange("p k s t -> p (k s t)")
            v.tensor_copy(xf[:, 0:1024], bank(0, 2)).then_inc(q["d_xT"], 1)

            def norm(n):
                l, i = n // 2, n % 2
                dve.wait_ge(q["a_sqrt"], n + 1)
                L(v.reciprocal(rstd[:], rstd[:]))
                L(v.tensor_tensor(sq, xT[:], rstd[:].rearrange("p (o s) t -> p o s t", o=1).broadcast_to([P, KD, NS, T]), ALU.mult))
                if n == 0:
                    mod(0)
                if n == 2:
                    pass
                for s in range(NS):
                    L(v.scalar_tensor_tensor(out=scl[:, n, :, s], in0=modT[:, l, 24 * i + 8:24 * i + 16, s], scalar=1.0,
                                             in1=V("norm_g")[:, 8 * n:8 * n + 8], op0=ALU.add, op1=ALU.mult))
                for k in range(KD):
                    for s in range(NS):
                        ins = v.tensor_scalar(hT[:, k, s, :], sq[:, k, s, :], scl[:, n, k, s:s + 1],
                                              modT[:, l, 24 * i + k, s:s + 1], ALU.mult, ALU.add)
                    ins.then_inc(q["d_h"], 1)

            MODS_DONE = [(0, 0, 16), (0, 16, 48), (1, 0, 48)]

            def mod(g):
                l, a, b = MODS_DONE[g]
                products_of(dve, MOD_AT[[3, 11, 23][g]])
                o = bank(6)[:, 0:192].rearrange("p (l j s) -> p l j s", l=2, s=NS)
                for s in range(NS):
                    ins = v.tensor_tensor(modT[:, l, a:b, s], o[:, l, a:b, s], V("mod_b")[:, 48 * l + a:48 * l + b], ALU.add)
                    if s == 0:
                        L(ins)
                ins.then_inc(q["d_mod"], 1)
                dve.wait_ge(q["d_mod"], g + 1)

            lb = V("hgrn_lb")
            L(v.tensor_tensor(lbt[:, 0], lb[:, 0:8], lb[:, 8:16], ALU.max))
            L(v.tensor_tensor(lbt[:, 1], lb[:, 0:8], lbt[:, 0], ALU.subtract))
            v.tensor_tensor(lbt[:, 2], lb[:, 8:16], lbt[:, 0], ALU.subtract).then_inc(q["d_ef"], 1)
            norm(0)
            dve.wait_ge(q["a_e4"], 1)
            L(v.tensor_tensor(lbt[:, 5], lbt[:, 3], lbt[:, 4], ALU.add))
            L(v.reciprocal(lbt[:, 5], lbt[:, 5]))
            L(v.tensor_tensor(lbt[:, 0], lbt[:, 3], lbt[:, 5], ALU.mult))
            L(v.tensor_tensor(lbt[:, 1], lbt[:, 4], lbt[:, 5], ALU.mult))
            for d in range(2):
                dve.wait_ge(q["a_proj"], d + 1)
                L(v.tensor_scalar(E[d], E[d], 1.0, None, ALU.add))
                L(v.reciprocal(E[d], E[d]))
                for h in range(HA):
                    sl = slice(h * 256, h * 256 + 256)
                    L(v.tensor_scalar(E[d][:, sl], E[d][:, sl], lbt[:, 1, 4 * d + h:4 * d + h + 1],
                                      lbt[:, 0, 4 * d + h:4 * d + h + 1], ALU.mult, ALU.add))
                v.tensor_scalar(K[d], E[d], -1.0, 1.0, ALU.mult, ALU.add).then_inc(q["d_kk"], 1)
            dve.wait_ge(q["g_const"], 6)
            for d in range(2):
                mid, last = [(CHUNK // 2, CHUNK - 1), (CHUNK - 1 - CHUNK // 2, 0)][d]
                dve.wait_ge(q["a_lf"], d + 1)
                if d == 0:
                    L(v.tensor_tensor_scan(B[d], seg[:], E[d], 0.0, ALU.mult, ALU.add))
                else:
                    L(v.tensor_tensor_scan(B[d][:, ::-1], seg[:], E[d][:, ::-1], 0.0, ALU.mult, ALU.add))
                b3 = B[d].rearrange("p (c t) -> p c t", t=CHUNK)
                x3 = X[d].rearrange("p (c t) -> p c t", t=CHUNK)
                t3 = A["tmp"].rearrange("p (c t) -> p c t", t=CHUNK)
                v.tensor_tensor(x3, b3, b3[:, :, mid:mid + 1].broadcast_to([P, 16, CHUNK]), ALU.subtract).then_inc(q["d_x1"], 1)
                if d == 1:
                    dve.wait_ge(q["d_kc"], 1)
                v.tensor_tensor(t3, b3[:, :, last:last + 1].broadcast_to([P, 16, CHUNK]), b3, ALU.subtract).then_inc(q["d_x2"], 1)
                dve.wait_ge(q["a_eb"], d + 1)
                dve.wait_ge(q["a_proj"], 3)
                L(v.tensor_tensor(E[d], E[d], A["q"], ALU.mult))
                v.tensor_tensor(X[d], X[d], K[d], ALU.mult).then_inc(q["d_kd"], 1)
                dve.wait_ge(q["a_e3"], d + 1)
                dve.wait_ge(q["d_kd"], d + 1)
                L(v.tensor_copy(decs[:, d, :], B[d].rearrange("p (c t) -> p c t", t=CHUNK)[:, :, last]))
                L(v.tensor_tensor(K[d], K[d], A["tmp"], ALU.mult))
                v.tensor_tensor(B[d], B[d], A["q"], ALU.mult).then_inc(q["d_kc"], 1)
            for d in range(2):
                dve.wait_ge(q["t_att"], d + 1)
                a4 = att[d].rearrange("p (n t) -> p n t", t=T)
                src = bank(4 + d).rearrange("p (n t) -> p n t", t=CHUNK)
                m = C("mask_r" if d else "mask_f").bitcast(U32)
                for c in range(2):
                    rows = slice(c * 64, c * 64 + 64)
                    mb = m[rows].rearrange("p (o t) -> p o t", o=1).broadcast_to([64, 8, CHUNK])
                    ins = v.copy_predicated(a4[rows, :, c * 64:c * 64 + 64], mb, src[rows])
                ins.then_inc(q["d_att"], 1)
            dve.wait_ge(q["a_qksq"], 1)
            v.tensor_reduce(small[:, 0:20], sqk.rearrange("p (n c) -> p n c", c=HD), AX.X, ALU.add).then_inc(q["d_var"], 1)
            dve.wait_ge(q["a_qksd"], 1)
            dve.wait_ge(q["small_in"], 16 * 7)
            L(v.reciprocal(small[:, 20:40], small[:, 20:40]))
            qk4 = A["qk"].rearrange("p (s n c) -> p s n c", s=NS, c=HD)
            rs = small[:, 20:40].rearrange("p (s n o) -> p s n o", s=NS, o=1)
            for s in range(NS):
                L(v.tensor_tensor(qn[:, s].rearrange("p (c g) d -> p g c d", g=KV),
                                  qk4[:, s, 0:8].rearrange("p (g c) d -> p g c d", g=KV),
                                  rs[:, s, 0:8].rearrange("p (g c) o -> p g c o", g=KV).broadcast_to([P, KV, 4, HD]), ALU.mult))
                L(v.tensor_tensor(qk4[:, s, 8:10], qk4[:, s, 8:10], rs[:, s, 8:10].broadcast_to([P, KV, HD]), ALU.mult))
                L(v.tensor_tensor(qn[:, s], qn[:, s], gqk[:, 0:1].broadcast_to([P, 8, HD]), ALU.mult))
                L(v.tensor_tensor(qk4[:, s, 8:10], qk4[:, s, 8:10], gqk[:, 1:2].broadcast_to([P, 2, HD]), ALU.mult))
            s4 = C("sin").rearrange("p (o r h c) -> p o r h c", o=1, r=2, h=2)
            for xs, t2, n in [(qn[:, 1], A["qk"][:, 0:512], 8), (qk4[:, 1, 8:10], A["qk"][:, 640:768], 2)]:
                t24 = t2.rearrange("p (n r h c) -> p n r h c", r=2, h=2, c=16)
                x4 = xs.rearrange("p n (r h c) -> p n r h c", r=2, h=2)
                for hh in range(2):
                    L(v.tensor_tensor(t24[:, :, :, hh], x4[:, :, :, 1 - hh], s4[:, :, :, hh].broadcast_to([P, n, 2, 16]), ALU.mult))
                L(v.tensor_tensor(xs, xs, C("cos").rearrange("p (o c) -> p o c", o=1).broadcast_to([P, n, HD]), ALU.mult))
                ins = v.tensor_tensor(xs, xs, t2.rearrange("p (n c) -> p n c", c=HD), ALU.add)
                if n == 8:
                    L(ins)
            ins.then_inc(q["d_qk"], 1)
            dve.wait_ge(q["state_in"], 32)
            for d in range(2):
                first, second = (0, 1) if d == 0 else (1, 0)
                dve.wait_ge(q["t_U"], d + 1)
                U = [bank(2 * c, 2).rearrange("p (s h c) -> p s h c", s=NS, h=HA) for c in range(2)]
                dec = decs[:, d, :].rearrange("p (h s c) -> p h s c", h=HA, s=NS)
                L(v.tensor_copy(S1[:, d, 0], U[first][:, 0]))
                for h in range(HA):
                    L(v.scalar_tensor_tensor(out=S1[:, d, 1, h], in0=S0[:, d, h], scalar=dec[:, h, 1, first:first + 1],
                                             in1=U[first][:, 1, h], op0=ALU.mult, op1=ALU.add))
                    ins = v.scalar_tensor_tensor(out=Sfin[:, d, h], in0=S1[:, d, 0, h],
                                                 scalar=dec[:, h, 0, second:second + 1],
                                                 in1=U[second][:, 0, h], op0=ALU.mult, op1=ALU.add)
                    if h < HA - 1:
                        L(ins)
                ins.then_inc(q["d_state"], 1)

            def score_max(s, b, nb, keys, at):
                dve.wait_ge(q["t_sc"], 2 - s)
                L(v.tensor_reduce(small[:, at:at + 8], bank(b, nb).rearrange("p (h c) -> p h c", c=keys), AX.X, ALU.max))
                v.tensor_scalar(small[:, at:at + 8], small[:, at:at + 8], -HD ** -0.5, None, ALU.mult).then_inc(q["d_max"], 1)

            score_max(1, 0, 4, 256, 48)
            for half in range(2):
                dve.wait_ge(q["a_osqrt"], half + 1)
                r = osd[:, half * 512:half * 512 + 512]
                L(v.reciprocal(r, r))
                L(v.tensor_tensor(r, bank(4 + half), r, ALU.mult))
            dve.wait_ge(q["a_proj"], 7)
            for h in range(HA):
                r4 = osd.rearrange("p (s h t) -> p s h t", s=NS, h=HA)
                ins = v.scalar_tensor_tensor(out=catT[:, h], in0=r4[:, :, h], scalar=V("onorm")[:, h:h + 1],
                                             in1=sga[:, h], op0=ALU.mult, op1=ALU.mult)
            ins.then_inc(q["d_oA"], 1)
            score_max(0, 4, 2, 128, 56)
            for s, b, sums in [(1, 7, 64), (0, 0, 72)]:
                dve.wait_ge(q["t_pv"], 2 - s)
                L(v.reciprocal(small[:, sums:sums + 8], small[:, sums:sums + 8]))
                v.tensor_tensor(otm[:, s * 512:s * 512 + 512].rearrange("p (h c) -> p h c", c=HD),
                                bank(b).rearrange("p (h c) -> p h c", c=HD),
                                small[:, sums:sums + 8].rearrange("p (h o) -> p h o", o=1).broadcast_to([P, 8, HD]),
                                ALU.mult).then_inc(q["d_o"], 1)
            mod(1)
            mod(2)

            def residual(l, g, banks, first_sem, base, out_sem=None):
                for k in range(KD):
                    for s in range(NS):
                        src = bank(banks[k // 2])[:, (k % 2) * 256 + s * 128:(k % 2) * 256 + s * 128 + 128]
                        ins = v.scalar_tensor_tensor(out=xT[:, k, s, :], in0=src, scalar=modT[:, l, g * 8 + k, s:s + 1],
                                                     in1=xT[:, k, s, :], op0=ALU.mult, op1=ALU.add)
                        if out_sem is None or k < KD - 1 or s == 0:
                            L(ins)
                if out_sem:
                    ins.then_inc(q[out_sem], 1)

            products_of(dve, OUT0_AT + 1)
            residual(0, 2, [3, 4, 5, 7], None, 0, "d_x")

            def rank(bi, n, gt, eq, out):
                bj = bi.rearrange("p (n o j) -> p n o j", o=1, j=4).broadcast_to([P, n, 4, 4])
                b_i = bi.rearrange("p (n i o) -> p n i o", i=4, o=1).broadcast_to([P, n, 4, 4])
                g4 = gt.rearrange("p (n i j) -> p n i j", i=4, j=4)
                e4 = eq.rearrange("p (n i j) -> p n i j", i=4, j=4)
                L(v.tensor_tensor(g4, bj, b_i, ALU.is_gt))
                L(v.tensor_tensor(e4, bj, b_i, ALU.is_equal))
                e3 = eq.rearrange("p (n i) -> p n i", i=16)
                L(v.tensor_tensor(e3, e3, C("tie").rearrange("p (o c) -> p o c", o=1).broadcast_to([P, n, 16]), ALU.mult))
                L(v.tensor_tensor(gt, gt, eq, ALU.add))
                L(v.tensor_reduce(out, gt.rearrange("p (n j) -> p n j", j=4), AX.X, ALU.add))

            def moe(l):
                if l == 0:
                    dve.wait_ge(q["cache_out"], 16 * 6)
                norm(2 * l + 1)

                def col(a, n):
                    return a.rearrange("p (s o) -> p s o", o=1).broadcast_to([P, NS, n])

                def g3(a):
                    return a.rearrange("p (s e) -> p s e", s=NS)

                dve.wait_ge(q["t_log"], l + 1)
                lg = g3(bank(7)[:, 256:288])
                L(v.tensor_reduce(R["c1"], lg, AX.X, ALU.max))
                v.tensor_tensor(g3(R["lg"]), lg, col(R["c1"], NE), ALU.subtract).then_inc(q["d_lg"], 1)
                dve.wait_ge(q["a_re"], l + 1)
                L(v.tensor_reduce(R["c2"], g3(R["e"]), AX.X, ALU.add))
                L(v.reciprocal(R["c2"], R["c2"]))
                L(v.tensor_tensor(g3(R["score"]), g3(R["e"]), col(R["c2"], NE), ALU.mult))
                L(v.tensor_tensor(g3(R["bi"]), g3(R["score"]),
                                  rb[:].rearrange("p (o e) -> p o e", o=1).broadcast_to([P, NS, NE]), ALU.add))
                rank(R["bi"], 8, R["gt"], R["eq"], R["rank"])
                L(v.tensor_scalar(R["selE"], R["rank"], 1.5, None, ALU.is_lt))
                L(v.tensor_tensor(R["bs"], R["bi"], R["selE"], ALU.mult))
                L(v.tensor_reduce(R["gs"], R["bs"].rearrange("p (n j) -> p n j", j=4), AX.X, ALU.add))
                rank(R["gs"], 2, R["gt"][:, 0:32], R["eq"][:, 0:32], R["grank"])
                L(v.tensor_scalar(R["selG"], R["grank"], 0.5, None, ALU.is_lt))
                L(v.tensor_tensor(R["mask"].rearrange("p (n j) -> p n j", j=4), R["selE"].rearrange("p (n j) -> p n j", j=4),
                                  R["selG"].rearrange("p (n o) -> p n o", o=1).broadcast_to([P, 8, 4]), ALU.mult))
                L(v.tensor_tensor(R["w"], R["score"], R["mask"], ALU.mult))
                v.tensor_reduce(R["c3"], g3(R["w"]), AX.X, ALU.add).then_inc(q["d_mask"], 1)
                dve.wait_ge(q["d_mask"], l + 1)
                L(v.reciprocal(R["c3"], R["c3"]))
                L(v.tensor_tensor(g3(R["gate"]), g3(R["w"]), col(R["c3"], NE), ALU.mult))
                dve.wait_ge(q["t_pos"], l + 1)
                pos = bank(7)[:, 288:320]
                L(v.tensor_scalar(R["over"], pos, CAP - 0.5, None, ALU.is_gt))
                L(v.tensor_tensor(R["over"], R["over"], R["gate"], ALU.mult))
                L(v.tensor_scalar(R["pos"], pos, 1.0, None, ALU.add))
                L(v.tensor_tensor(R["pos"], R["pos"], R["mask"], ALU.mult))
                L(v.tensor_scalar(R["pos"], R["pos"], -1.0, None, ALU.add))
                L(v.tensor_reduce(R["mxc"], bank(7)[:, 320:336], AX.X, ALU.max))
                v.tensor_scalar(flag[:, l:l + 1], R["mxc"], CAP + 0.5, None, ALU.is_gt).then_inc(q["d_flag"], 1)
                sgt = sqs[:, 0:2048].rearrange("p (s e c) -> p s e c", s=NS, e=NE)
                for s in range(NS):
                    s3 = S[:, s].rearrange("p (e c) -> p e c", e=NE)
                    L(v.tensor_tensor(s3, C("slot").rearrange("p (o c) -> p o c", o=1).broadcast_to([P, NE, CAP]),
                                      R["pos"][:, s * NE:s * NE + NE].rearrange("p (e o) -> p e o", o=1).broadcast_to([P, NE, CAP]),
                                      ALU.is_equal))
                    v.tensor_tensor(sgt[:, s], s3,
                                    R["gate"][:, s * NE:s * NE + NE].rearrange("p (e o) -> p e o", o=1).broadcast_to([P, NE, CAP]),
                                    ALU.mult).then_inc(q["d_sg"], 1)
                n0, n2 = l * NPAIR, 2 * l * NPAIR
                with dve.Fori(0, NPAIR) as i:
                    dve.wait_ge(q["m_xg"], i + (n0 + 1))
                    v.tensor_copy(xg[:, 4:8, :].rearrange("p k c -> p (k c)"), bank(7)).then_inc(q["d_xg"], 1)
                    for e in range(2):
                        dve.wait_ge(q["a_sg"], i * 2 + (n2 + e + 1))
                        v.tensor_tensor(hid[:, e].rearrange("p f c -> p (f c)"), bank(6 + e)[:, 256:512],
                                        sg[:, e, :], ALU.mult).then_inc(q["d_hid"], 1)
                    products_of(dve, MOE_AT[l] + 5, i)
                    v.tensor_copy(yT[:, 4:8, :].rearrange("p k c -> p (k c)"), bank(5)).then_inc(q["d_yT"], 1)
                    dve.wait_ge(q["m_y"], i + (n0 + 1))
                    v.tensor_copy(y[:, 512:1024], bank(5)).then_inc(q["d_y"], 1)
                dve.wait_ge(q["m_sc"], (l + 1) * NPAIR)
                residual(l, 5, [0, 1, 2, 3], None, 0)
                dve.wait_ge(q["d_flag"], l + 1)
                more = dve.value_load(flag[0:1, l:l + 1])
                with dve.If(more > 0):
                    v.tensor_copy(small[:, 91:92], xT[:, 0, 0, 0:1]).then_inc(fb["fb_done"][l], 1)
                    with dve.Fori(0, NE) as e:
                        for s in range(NS):
                            v.tensor_copy(R["gcol"][:, s:s + 1], R["over"][:, bass.ds(e + s * NE, 1)]).then_inc(fb["fb_col"][l], 1)
                            dve.wait_ge(fb["fb_col"][l], e * 2 + (s + 1))
                            dve.wait_ge(fb["fb_silu"][l], e * 2 + (s + 1))
                            v.scalar_tensor_tensor(out=M["fh"], in0=bank(5), scalar=R["gcol"][:, s:s + 1], in1=M["fh"],
                                                   op0=ALU.mult, op1=ALU.mult).then_inc(fb["fb_hid"][l], 1)
                            dve.wait_ge(fb["fb_tr"][l], e * 2 + (s + 1))
                            v.tensor_copy(M["fhT"], bank(6)).then_inc(fb["fb_hidT"][l], 1)
                            dve.wait_ge(fb["fb_down"][l], e * 2 + (s + 1))
                            for k in range(KD):
                                ins = v.scalar_tensor_tensor(
                                    out=xT[:, k, s, :], in0=bank(0, 2)[:, k * 128:k * 128 + 128],
                                    scalar=modT[:, l, 40 + k, s:s + 1], in1=xT[:, k, s, :], op0=ALU.mult, op1=ALU.add)
                            ins.then_inc(fb["fb_done"][l], 1)
                            dve.wait_ge(fb["fb_done"][l], e * 2 + (s + 2))
                v.tensor_copy(small[:, 90:91], xT[:, 0, 0, 0:1]).then_inc(q["d_x"], 1)

            moe(0)
            PI = float(np.pi)
            C1 = 6.28125
            C2 = 2 * PI - 6.28125
            MAGIC = 12582912.0
            dve.wait_ge(q["small_in"], 16 * 7)
            for i in range(2):
                dve.wait_ge(q[["hy_l1", "hy_l2"][i]], 1)
                a, b = hid1[:, 2 * i, :], hid1[:, 2 * i + 1, :]
                L(v.tensor_scalar(a, bank(6)[0:HY, 256 + 128 * i:384 + 128 * i], fcol[0:HY, i:i + 1], fcol[0:HY, 2:3],
                                  ALU.add, ALU.mult))
                L(v.tensor_scalar(b, a, 1.0 / (2 * PI), MAGIC, ALU.mult, ALU.add))
                L(v.tensor_scalar(b, b, -MAGIC, None, ALU.add))
                L(v.scalar_tensor_tensor(out=a, in0=b, scalar=-C1, in1=a, op0=ALU.mult, op1=ALU.add))
                L(v.scalar_tensor_tensor(out=a, in0=b, scalar=-C2, in1=a, op0=ALU.mult, op1=ALU.add))
                v.tensor_scalar(a, a, PI, -PI, ALU.min, ALU.max).then_inc(q[["hy_r1", "hy_r2"][i]], 1)
            dve.wait_ge(q["decay_in"], 16)
            for i in range(2):
                dve.wait_ge(q["hy_f"], i + 1)
                v.tensor_tensor(filt[:, i * 1024:i * 1024 + 1024], bank(2 * i, 2), decay, ALU.mult).then_inc(q["hy_fd"], 1)
            norm(2)
            ub4 = H["ub"].rearrange("p (b s t) -> p b s t", b=4, s=NS)
            uc4 = H["uc"].rearrange("p (b s t) -> p b s t", b=4, s=NS)
            L(v.memset(ub4[:, :, :, 0:1], 0.0))
            L(v.memset(ub4[:, :, :, T + 1:T + 2], 0.0))
            cw, cb = V("hy_conv_w"), V("hy_conv_b")
            for j in range(24):
                ch = HY_ORDER[j]
                u, o = ub4[:, j % 4], uc4[:, j % 4]
                dst = {1: H["x1"], 2: o, 0: H["x0"]}[ch // 8]
                if ch // 8 != 2:
                    dst = dst.rearrange("p (k s t) -> p k s t", k=KD, s=NS)[:, ch % 8]
                dve.wait_ge(q["a_u"], j + 1)
                L(v.tensor_scalar(o, u[:, :, 1:T + 1], cw[:, 24 + ch:25 + ch], cb[:, ch:ch + 1], ALU.mult, ALU.add))
                L(v.scalar_tensor_tensor(out=o, in0=u[:, :, 0:T], scalar=cw[:, ch:ch + 1], in1=o, op0=ALU.mult, op1=ALU.add))
                v.scalar_tensor_tensor(out=dst, in0=u[:, :, 2:T + 2], scalar=cw[:, 48 + ch:49 + ch], in1=o,
                                       op0=ALU.mult, op1=ALU.add).then_inc(q["d_uc"], 1)
                dve.wait_ge(q["d_uc"], j + 1)
                if ch // 8 == 2:
                    k = ch % 8
                    v.tensor_tensor(H["zz"].rearrange("p (k s t) -> p k s t", k=KD, s=NS)[:, k], dst,
                                    H["x1"].rearrange("p (k s t) -> p k s t", k=KD, s=NS)[:, k],
                                    ALU.mult).then_inc(q["d_zz"], 1)
            for s in range(NS):
                dve.wait_ge(q["t_spec"], s + 1)
                dve.wait_ge(q["a_k"], 3)
                dve.wait_ge(q["d_uc"], 24)
                Ua, Ub = bank(0, 2), bank(2, 2)
                ya, yb, t1 = YS[s][0], YS[s][1], H["t1"]
                L(v.tensor_tensor(ya, Ua, H["KA"], ALU.mult))
                L(v.tensor_tensor(t1, Ub, H["KB"], ALU.mult))
                L(v.tensor_tensor(ya, ya, t1, ALU.subtract))
                L(v.tensor_tensor(yb, Ua, H["KB"], ALU.mult))
                L(v.tensor_tensor(t1, Ub, H["KC"], ALU.mult))
                v.tensor_tensor(yb, yb, t1, ALU.add).then_inc(q["d_spec"], 1)
                dve.wait_ge(q["d_spec"], s + 1)
            z4 = H["zz"].rearrange("p (k s t) -> p k s t", k=KD, s=NS)
            x04 = H["x0"].rearrange("p (k s t) -> p k s t", k=KD, s=NS)
            for s in range(NS):
                dve.wait_ge(q["t_y"], s + 1)
                yp = bank(4, 2).rearrange("p (k t) -> p k t", k=KD)
                for k in range(KD):
                    L(v.scalar_tensor_tensor(out=z4[:, k, s], in0=z4[:, k, s], scalar=V("dskip")[:, k:k + 1],
                                             in1=yp[:, k], op0=ALU.mult, op1=ALU.add))
                    ins = v.tensor_tensor(x04[:, k, s], x04[:, k, s], z4[:, k, s], ALU.mult)
                ins.then_inc(q["d_r"], 1)
            products_of(dve, OUT1_AT + 1)
            residual(1, 2, [0, 1, 2, 3], None, 0, "d_x")
            moe(1)

        @block.tensor
        def _(pe):
            mm = nc.tensor.matmul
            tr = nc.tensor.transpose

            rows = ring[:, RING - 1, 0:384].rearrange("p (t c) -> p t c", t=3)
            pe.wait_ge(q["rows_in"], 160)
            pe.wait_ge(q["cst_in"], 16)
            for t in range(3):
                n = ROWS_IN_TILE[t]
                ins = tr(bank(7)[:, t * 128:t * 128 + n], rows[0:n, t, :], ident[0:n, 0:n])
            ins.then_inc(q["t_rows"], 1)
            xin = arena[:, 0:2048].rearrange("p (s d) -> p s d", s=NS)
            pe.wait_ge(q["x_in"], 32)
            for k in range(KD):
                for s in range(NS):
                    c = k * 256 + s * 128
                    ins = tr(bank(0, 4)[:, c:c + 128], xin[:, s, k * 128:k * 128 + 128], ident)
            ins.then_inc(q["t_xT"], 1)

            def norm(n):
                if n == 0:
                    pe.wait_ge(q["g_const"], 6)
                    pe.wait_ge(q["d_rows"], 1)
                for k in range(KD):
                    if k % 4 == 0:
                        pe.wait_ge(q["a_sq"], 2 * n + k // 4 + 1)
                    ins = mm(bank(7)[:, 0:256], ones[:], sq[:, k].rearrange("p s t -> p (s t)"),
                             start=(k == 0), stop=(k == KD - 1))
                ins.then_inc(q["t_ss"], 1)

            def used(ins, n):
                ins.then_inc(ring_free[n % RING], 1)

            def mod(m):
                l, j0 = m // 12, (m % 12) * 4
                n = MOD_AT[m]
                arrived(pe, n)
                if m == 0:
                    pe.wait_ge(q["a_cs"], 1)
                for j in range(4):
                    c = (l * 48 + j0 + j) * 2
                    for k in range(KD):
                        ins = mm(bank(6)[:, c:c + 2], unit(n)[:, k, j * 128:j * 128 + 128], csil[:, k, :],
                                 start=(k == 0), stop=(k == KD - 1))
                used(ins, n)

            norm(0)
            for m in range(4):
                mod(m)

            def feature_major(n, out, src, cols, chunks):
                for c in range(chunks):
                    for k in range(KD):
                        ins = mm(out(c), unit(n)[:, k, c * 128:c * 128 + 128], src(k), start=(k == 0), stop=(k == KD - 1))
                return ins

            def hk(k):
                return hT[:, k].rearrange("p s t -> p (s t)")

            def projection(j):
                n = AB_AT[j]
                b = 2 * (j % 2)
                arrived(pe, n)
                if j >= 2:
                    pe.wait_ge(q["a_proj"], j - 1)
                if j == 0:
                    pe.wait_ge(q["a_xT"], 1)
                    pe.wait_ge(q["d_xT"], 1)
                    pe.wait_ge(q["d_h"], KD)
                if j in (0, 1, 2, 6):
                    ins = feature_major(n, lambda c: bank(b, 2)[:, c * 256:c * 256 + 256], hk, 512, 4)
                else:
                    w = 256 if j == 5 else 512
                    for s in range(NS):
                        for k in range(KD):
                            ins = mm(bank(b + s)[:, 0:w], hT[:, k, s, :], unit(n)[:, k, 0:w],
                                     start=(k == 0), stop=(k == KD - 1))
                used(ins, n)

            def at(d):
                pe.wait_ge(q["d_kd"], d + 1)
                Aq = E[d].rearrange("p (h s t) -> p h s t", h=HA, s=NS)
                Kd = X[d].rearrange("p (h s t) -> p h s t", h=HA, s=NS)
                for c in range(2):
                    for s in range(NS):
                        for h in range(HA):
                            col = (s * HA + h) * 64
                            ins = mm(bank(4 + d)[c * 64:c * 64 + 64, col:col + 64], Kd[:, h, s, c * 64:c * 64 + 64],
                                     Aq[:, h, s, c * 64:c * 64 + 64], start=True, stop=True)
                ins.then_inc(q["t_att"], 1)

            def kc(d):
                pe.wait_ge(q["d_kc"], d + 1)
                Kc = K[d].rearrange("p (h s t) -> p h s t", h=HA, s=NS)
                for s in range(NS):
                    if d * 2 + s >= 1:
                        pe.wait_ge(q["a_kcT"], d * 2 + s)
                    for h in range(HA):
                        ins = tr(bank(7)[:, h * 128:h * 128 + 128], Kc[:, h, s, :], ident)
                    ins.then_inc(q["t_kcT"], 1)

            vtm = A["v"].rearrange("p (s h c) -> p s h c", s=NS, h=HA)

            def chunk_states(d):
                pe.wait_ge(q["a_kcT"], 2 * d + 2)
                if d == 0:
                    pe.wait_ge(q["a_proj"], 7)
                else:
                    pe.wait_ge(q["d_state"], d)
                kT4 = A["kcT"].rearrange("p (s h c) -> p s h c", s=NS, h=HA)
                for c in range(2):
                    rows = slice(c * 64, c * 64 + 64)
                    for s in range(NS):
                        for h in range(HA):
                            col = (s * HA + h) * 128
                            ins = mm(bank(2 * c, 2)[:, col:col + 128], kT4[rows, s, h, :], vtm[rows, s, h, :],
                                     start=True, stop=True)
                ins.then_inc(q["t_U"], 1)

            projection(0); mod(4); mod(5)
            projection(1); mod(6); mod(7)
            projection(2); mod(8); mod(9)
            projection(3); mod(10); mod(11)
            projection(4); at(0); mod(12); mod(13)
            projection(5); at(1); kc(0); mod(14); mod(15)
            projection(6); mod(16); mod(17)
            chunk_states(0)
            mod(18)
            kc(1)
            mod(19)
            chunk_states(1)
            mod(20)
            pe.wait_ge(q["d_qk"], 1)
            pe.wait_ge(q["d_state"], 2)
            pe.wait_ge(q["cache_in"], 64)
            qkt = A["qk"].rearrange("p (s c) -> p s c", s=NS)
            for s in range(NS):
                for c in range(4):
                    src = qn[:, s, 2 * c:2 * c + 2].rearrange("p g d -> p (g d)")
                    tr(bank(2 * s)[:, c * 128:c * 128 + 128], src, ident)
                ins = tr(bank(2 * s + 1)[:, 0:128], qkt[:, s, 512:640], ident)
            ins = tr(bank(3)[:, 128:256], ckv[:, 0], ident)
            ins.then_inc(q["t_qkT"], 1)
            pe.wait_ge(q["d_att"], 2)
            for s in range(NS):
                for h in range(HA):
                    o = bank(4 + s)[:, h * 128:h * 128 + 128]
                    for d in range(2):
                        mm(o, vtm[:, s, h, :], att[d].rearrange("p (s h t) -> p s h t", s=NS, h=HA)[:, s, h, :],
                           start=(d == 0), stop=False)
                    for d in range(2):
                        Q2 = B[d].rearrange("p (h s t) -> p h s t", h=HA, s=NS)
                        first, second = (0, 1) if d == 0 else (1, 0)
                        for c, st in ([(second, S1[:, d, s, h, :])] + ([(first, S0[:, d, h, :])] if s == 1 else [])):
                            last = d == 1 and (s == 0 or c == first)
                            ins = mm(o[:, c * 64:c * 64 + 64], st, Q2[:, h, s, c * 64:c * 64 + 64], start=False, stop=last)
            ins.then_inc(q["t_o"], 1)

            def scores(s, banks, keys, nk):
                for h in range(HB):
                    g, c = h // 4, h % 4
                    rows = slice(64 * g, 64 * g + 64)
                    out = bank(banks, 4)[:, h * nk:h * nk + nk] if nk == 256 else bank(banks, 2)[:, h * nk:h * nk + nk]
                    ins = mm(out, qT[rows, s, c, :], keys[rows], start=True, stop=True)
                ins.then_inc(q["t_sc"], 1)

            pe.wait_ge(q["a_qkT"], 1)
            scores(1, 0, kT[:, 1:3].rearrange("p c t -> p (c t)"), 256)
            mod(21)
            sqf = sqs[:, 0:2048]
            for half in range(2):
                pe.wait_ge(q["a_osq"], half + 1)
                if half:
                    pe.wait_ge(q["a_osqrt"], 1)
                mm(bank(7), ones[:], sqf[:, half * 512:half * 512 + 512], start=True, stop=True).then_inc(q["t_oss"], 1)
            mod(22)

            def turn_probs(s, b, src, nk):
                pe.wait_ge(q["a_exp"], 2 - s)
                nkb = nk // 128
                for h in range(HB):
                    for kb in range(nkb):
                        c = (h * nkb + kb) * 128
                        ins = tr(bank(b, 4 if s else 2)[:, c:c + 128], src[:, c:c + 128], ident)
                ins.then_inc(q["t_pT"], 1)

            turn_probs(1, 0, probs_s, 256)
            mod(23)
            pe.wait_ge(q["d_oA"], 1)
            scores(0, 4, kT[:, 0], 128)

            def attend(s, b, pT, nkb):
                pe.wait_ge(q["a_pT"], 2 - s)
                for h in range(HB):
                    g = h // 4
                    for kb in range(nkb):
                        c = (h * nkb + kb) * 128
                        vals = ckv[:, 1, g * 64:g * 64 + 64] if kb else A["vb"][:, s * 128 + g * 64:s * 128 + g * 64 + 64]
                        ins = mm(bank(b)[:, h * 64:h * 64 + 64], pT[:, c:c + 128], vals, start=(kb == 0), stop=(kb == nkb - 1))
                ins.then_inc(q["t_pv"], 1)

            def turn_out(s, b):
                pe.wait_ge(q["d_o"], 2 - s)
                for c in range(4):
                    ins = tr(bank(b)[:, c * 128:c * 128 + 128], otm[:, s * 512 + c * 128:s * 512 + c * 128 + 128], ident)
                ins.then_inc(q["t_oT"], 1)

            pe.wait_ge(q["a_osqrt"], 2)
            attend(1, 7, pT_s, 2)
            turn_probs(0, 4, probs_p, 128)
            turn_out(1, 1)
            attend(0, 0, pT_p, 1)
            turn_out(0, 2)
            pe.wait_ge(q["a_cat"], 2)

            def out_projection(at_unit, banks, src):
                for half in range(2):
                    n = at_unit + half
                    arrived(pe, n)
                    for c in range(4):
                        k8 = half * 4 + c
                        out = bank(banks[k8 // 2])[:, (k8 % 2) * 256:(k8 % 2) * 256 + 256]
                        for k in range(KD):
                            ins = mm(out, unit(n)[:, k, c * 128:c * 128 + 128], src(k), start=(k == 0), stop=(k == KD - 1))
                    used(ins, n)

            out_projection(OUT0_AT, [3, 4, 5, 7], hk)

            def moe(l):
                norm(2 * l + 1)
                pe.wait_ge(q["d_h"], KD * (2 * l + 2))
                pe.wait_ge(q["small_in"], 16 * 7)
                for s in range(NS):
                    for k in range(KD):
                        ins = mm(bank(7)[:, 256 + s * 16:272 + s * 16], hT[:, k, s, :], rw[:, k, :],
                                 start=(k == 0), stop=(k == KD - 1))
                ins.then_inc(q["t_log"], 1)
                for s in range(NS):
                    for k in range(KD):
                        c = s * 1024 + k * 128
                        ins = tr(bank(0, 4)[:, c:c + 128], hT[:, k, s, :], ident)
                ins.then_inc(q["t_htm"], 1)
                pe.wait_ge(q["d_mask"], l + 1)
                pos = bank(7)[:, 288:320]
                tot = bank(7)[:, 320:336]
                m0, m1 = R["mask"][:, 0:16], R["mask"][:, 16:32]
                mm(pos[:, 0:16], C("tri"), m0, start=True, stop=True)
                mm(pos[:, 16:32], ones[:], m0, start=True, stop=False)
                mm(pos[:, 16:32], C("tri"), m1, start=False, stop=True)
                mm(tot, ones[:], m0, start=True, stop=False)
                mm(tot, ones[:], m1, start=False, stop=True).then_inc(q["t_pos"], 1)
                pe.wait_ge(q["a_htm"], l + 1)
                sgt = sqs[:, 0:2048].rearrange("p (s g c) -> p s g c", s=NS, g=NPAIR)
                for s in range(NS):
                    pe.wait_ge(q["d_sg"], 2 * l + s + 1)
                    for g in range(NPAIR):
                        c = g * 256 + s * 128
                        ins = tr(bank(0, 4)[:, c:c + 128], sgt[:, s, g, :], ident)
                ins.then_inc(q["t_ST"], 1)
                pe.wait_ge(q["a_ST"], l + 1)
                for b in range(4):
                    mm(bank(b), zero16[:], zero16[:].rearrange("p (o c) -> p o c", o=1).broadcast_to([P, 4, 128]), start=True, stop=False, skip_group_check=True)
                n = MOE_AT[l]
                n0, n2 = l * NPAIR, 2 * l * NPAIR
                with pe.Fori(0, NPAIR) as i:
                    for k in range(KD):
                        for s in range(NS):
                            ins = mm(bank(6, 2)[:, k * 128:k * 128 + 128], htm[:, s, k * 128:k * 128 + 128],
                                     S[:, s, bass.ds(i * 128, 128)], start=(s == 0), stop=(s == 1))
                    ins.then_inc(q["m_xg"], 1)
                    pe.wait_ge(q["a_xg"], i + (n0 + 1))
                    pe.wait_ge(q["d_xg"], i + (n0 + 1))
                    for e in range(2):
                        for w in range(2):
                            u = n + 2 * e + w
                            arrived(pe, u, i)
                            for f in range(KF):
                                c = w * 256 + f * 64
                                for k in range(KD):
                                    ins = mm(bank(6 + e)[:, c:c + 64], unit(u)[:, k, f * 128:f * 128 + 128],
                                             xg[:, k, e * 64:e * 64 + 64], start=(k == 0), stop=(k == KD - 1))
                            used(ins, u)
                    for e in range(2):
                        u = n + 4 + e
                        arrived(pe, u, i)
                        pe.wait_ge(q["d_hid"], i * 2 + (n2 + e + 1))
                        for k in range(KD):
                            for f in range(KF):
                                ins = mm(bank(4, 2)[:, k * 128 + e * 64:k * 128 + e * 64 + 64],
                                         down_unit(u)[:, f, k * 128:k * 128 + 128], hid[:, e, f, :],
                                         start=(f == 0), stop=(f == KF - 1))
                        used(ins, u)
                    pe.wait_ge(q["a_yT"], i + (n0 + 1))
                    pe.wait_ge(q["d_yT"], i + (n0 + 1))
                    for k in range(KD):
                        ins = tr(bank(4, 2)[:, k * 128:k * 128 + 128], yT[:, k, :], ident)
                    ins.then_inc(q["m_y"], 1)
                    pe.wait_ge(q["a_y"], i + (n0 + 1))
                    pe.wait_ge(q["d_y"], i + (n0 + 1))
                    for k in range(KD):
                        ins = mm(bank(0, 4)[:, k * 256:k * 256 + 256], y[:, k * 128:k * 128 + 128],
                                 ST[:, bass.ds(i, 1), :].rearrange("p o c -> p (o c)"), start=False, stop=False,
                                 skip_group_check=True)
                    ins.then_inc(q["m_sc"], 1)
                pe.wait_ge(q["d_flag"], l + 1)
                more = pe.value_load(flag[0:1, l:l + 1])
                u0 = n + 6 * NPAIR
                with pe.If(more > 0):
                    pe.wait_ge(q["m_sc"], (l + 1) * NPAIR)
                    with pe.Fori(0, NE) as e:
                        pe.wait_ge(fb["fb_in"][l], e * 48 + 48)
                        for s in range(NS):
                            for w in range(2):
                                for k in range(KD):
                                    ins = mm(bank(4 + w), hT[:, k, s, :], unit(u0 + w)[:, k, :], start=(k == 0), stop=(k == KD - 1))
                            ins.then_inc(fb["fb_gate"][l], 1)
                            pe.wait_ge(fb["fb_hid"][l], e * 2 + (s + 1))
                            for f in range(KF):
                                ins = tr(bank(6)[:, f * 128:f * 128 + 128], M["fh"][:, f * 128:f * 128 + 128], ident)
                            ins.then_inc(fb["fb_tr"][l], 1)
                            pe.wait_ge(fb["fb_hidT"][l], e * 2 + (s + 1))
                            for k in range(KD):
                                for f in range(KF):
                                    ins = mm(bank(0, 2)[:, k * 128:k * 128 + 128],
                                             down_unit(u0 + 2)[:, f, k * 128:k * 128 + 128],
                                             M["fhT"][:, f * 128:f * 128 + 128], start=(f == 0), stop=(f == KF - 1))
                            ins.then_inc(fb["fb_down"][l], 1)
                            pe.wait_ge(fb["fb_done"][l], e * 2 + (s + 2))

            moe(0)
            pe.wait_ge(q["d_x"], 2)
            pe.wait_ge(q["hyc_in"], 16)
            pe.wait_ge(q["fw_in"], 32)
            mm(bank(6)[0:HY, 256:384], fw[0:EMB, 0], HC("zT")[0:EMB, :], start=True, stop=True).then_inc(q["hy_l1"], 1)
            pe.wait_ge(q["hy_s1"], 1)
            mm(bank(6)[0:HY, 384:512], fw[0:HY, 1], hid1[:, 1, :], start=True, stop=True).then_inc(q["hy_l2"], 1)
            pe.wait_ge(q["hy_s2"], 1)
            pe.wait_ge(q["w3_in"], 16)
            for i in range(4):
                ins = mm(bank(i), hid1[:, 3, :], w3s[0:HY, i * 512:i * 512 + 512], start=True, stop=True)
                if i % 2:
                    ins.then_inc(q["hy_f"], 1)
            pe.wait_ge(q["hy_fd"], 2)
            for i, nm in enumerate(["ka", "kb", "kc"]):
                if i:
                    pe.wait_ge(q["a_k"], i)
                for half in range(2):
                    for j in range(2):
                        ins = mm(bank(4 + half), HC(nm + str(j)), filt[:, j * 1024 + half * 512:j * 1024 + half * 512 + 512],
                                 start=(j == 0), stop=(j == 1))
                ins.then_inc(q["hy_k"], 1)
            pe.wait_ge(q["a_k"], 3)
            norm(2)
            z4 = H["zz"].rearrange("p (k s t) -> p k s t", k=KD, s=NS)
            for j in range(24):
                n = HYIN_AT + j // 4
                if j % 4 == 0:
                    arrived(pe, n)
                if j == 0:
                    pe.wait_ge(q["d_h"], KD * 3)
                if j == 3:
                    pe.wait_ge(q["a_sqrt"], 3)
                if j >= 4:
                    pe.wait_ge(q["a_u"], j - 3)
                for k in range(KD):
                    ins = mm(bank(4 + j % 4)[:, 0:256], unit(n)[:, k, (j % 4) * 128:(j % 4) * 128 + 128], hk(k),
                             start=(k == 0), stop=(k == KD - 1))
                if j % 4 == 3:
                    used(ins, n)
                else:
                    ins.then_inc(q["t_u"], 1)
                if j == 17:
                    for s in range(NS):
                        if s == 0:
                            pe.wait_ge(q["d_zz"], KD)
                        else:
                            pe.wait_ge(q["a_zt"], 1)
                        for k in range(KD):
                            ins = tr(bank(0, 2)[:, k * 128:k * 128 + 128], z4[:, k, s, :], ident)
                        ins.then_inc(q["t_zt"], 1)
            for s in range(NS):
                pe.wait_ge(q["a_zt"], 2)
                if s:
                    pe.wait_ge(q["d_spec"], s)
                for part, nm in enumerate(["fa", "fb"]):
                    for half in range(2):
                        ins = mm(bank(2 * part + half), HC(nm), H["zt"][:, s * 1024 + half * 512:s * 1024 + half * 512 + 512],
                                 start=True, stop=True)
                ins.then_inc(q["t_spec"], 1)
            pe.wait_ge(q["a_u"], 24)
            for s in range(NS):
                pe.wait_ge(q["d_spec"], s + 1)
                if s:
                    pe.wait_ge(q["d_r"], s)
                for k in range(KD):
                    o = bank(4, 2)[:, k * 128:k * 128 + 128]
                    mm(o, YS[s][0][:, k * 128:k * 128 + 128], HC("ga"), start=True, stop=False)
                    ins = mm(o, YS[s][1][:, k * 128:k * 128 + 128], HC("gb"), start=False, stop=True)
                ins.then_inc(q["t_y"], 1)
            pe.wait_ge(q["d_r"], 2)
            out_projection(OUT1_AT, [0, 1, 2, 3], lambda k: H["x0"][:, k * 256:k * 256 + 256])
            moe(1)
            pe.wait_ge(q["d_x"], 4)
            for s in range(NS):
                for k in range(KD):
                    c = s * 1024 + k * 128
                    ins = tr(bank(0, 4)[:, c:c + 128], xT[:, k, s, :], ident)
            ins.then_inc(q["t_fin"], 1)


_INS = ['x_prompt', 'x_sample', 'cache_k', 'cache_v', 'state_hgrn', 'c', 'c_ctx', 'norm_g', 'mod_w', 'mod_b',
        'ab_in_w', 'hgrn_lb', 'hgrn_onorm_g', 'attn_qnorm_g', 'attn_knorm_g', 'ab_out_w',
        'hy_in_w', 'hy_in_b', 'hy_conv_w', 'hy_conv_b', 'hy_f_w1', 'hy_f_b1', 'hy_f_w2', 'hy_f_b2',
        'hy_f_w3', 'hy_f_freq', 'hy_dskip', 'hy_out_w', 'router_w', 'router_b',
        'moe_w_gate', 'moe_w_up', 'moe_w_down']
_OUTS = [("y_prompt", (1, T, D)), ("y_sample", (1, T, D)), ("new_cache_k", (1, 1, KV, T, HD)),
         ("new_cache_v", (1, 1, KV, T, HD)), ("new_state", (1, 1, 2, HA, 128, 128))]


def kernel(**inputs):
    import concourse.bacc as _bacc
    from concourse.bass_utils import run_bass_kernel_spmd as _run

    nc = _bacc.Bacc("TRN2", target_bir_lowering=False, num_devices=1)
    arrays, ins, outs = {}, {}, {}
    for name in _INS:
        a = np.ascontiguousarray(inputs[name])
        arrays[f"in_{name}"] = a
        ins[name] = nc.dram_tensor(f"in_{name}", a.shape, F32, kind="ExternalInput").ap()
    for name, a in zip(["cst", "hyc"], shape_constants()):
        arrays[f"in_{name}"] = a
        ins[name] = nc.dram_tensor(f"in_{name}", a.shape, F32, kind="ExternalInput").ap()
    for name, shape in _OUTS:
        outs[name] = nc.dram_tensor(f"out_{name}", shape, F32, kind="ExternalOutput").ap()
    build(nc, ins, outs)
    r = _run(nc, [arrays], core_ids=[0])
    return tuple(r.results[0][f"out_{name}"] for name, _ in _OUTS)
```

```python
from contextlib import ExitStack

import numpy as np

import concourse.bass as bass
from concourse import mybir

F32 = mybir.dt.float32
BF16 = mybir.dt.bfloat16
U32 = mybir.dt.uint32
I32 = mybir.dt.int32
ALU = mybir.AluOpType
ACT = mybir.ActivationFunctionType
AX = mybir.AxisListType

P = 128
D = 1024
KD = D // P
T = 128
NS = 2
CHUNK = 64
HA = 4
HB = 8
KV = 2
HD = 64
NE = 16
NG = 4
F = 512
KF = F // P
CAP = 64
NPAIR = NE // 2
RING = 6
UNIT = KD * 512
EPS = 1e-6
HY = 64
EMB = 33
ARENA = 17920

_GAPS = {(1, 0): [("lf", 0)], (1, 2): [("ex", 0)], (2, 0): [("lf", 1)], (2, 2): [("ex", 1)],
         (5, 1): [("qkT",)], (5, 3): [("at", 0), ("at", 1)],
         (6, 0): [("kc", 0, 0)], (6, 1): [("U", 0, 0), ("kc", 0, 1)], (6, 2): [("U", 0, 1), ("kc", 1, 0)],
         (6, 3): [("U", 1, 0), ("kc", 1, 1)]}
SCHED = []
for _j in range(7):
    for _c in range(4):
        SCHED += [("proj", _j, _c), ("RS"[_c % 2], 4 + 2 * _j + _c // 2)] + _GAPS.get((_j, _c), [])
SCHED += [("U", 1, 1), ("R", 18), ("sc", 1), ("o",), ("S", 18), ("ex1",), ("R", 19), ("oss", 0), ("S", 19), ("oss", 1),
          ("R", 20), ("pT", 1), ("S", 20), ("sc", 0), ("R", 21), ("ex0",), ("pv", 1), ("S", 21), ("pT", 0), ("R", 22),
          ("oT", 1), ("S", 22), ("pv", 0), ("R", 23), ("oT", 0), ("S", 23)]

CST = {}
CST_N = 0
for _name, _n in [("ident", 128), ("tri", 128), ("mask_f", 64), ("mask_r", 64), ("cos", 64), ("sin", 64),
                  ("slot", CAP), ("tie", 16), ("sel", 16)]:
    CST[_name] = (CST_N, _n)
    CST_N += _n
HYC = {}
HYC_N = 0
for _name, _n in [("zT", 128), ("fa", 128), ("fb", 128), ("ka0", 128), ("kb0", 128), ("kc0", 128), ("ka1", 128),
                  ("kb1", 128), ("kc1", 128), ("ga", 128), ("gb", 128), ("decay", D)]:
    HYC[_name] = (HYC_N, _n)
    HYC_N += _n


def shape_constants():
    f32 = np.float32
    a = np.zeros((P, CST_N), f32)

    def put(arr, table, name, val):
        o, n = table[name]
        arr[:val.shape[0], o:o + n] = val

    i = np.arange(P)
    put(a, CST, "ident", np.eye(P, dtype=f32))
    put(a, CST, "tri", (i[:, None] < i[None, :]).astype(f32))
    j = i[:, None] % CHUNK
    put(a, CST, "mask_f", (j <= np.arange(CHUNK)[None]).astype(f32))
    put(a, CST, "mask_r", (j >= np.arange(CHUNK)[None]).astype(f32))
    inv = (f32(10000.0) ** (-np.arange(16, dtype=f32) / f32(16))).astype(f32)
    row, col = (i // 64).astype(f32), (i % 64).astype(f32)
    ang = np.stack([row[:, None] * inv, col[:, None] * inv], 1).astype(f32)
    cos, sin = np.cos(ang.astype(np.float64)), np.sin(ang.astype(np.float64))
    put(a, CST, "cos", np.stack([cos, cos], 2).reshape(P, 64).astype(f32))
    put(a, CST, "sin", np.stack([-sin, sin], 2).reshape(P, 64).astype(f32))
    put(a, CST, "slot", np.tile(np.arange(CAP, dtype=f32), (P, 1)))
    put(a, CST, "sel", (i[:, None] % 32 == np.arange(NE)[None]).astype(f32))
    tie = (np.arange(4)[None] < np.arange(4)[:, None]).astype(f32).reshape(1, 16)
    put(a, CST, "tie", np.tile(tie, (P, 1)))

    b = np.zeros((P, HYC_N), f32)
    L, N = T, 2 * T
    t = np.linspace(0.0, 1.0, L, dtype=f32)
    w = (2.0 * np.pi * np.arange(L) / L)
    fb = np.linspace(1e-4, 15, 16, dtype=f32).astype(np.float64)
    z = np.concatenate([t[:, None], np.cos(w[:, None] * fb), -np.sin(w[:, None] * fb)], 1)
    put(b, HYC, "zT", z.T.astype(f32))
    n = np.arange(L)[:, None]
    f = np.arange(L)[None]
    ang = 2 * np.pi * n * f / N
    alt = (-1.0) ** n
    fa, fbm = np.cos(ang), np.sin(ang)
    fbm = np.where(f == 0, alt, fbm)
    late = n >= 1
    put(b, HYC, "fa", fa)
    put(b, HYC, "fb", fbm)
    put(b, HYC, "ka0", fa)
    put(b, HYC, "kb0", np.sin(ang))
    put(b, HYC, "kc0", np.where(f == 0, alt, fa))
    put(b, HYC, "ka1", fa * late)
    put(b, HYC, "kb1", -np.sin(ang) * late)
    put(b, HYC, "kc1", np.where(f == 0, alt, fa) * late)
    wgt = np.where(np.arange(L) == 0, 1.0, 2.0)[:, None] / N
    ang = ang.T
    put(b, HYC, "ga", np.cos(ang) * wgt)
    put(b, HYC, "gb", np.where(np.arange(L)[:, None] == 0, alt.T / N, np.sin(ang) * wgt))
    lo, hi = np.log(1e-2) / 1.5, np.log(1e-2) / 0.3
    deltas = np.abs(np.linspace(lo, hi, D, dtype=f32)).astype(np.float64)
    put(b, HYC, "decay", np.exp(-t.astype(np.float64)[:, None] * deltas).astype(f32))
    return a, b


ROWS = {"norm_g": (0, 0, 32), "hgrn_lb": (0, 32, 16), "onorm": (0, 48, 4), "c": (0, 52, 8), "c_ctx": (0, 60, 8),
        "dskip": (0, 68, 8), "hy_in_b": (0, 76, 24), "hy_conv_b": (0, 100, 24), "mod_b": (1, 0, 96),
        "hy_conv_w": (2, 0, 72)}
ROWS_IN_TILE = [124, 96, 72]

AB_UNITS = [("ab", 512), ("ab", 1024), ("ab", 2560), ("ab", 3072), ("ab", 0), ("ab", 1536), ("ab", 2048)]
ZF, ZB, QB, KVB, QA, IA, GA = range(7)
MODS = [("mod", n // 12, n % 12) for n in range(24)]
UNITS = list(MODS[0:4])
AB_AT = []
for _j, _u in enumerate(AB_UNITS):
    AB_AT.append(len(UNITS))
    UNITS.append(_u)
    UNITS += MODS[4 + 2 * _j:6 + 2 * _j]
UNITS += MODS[18:]
OUT0_AT = len(UNITS)
UNITS += [("about", 0), ("about", 1)]
MOE_AT = [len(UNITS)]
UNITS += [("moe", 0)] * 48
HYIN_AT = len(UNITS)
UNITS += [("hyin", c) for c in (2, 3, 4, 5, 0, 1)]
OUT1_AT = len(UNITS)
UNITS += [("hyout", 0), ("hyout", 1)]
MOE_AT.append(len(UNITS))
UNITS += [("moe", 1)] * 48
MOD_AT = {u[1] * 12 + u[2]: n for n, u in enumerate(UNITS) if u[0] == "mod"}


def build(nc, I, O):
    ctx = ExitStack()
    with ctx:
        def sb(name, shape, dt=F32):
            return ctx.enter_context(nc.sbuf_tensor(name, shape, dt))

        def sem(name):
            return ctx.enter_context(nc.semaphore(name))

        ps = ctx.enter_context(nc.psum_tensor("ps", [P, 8, 512], F32))

        def bank(b, n=1):
            return ps[:, b:b + n, :].rearrange("p b c -> p (b c)")

        ring = sb("ring", [P, RING, UNIT])
        xT = sb("xT", [P, KD, NS, T])
        hT = sb("hT", [P, KD, NS, T])
        sqs = sb("sqs", [P, 2304])
        sq = sqs[:, 0:2048].rearrange("p (k s t) -> p k s t", k=KD, s=NS)
        rstd = sb("rstd", [P, NS, T])
        cst = sb("cst", [P, CST_N])
        ones = sb("ones", [P, P])
        VT = sb("VT", [P, 3, 128])
        modT = sb("modT", [P, 2, 48, NS])
        scl = sb("scl", [P, 4, KD, NS])
        csil = sb("csil", [P, KD, 32])
        eps = sb("eps", [P, 1])
        rw = sb("rw", [P, KD, 32])
        tri16 = sb("tri16", [P, 2, P], BF16)
        rb = sb("rb", [P, NE])
        fcol = sb("fcol", [P, 8])
        zero16 = sb("zero16", [P, 128], BF16)
        arena = sb("arena", [P, ARENA])

        def carve(sizes):
            out, at = {}, 0
            for name, n in sizes:
                out[name] = arena[:, at:at + n]
                at += n
            assert at <= ARENA, at
            return out

        def C(name):
            o, n = CST[name]
            return cst[:, o:o + n]

        ident = C("ident")

        def V(name):
            t, r, n = ROWS[name]
            return VT[:, t, r:r + n]

        A = carve([("E0", 1024), ("E1", 1024), ("K0", 1024), ("K1", 1024), ("B0", 1024), ("B1", 1024),
                   ("X0", 1024), ("X1", 1024), ("tmp", 1024),
                   ("kcT", 512), ("mrow", 128), ("att0", 1024), ("att1", 1024), ("q", 1024), ("v", 1024), ("S1", 2048),
                   ("qk", 1280), ("vb", 256), ("gqk", 2 * HD)])
        E, K, B, X = ([A[n + d] for d in "01"] for n in "EKBX")
        att = [A["att0"], A["att1"]]
        probs_s = arena[:, 0:2048]
        probs_p = arena[:, 3072:4096]
        pT_s = arena[:, 4096:6144]
        pT_p = arena[:, 6144:7168]
        otm = arena[:, 7168:8192]
        sqk = sqs[:, 0:1280]
        S0 = sqs[:, 1280:2304].rearrange("p (d h c) -> p d h c", d=2, h=HA)
        qn = sqs[:, 0:1024].rearrange("p (s n c) -> p s n c", s=NS, c=HD)
        osd = sqs[:, 1280:2304]
        seg = sb("seg", [P, 1024])
        qT = seg[:].rearrange("p (s c t) -> p s c t", s=NS, c=4)
        Sfin = A["tmp"].rearrange("p (d h c) -> p d h c", d=2, h=HA)
        S1 = A["S1"].rearrange("p (d s h c) -> p d s h c", d=2, s=NS, h=HA)
        decs = sb("decs", [P, 2, 16])
        kT = sb("kT", [P, 3, 128])
        ckv = sb("ckv", [P, 2, 128])
        gqk = A["gqk"].rearrange("p (n c) -> p n c", n=2)
        sga = A["K0"].rearrange("p (h s t) -> p h s t", h=HA, s=NS)
        lbt = sb("lbt", [P, 6, 8])
        small = sb("small", [P, 96])
        catT = hT

        M_SIZES = [("htm", 2048), ("S", 2048), ("ST", 2048), ("xg", 1024), ("sg", 512), ("hid", 512), ("hidT", 512),
                   ("y", 1024), ("r", 1024), ("fhT", 512), ("fh", 512)]
        M = carve(M_SIZES)
        lrow = M["fhT"][:, 0:256]
        mask16 = M["fhT"][:, 256:272].bitcast(BF16)
        htm = M["htm"].rearrange("p (s d) -> p s d", s=NS)
        S = M["S"].rearrange("p (s c) -> p s c", s=NS)
        ST = M["ST"].rearrange("p (g c) -> p g c", g=NPAIR)
        xg = M["xg"].rearrange("p (k c) -> p k c", k=KD)
        hidT = M["hidT"].rearrange("p (f c) -> p f c", f=KF)
        y = M["y"]
        R = {}
        _at = 0
        for name, n in [("lg", 32), ("e", 32), ("score", 32), ("bi", 32), ("gt", 128), ("eq", 128), ("rank", 32),
                        ("selE", 32), ("bs", 32), ("gs", 8), ("grank", 8), ("selG", 8), ("mask", 32), ("w", 32),
                        ("gate", 32), ("pos", 32), ("over", 32), ("c1", 2), ("c2", 2), ("c3", 2), ("cnt", 16),
                        ("mxc", 1), ("gcol", 2)]:
            R[name] = M["r"][:, _at:_at + n]
            _at += n
        flag = sb("flag", [P, 2], I32)

        H = carve([("zz", 2048), ("x1", 2048), ("x0", 2048), ("zt", 2048), ("ub", 4 * 264), ("uc", 4 * 256), ("ya", 1024),
                   ("gap", 480), ("KA", 1024), ("KB", 1024), ("KC", 1024), ("hyc", HYC_N - D), ("yb", 1024)])
        t1 = sqs[:, 0:1024]
        w3s = arena[:, 2048:4096]
        filt = arena[:, 4096:6144]
        decay = arena[:, 16256:17280]
        fw = arena[:, 17280:17408].rearrange("p (n c) -> p n c", n=2)
        hid1 = arena[0:HY, 17408:17920].rearrange("p (n c) -> p n c", n=4)
        assert sum(n for _, n in M_SIZES) <= 11776

        YS = [(H["ya"], H["yb"]), (H["x1"][:, 0:1024], H["x1"][:, 1024:2048])]
        HY_ORDER = list(range(8, 16)) + list(range(16, 24)) + list(range(0, 8))

        fscr = arena[:, 9856:9984]
        PI = float(np.pi)

        def HC(name):
            o, n = HYC[name]
            return H["hyc"][:, o:o + n]

        ring_full = [sem(f"ring_full{i}") for i in range(RING)]
        ring_free = [sem(f"ring_free{i}") for i in range(RING)]
        names = """fw_in rows_in cst_in x_in small_in state_in cache_in hyc_in w3_in decay_in out_done cache_out
            g_const g_rw g_fb t_rows d_rows t_xT a_xT d_xT a_cs a_sq t_ss a_sqrt d_h t_sel a_row a_mod
            a_proj d_ef d_kk a_lf d_x1 a_ea a_eb d_kd d_x2 a_e2 d_aq d_q2 d_kc a_e3 a_e4
            d_xn a_h t_lrow a_lrow d_S g_sg t_att d_att t_kcT a_kcT t_U d_state t_o a_osq t_oss a_osqrt d_oA
            a_qksq d_var a_qksd d_qk t_qkT a_qkT t_sc d_max a_exp t_pT a_pT d_pT t_pv d_o t_oT a_cat d_x
            t_log a_htm d_lg a_re d_mask t_pos t_ST a_ST t_htm
            m_xg a_xg d_xg a_sg d_hid m_hT a_hT d_hT a_y d_y m_sc
            d_flag hy_l1 hy_a1 hy_r1 hy_s1 hy_l2 hy_a2 hy_r2 hy_s2 hy_f hy_fd hy_k a_k t_u a_u d_uc d_zz t_zt a_zt a_zd t_spec
            d_spec t_y d_r t_fin a_fin d_chain a_chain g_chain""".split()
        q = {n: sem(n) for n in names}
        fb = {n: [sem(f"{n}{l}") for l in range(2)] for n in
              ["fb_in", "fb_gate", "fb_silu", "fb_hid", "fb_tr", "fb_hidT", "fb_down", "fb_done", "fb_col"]}

        chain = {"d_chain": 0, "a_chain": 0, "g_chain": 0}

        def link(eng, name, ins):
            chain[name] += 1
            ins.then_inc(q[name], 1)
            eng.wait_ge(q[name], chain[name])

        def unit(n):
            return ring[:, n % RING, :].rearrange("p (k c) -> p k c", k=KD)

        def down_unit(n):
            return ring[:, n % RING, :].rearrange("p (k c) -> p k c", k=KF)

        def arrived(eng, n, more=0):
            eng.wait_ge(ring_full[n % RING], (more + (n // RING + 1)) * 16)

        def products_of(eng, n, more=0):
            eng.wait_ge(ring_free[n % RING], more + (n // RING + 1))

        block = ctx.enter_context(nc.Block())

        @block.sync
        def _(sp):
            def rows_of(name, ap):
                t, r, n = ROWS[name]
                sp.dma_start(rows[r:r + n, t, :], ap).then_inc(q["rows_in"], 16)

            rows = ring[:, RING - 1, 0:384].rearrange("p (t c) -> p t c", t=3)
            rows_of("norm_g", I["norm_g"].rearrange("l i (k p) -> (l i k) p", p=P))
            rows_of("hgrn_lb", I["hgrn_lb"].rearrange("n d (k p) -> (n d k) p", p=P))
            rows_of("onorm", I["hgrn_onorm_g"].rearrange("n (k p) -> (n k) p", p=P))
            rows_of("c", I["c"].rearrange("n (k p) -> (n k) p", p=P))
            rows_of("c_ctx", I["c_ctx"].rearrange("(k p) -> k p", p=P))
            rows_of("dskip", I["hy_dskip"].rearrange("n (k p) -> (n k) p", p=P))
            rows_of("hy_in_b", I["hy_in_b"].rearrange("n (k p) -> (n k) p", p=P))
            rows_of("hy_conv_b", I["hy_conv_b"].rearrange("n (k p) -> (n k) p", p=P))
            rows_of("mod_b", I["mod_b"].rearrange("l (k p) -> (l k) p", p=P))
            rows_of("hy_conv_w", I["hy_conv_w"].rearrange("n w (k p) -> (n w k) p", p=P))

            w_dram = {
                "mod": lambda u: I["mod_w"][u[1]].rearrange("(k p) c -> p k c", p=P)[:, :, u[2] * 512:u[2] * 512 + 512],
                "ab": lambda u: I["ab_in_w"][0].rearrange("(k p) c -> p k c", p=P)[:, :, u[1]:min(u[1] + 512, 3328)],
                "about": lambda u: I["ab_out_w"][0].rearrange("(k p) c -> p k c", p=P)[:, :, u[1] * 512:u[1] * 512 + 512],
                "hyin": lambda u: I["hy_in_w"][0].rearrange("(k p) c -> p k c", p=P)[:, :, u[1] * 512:u[1] * 512 + 512],
                "hyout": lambda u: I["hy_out_w"][0].rearrange("(k p) c -> p k c", p=P)[:, :, u[1] * 512:u[1] * 512 + 512],
            }
            n = 0
            while n < len(UNITS):
                u = UNITS[n]
                if u[0] != "moe":
                    src = w_dram[u[0]](u)
                    if n == RING - 1:
                        sp.wait_ge(q["t_rows"], 1)
                    if n >= RING:
                        sp.wait_ge(ring_free[n % RING], n // RING)
                    sp.dma_start(unit(n)[:, :, 0:src.shape[2]], src).then_inc(ring_full[n % RING], 16)
                    n += 1
                    continue
                l = u[1]
                with sp.Fori(0, NPAIR) as i:
                    for j, (e, w) in enumerate([(0, "gate"), (1, "gate"), (0, "up"), (1, "up"), (0, "down"), (1, "down")]):
                        m = n + j
                        sp.wait_ge(ring_free[m % RING], i + m // RING)
                        src = I["moe_w_" + w][l, bass.ds(i * 2 + e, 1)].rearrange("o (k p) c -> p (o k) c", p=P)
                        dst = down_unit(m) if w == "down" else unit(m)
                        sp.dma_start(dst, src).then_inc(ring_full[m % RING], 16)
                n += 6 * NPAIR
                sp.wait_ge(q["d_flag"], l + 1)
                more = sp.value_load(flag[0:1, l:l + 1])
                with sp.If(more > 0):
                    for m in range(n - 6, n):
                        sp.wait_ge(ring_free[m % RING], m // RING + 1)
                    with sp.Fori(0, NE) as e:
                        sp.wait_ge(fb["fb_done"][l], e * 2 + 1)
                        for j, w in enumerate(["gate", "up", "down"]):
                            src = I["moe_w_" + w][l, bass.ds(e, 1)].rearrange("o (k p) c -> p (o k) c", p=P)
                            dst = down_unit(n + j) if w == "down" else unit(n + j)
                            sp.dma_start(dst, src).then_inc(fb["fb_in"][l], 16)
                    sp.wait_ge(fb["fb_done"][l], 2 * NE + 1)
            sp.wait_ge(q["cache_out"], 16 * 6)
            sp.wait_ge(q["out_done"], 16 * 4)

        @block.gpsimd
        def _(pool):
            nc.gpsimd.memset(ones[:], 1.0).then_inc(q["g_const"], 1)
            nc.gpsimd.memset(eps[:], EPS).then_inc(q["g_const"], 1)
            nc.gpsimd.memset(zero16[:], 0.0).then_inc(q["g_const"], 1)
            link(pool, "g_chain", nc.gpsimd.memset(seg[:], 1.0))
            nc.gpsimd.memset(seg[:].rearrange("p (c t) -> p c t", t=CHUNK)[:, :, 0:1], 0.0).then_inc(q["g_const"], 1)
            nc.gpsimd.memset(csil[:], 0.0).then_inc(q["g_const"], 1)
            nc.gpsimd.memset(rw[:], 0.0).then_inc(q["g_rw"], 1)
            nc.gpsimd.memset(tri16[:, 1], 1.0).then_inc(q["g_const"], 1)
            nc.gpsimd.memset(att[0], 0.0).then_inc(q["g_const"], 1)
            nc.gpsimd.memset(att[1], 0.0).then_inc(q["g_const"], 1)
            pool.wait_ge(q["d_qk"], 1)
            qkt = A["qk"].rearrange("p (s c) -> p s c", s=NS)
            for g in range(KV):
                pool.dma_start(O["new_cache_k"][0, 0, g], qkt[:, 0, 512 + 64 * g:576 + 64 * g]).then_inc(q["cache_out"], 16)
                pool.dma_start(O["new_cache_v"][0, 0, g], A["vb"][:, 64 * g:64 * g + 64]).then_inc(q["cache_out"], 16)
            pool.wait_ge(q["d_state"], 4)
            for d in range(2):
                pool.dma_start(O["new_state"][0, 0, d].rearrange("h k v -> k h v"), Sfin[:, d]).then_inc(q["cache_out"], 16)
            g = nc.gpsimd
            pool.wait_ge(q["small_in"], 16 * 7)
            link(pool, "g_chain", g.tensor_tensor(fcol[0:HY, 3:5], fcol[0:HY, 0:2], fcol[0:HY, 2:3].broadcast_to([HY, 2]), ALU.mult))
            g.tensor_copy(fcol[0:HY, 5:6], fcol[0:HY, 2:3]).then_inc(q["g_fb"], 1)
            C1 = 6.28125
            C2 = 2 * PI - 6.28125
            MAGIC = 12582912.0
            for i in range(2):
                pool.wait_ge(q[["hy_a1", "hy_a2"][i]], 1)
                a, b, c = hid1[:, 2 * i, :], hid1[:, 2 * i + 1, :], hid1[:, 2 - 2 * i, :]
                c = fscr[0:HY, :]
                link(pool, "g_chain", g.tensor_scalar(b, a, 1.0 / (2 * PI), MAGIC, ALU.mult, ALU.add))
                link(pool, "g_chain", g.tensor_scalar(b, b, -MAGIC, None, ALU.add))
                for part in (C1, C2):
                    link(pool, "g_chain", g.tensor_scalar(c, b, -part, None, ALU.mult))
                    link(pool, "g_chain", g.tensor_tensor(a, a, c, ALU.add))
                g.tensor_scalar(a, a, PI, -PI, ALU.min, ALU.max).then_inc(q[["hy_r1", "hy_r2"][i]], 1)
            sgt = sqs[:, 0:2048].rearrange("p (s e c) -> p s e c", s=NS, e=NE)
            for l in range(2):
                for s in range(NS):
                    pool.wait_ge(q["d_S"], 2 * l + s + 1)
                    g.tensor_tensor(sgt[:, s], S[:, s].rearrange("p (e c) -> p e c", e=NE),
                                    R["gate"][:, s * NE:s * NE + NE].rearrange("p (e o) -> p e o", o=1).broadcast_to([P, NE, CAP]),
                                    ALU.mult).then_inc(q["g_sg"], 1)

        @block.scalar
        def _(act):
            def dma(dst, src, s):
                act.dma_start(dst, src).then_inc(q[s], 16)

            xin = arena[:, 0:2048].rearrange("p (s d) -> p s d", s=NS)
            dma(cst[:], I["cst"], "cst_in")
            dma(xin[:, 0], I["x_prompt"][0], "x_in")
            dma(xin[:, 1], I["x_sample"][0], "x_in")
            act.wait_ge(q["g_rw"], 1)
            dma(rw[:, :, 0:NE], I["router_w"].rearrange("(k p) e -> p k e", p=P), "small_in")
            dma(rb[:], I["router_b"].rearrange("(a e) -> a e", a=1).broadcast_to([P, NE]), "small_in")
            dma(gqk[:, 0], I["attn_qnorm_g"].broadcast_to([P, HD]), "small_in")
            dma(gqk[:, 1], I["attn_knorm_g"].broadcast_to([P, HD]), "small_in")
            for c, n in enumerate(["hy_f_b1", "hy_f_b2", "hy_f_freq"]):
                dma(fcol[0:HY, c:c + 1], I[n].rearrange("n (c a) -> (n c) a", a=1), "small_in")
            for g in range(KV):
                dma(ckv[:, 0, 64 * g:64 * g + 64], I["cache_k"][0, 0, g], "cache_in")
                dma(ckv[:, 1, 64 * g:64 * g + 64], I["cache_v"][0, 0, g], "cache_in")

            def act_fn(out, in_, f, **k):
                return nc.scalar.activation(out, in_, f, **k)

            xf = xT[:].rearrange("p k s t -> p (k s t)")
            sqf = sqs[:, 0:2048]
            act.wait_ge(q["d_rows"], 1)
            for s, n in enumerate(["c_ctx", "c"]):
                if s == 0:
                    act.wait_ge(q["g_const"], 8)
                ins = act_fn(csil[:, :, s], V(n), ACT.Silu)
            ins.then_inc(q["a_cs"], 1)
            act.wait_ge(q["t_xT"], 1)
            nc.scalar.copy(xf[:, 1024:2048], bank(2, 2)).then_inc(q["a_xT"], 1)

            def norm(n):
                for half in range(2):
                    sl = slice(half * 1024, half * 1024 + 1024)
                    if n:
                        act.wait_ge(q["d_x"], 2 * n - 1 + half)
                    elif half:
                        act.wait_ge(q["a_xT"], 1)
                    else:
                        act.wait_ge(q["d_xT"], 1)
                    act_fn(sqf[:, sl], xf[:, sl], ACT.Square).then_inc(q["a_sq"], 1)
                act.wait_ge(q["t_ss"], n + 1)
                act.wait_ge(q["g_const"], 8)
                act_fn(rstd[:].rearrange("p s t -> p (s t)"), bank(7)[:, 0:256], ACT.Sqrt, bias=eps[:],
                       scale=1.0 / D).then_inc(q["a_sqrt"], 1)

            def scaled(n):
                l, i = n // 2, n % 2
                act.wait_ge(q["d_xn"], n + 1)
                for k in range(4, KD):
                    for s in range(NS):
                        ins = act_fn(hT[:, k, s, :], sq[:, k, s, :], ACT.Identity, bias=modT[:, l, 24 * i + k, s:s + 1],
                                     scale=scl[:, n, k, s:s + 1])
                ins.then_inc(q["a_h"], 1)

            def mod_row(m):
                products_of(act, MOD_AT[m])
                nc.scalar.copy(A["mrow"], bank(6)[:, 0:128]).then_inc(q["a_row"], 1)

            def mod_col(m):
                act.wait_ge(q["t_sel"], m + 1)
                j = m % 12 * 4
                nc.scalar.copy(modT[:, m // 12, j:j + 4], bank(6)[:, 0:128].rearrange("p (g c) -> p g c", g=4)[:, :, 0:NS]
                               ).then_inc(q["a_mod"], 1)

            norm(0)
            for m in range(4):
                mod_row(m)
                mod_col(m)
            scaled(0)
            act.wait_ge(q["d_ef"], 1)
            act_fn(lbt[:, 3:5], lbt[:, 1:3], ACT.Exp).then_inc(q["a_e4"], 1)
            act.wait_ge(q["a_h"], 1)
            act.wait_ge(q["d_h"], 4)
            for d in range(2):
                dma(S0[:, d], I["state_hgrn"][0, 0, d].rearrange("h k v -> k h v"), "state_in")
            qkt = A["qk"].rearrange("p (s c) -> p s c", s=NS)

            def proj_out(j):
                products_of(act, AB_AT[j])
                src = bank(2 * (j % 2), 2)
                sv = src.rearrange("p (s c) -> p s c", s=NS)
                if j in (ZF, ZB):
                    ins = act_fn(E[j], src, ACT.Exp, scale=-1.0)
                elif j in (QA, IA):
                    ins = nc.scalar.copy(A["q" if j == QA else "v"], src)
                elif j == QB:
                    ins = nc.scalar.copy(qkt[:, :, 0:512], sv)
                elif j == KVB:
                    link(act, "a_chain", nc.scalar.copy(qkt[:, :, 512:640], sv[:, :, 0:128]))
                    ins = nc.scalar.copy(A["vb"].rearrange("p (s c) -> p s c", s=NS), sv[:, :, 128:256])
                else:
                    act.wait_ge(q["t_kcT"], 2)
                    ins = act_fn(A["K0"], src, ACT.Silu)
                ins.then_inc(q["a_proj"], 1)
                if j == KVB:
                    act.wait_ge(q["a_proj"], KVB + 1)
                    act_fn(sqk, A["qk"], ACT.Square).then_inc(q["a_qksq"], 1)
                    act.wait_ge(q["d_var"], 1)
                    act_fn(small[:, 20:40], small[:, 0:20], ACT.Sqrt, bias=eps[:], scale=1.0 / HD).then_inc(q["a_qksd"], 1)

            def exponentials(s):
                act.wait_ge(q["d_max"], 2 - s)
                n, probs, b = (256, probs_s, bank(0, 4)) if s else (128, probs_p, bank(4, 2))
                c = 0 if s else 8
                for h in range(HB):
                    ins = act_fn(probs[:, h * n:h * n + n], b[:, h * n:h * n + n], ACT.Exp, bias=small[:, 48 + c + h:49 + c + h],
                                 scale=HD ** -0.5, accum_out=small[:, 64 + c + h:65 + c + h])
                ins.then_inc(q["a_exp"], 1)

            for step in SCHED:
                what, a = step[0], step[1:]
                if what == "R":
                    mod_row(*a)
                elif what == "S":
                    mod_col(*a)
                elif what == "proj" and a[1] == 3:
                    proj_out(a[0])
                elif what == "lf":
                    act.wait_ge(q["d_kk"], a[0] + 1)
                    act_fn(E[a[0]], E[a[0]], ACT.Ln).then_inc(q["a_lf"], 1)
                elif what == "ex":
                    d = a[0]
                    act.wait_ge(q["d_x1"], d + 1)
                    act_fn(E[d], X[d], ACT.Exp).then_inc(q["a_ea"], 1)
                    act.wait_ge(q["a_ea"], d + 1)
                    act_fn(X[d], X[d], ACT.Exp, scale=-1.0).then_inc(q["a_eb"], 1)
                    act.wait_ge(q["d_x2"], d + 1)
                    act_fn(A["tmp"], A["tmp"], ACT.Exp).then_inc(q["a_e2"], 1)
                    act_fn(B[d], B[d], ACT.Exp).then_inc(q["a_e3"], 1)
                elif what == "qkT":
                    act.wait_ge(q["t_qkT"], 1)
                    nc.scalar.copy(qT[:, 0].rearrange("p c t -> p (c t)"), bank(4))
                    nc.scalar.copy(qT[:, 1].rearrange("p c t -> p (c t)"), bank(5))
                    nc.scalar.copy(kT[:].rearrange("p c t -> p (c t)"), bank(7)[:, 0:384]).then_inc(q["a_qkT"], 1)
                elif what == "kc":
                    act.wait_ge(q["t_kcT"], a[0] * 2 + a[1] + 1)
                    nc.scalar.copy(A["kcT"], bank(7)).then_inc(q["a_kcT"], 1)
                elif what == "o":
                    act.wait_ge(q["t_o"], 1)
                    for half in range(2):
                        act_fn(sqs[:, half * 512:half * 512 + 512], bank(4 + half), ACT.Square).then_inc(q["a_osq"], 1)
                elif what in ("ex1", "ex0"):
                    exponentials(int(what[2]))
                elif what == "oss":
                    act.wait_ge(q["t_oss"], a[0] + 1)
                    act_fn(osd[:, a[0] * 512:a[0] * 512 + 512], bank(7), ACT.Sqrt, bias=eps[:],
                           scale=1.0 / 128).then_inc(q["a_osqrt"], 1)
                elif what == "pT":
                    act.wait_ge(q["t_pT"], 2 - a[0])
                    if a[0]:
                        nc.scalar.copy(pT_s[:, 0:1024], bank(0, 2)).then_inc(q["a_pT"], 1)
                    else:
                        nc.scalar.copy(pT_p, bank(4, 2)).then_inc(q["a_pT"], 1)
                elif what == "oT":
                    s = a[0]
                    act.wait_ge(q["t_oT"], 2 - s)
                    nc.scalar.copy(catT[:, 4:8, s, :], bank(1 if s else 2).rearrange("p (c t) -> p c t", c=4)).then_inc(q["a_cat"], 1)

            def moe(l):
                norm(2 * l + 1)
                scaled(2 * l + 1)
                act.wait_ge(q["t_lrow"], l + 1)
                nc.scalar.copy(lrow, bank(0)[:, 0:256]).then_inc(q["a_lrow"], 1)
                act.wait_ge(q["d_lg"], l + 1)
                act_fn(R["e"], R["lg"], ACT.Exp).then_inc(q["a_re"], 1)
                if l == 0:
                    spectrum(1)
                    spectrum(2)
                act.wait_ge(q["t_htm"], l + 1)
                nc.scalar.copy(M["htm"], bank(0, 4)).then_inc(q["a_htm"], 1)
                n0 = l * NPAIR

                def pair(i, first=False):
                    act.wait_ge(q["m_xg"], i + (n0 + 1))
                    nc.scalar.copy(xg[:, 0:4, :].rearrange("p k c -> p (k c)"), bank(4)).then_inc(q["a_xg"], 1)
                    products_of(act, MOE_AT[l] + 1, i)
                    act_fn(M["sg"], bank(4), ACT.Silu).then_inc(q["a_sg"], 1)
                    if first:
                        act.wait_ge(q["t_ST"], l + 1)
                        nc.scalar.copy(M["ST"], bank(0, 4)).then_inc(q["a_ST"], 1)
                    act.wait_ge(q["m_hT"], i + (n0 + 1))
                    nc.scalar.copy(M["hidT"][:, 0:256], bank(6)[:, 0:256]).then_inc(q["a_hT"], 1)
                    products_of(act, MOE_AT[l] + 5, i)
                    nc.scalar.copy(y[:, 0:512], bank(6)).then_inc(q["a_y"], 1)

                pair(0, True)
                with act.Fori(1, NPAIR - 1) as i:
                    pair(i)
                pair(NPAIR - 1)
                act.wait_ge(q["d_flag"], l + 1)
                more = act.value_load(flag[0:1, l:l + 1])
                with act.If(more > 0):
                    with act.Fori(0, NE) as e:
                        for s in range(NS):
                            act.wait_ge(fb["fb_gate"][l], e * 2 + (s + 1))
                            act_fn(M["fh"], bank(4), ACT.Silu).then_inc(fb["fb_silu"][l], 1)

            def spectrum(i):
                act.wait_ge(q["hy_k"], i + 1)
                nc.scalar.copy(H[["KA", "KB", "KC"][i]], bank([1, 3, 5][i], 2)).then_inc(q["a_k"], 1)

            act.wait_ge(q["cache_out"], 16 * 6)
            act.dma_start(fw[0:EMB, 0], I["hy_f_w1"][0]).then_inc(q["fw_in"], 16)
            act.dma_start(fw[0:HY, 1], I["hy_f_w2"][0]).then_inc(q["fw_in"], 16)
            act.dma_start(H["hyc"], I["hyc"][:, 0:HYC_N - D]).then_inc(q["hyc_in"], 16)
            act.dma_start(w3s[0:HY, :], I["hy_f_w3"][0]).then_inc(q["w3_in"], 16)
            act.dma_start(decay, I["hyc"][:, HYC_N - D:]).then_inc(q["decay_in"], 16)
            act.wait_ge(q["g_fb"], 1)
            for i in range(2):
                act.wait_ge(q[["hy_l1", "hy_l2"][i]], 1)
                act_fn(hid1[:, 2 * i, :], bank(6)[0:HY, 256 * i:256 * i + 128], ACT.Identity, bias=fcol[0:HY, 3 + i:4 + i],
                       scale=fcol[0:HY, 5:6]).then_inc(q[["hy_a1", "hy_a2"][i]], 1)
                act.wait_ge(q[["hy_r1", "hy_r2"][i]], 1)
                act_fn(hid1[:, 1 + 2 * i, :], hid1[:, 2 * i, :], ACT.Sin).then_inc(q[["hy_s1", "hy_s2"][i]], 1)
            spectrum(0)
            moe(0)
            norm(2)
            scaled(2)
            for j in range(24):
                if j % 4 == 3:
                    products_of(act, HYIN_AT + j // 4)
                else:
                    act.wait_ge(q["t_u"], j // 4 * 3 + j % 4 + 1)
                ch = HY_ORDER[j]
                b = j % 4
                if j >= 4:
                    act.wait_ge(q["d_uc"], j - 3)
                ub = H["ub"].rearrange("p (b s t) -> p b s t", b=4, s=NS)[:, b, :, 1:T + 1]
                act_fn(ub, bank(4 + b)[:, 0:256].rearrange("p (s t) -> p s t", s=NS), ACT.Identity,
                       bias=V("hy_in_b")[:, ch:ch + 1]).then_inc(q["a_u"], 1)
                if j in (16, 17):
                    s = j - 16
                    act.wait_ge(q["t_zt"], s + 1)
                    nc.scalar.copy(H["zt"][:, s * 1024:s * 1024 + 1024], bank(2 * s, 2)).then_inc(q["a_zt"], 1)
                if j == 18:
                    z3 = H["zz"].rearrange("p (k c) -> p k c", k=KD)
                    for k in range(KD):
                        ins = act_fn(z3[:, k], z3[:, k], ACT.Identity, scale=V("dskip")[:, k:k + 1])
                    ins.then_inc(q["a_zd"], 1)
            moe(1)
            act.wait_ge(q["t_fin"], 1)
            fin = arena[:, 0:2048].rearrange("p (s d) -> p s d", s=NS)
            nc.scalar.copy(arena[:, 0:2048], bank(0, 4)).then_inc(q["a_fin"], 1)
            act.wait_ge(q["a_fin"], 1)
            for s, o in enumerate(["y_prompt", "y_sample"]):
                act.dma_start(O[o][0, 0:64], fin[0:64, s]).then_inc(q["out_done"], 16)
                act.dma_start(O[o][0, 64:128], fin[64:128, s]).then_inc(q["out_done"], 16)

        @block.vector
        def _(dve):
            v = nc.vector

            def L(ins):
                link(dve, "d_chain", ins)

            dve.wait_ge(q["t_rows"], 1)
            L(v.tensor_copy(VT[:, 0, 0:124], bank(7)[:, 0:124]))
            L(v.tensor_copy(VT[:, 1, 0:96], bank(7)[:, 128:224]))
            v.tensor_copy(VT[:, 2, 0:72], bank(7)[:, 256:328]).then_inc(q["d_rows"], 1)
            dve.wait_ge(q["t_xT"], 1)
            xf = xT[:].rearrange("p k s t -> p (k s t)")
            v.tensor_copy(xf[:, 0:1024], bank(0, 2)).then_inc(q["d_xT"], 1)

            def norm(n):
                l, i = n // 2, n % 2
                dve.wait_ge(q["a_sqrt"], n + 1)
                L(v.reciprocal(rstd[:], rstd[:]))
                if n == 0:
                    mod(0)
                for s in range(NS):
                    L(v.scalar_tensor_tensor(out=scl[:, n, :, s], in0=modT[:, l, 24 * i + 8:24 * i + 16, s], scalar=1.0,
                                             in1=V("norm_g")[:, 8 * n:8 * n + 8], op0=ALU.add, op1=ALU.mult))
                for half in (1, 0):
                    ks = slice(4 * half, 4 * half + 4)
                    ins = v.tensor_tensor(sq[:, ks], xT[:, ks], rstd[:].rearrange("p (o s) t -> p o s t", o=1).broadcast_to([P, 4, NS, T]), ALU.mult)
                    if half:
                        ins.then_inc(q["d_xn"], 1)
                L(ins)
                for k in range(4):
                    for s in range(NS):
                        ins = v.tensor_scalar(hT[:, k, s, :], sq[:, k, s, :], scl[:, n, k, s:s + 1],
                                              modT[:, l, 24 * i + k, s:s + 1], ALU.mult, ALU.add)
                    ins.then_inc(q["d_h"], 1)

            MODS_DONE = [(0, 0, 16), (0, 16, 48), (1, 0, 48)]

            def mod(g):
                l, a, b = MODS_DONE[g]
                dve.wait_ge(q["a_mod"], [4, 12, 24][g])
                bias = V("mod_b")[:, 48 * l + a:48 * l + b].rearrange("p (j o) -> p j o", o=1).broadcast_to([P, b - a, NS])
                L(v.tensor_tensor(modT[:, l, a:b], modT[:, l, a:b], bias, ALU.add))

            lb = V("hgrn_lb")
            L(v.tensor_tensor(lbt[:, 0], lb[:, 0:8], lb[:, 8:16], ALU.max))
            L(v.tensor_tensor(lbt[:, 1], lb[:, 0:8], lbt[:, 0], ALU.subtract))
            v.tensor_tensor(lbt[:, 2], lb[:, 8:16], lbt[:, 0], ALU.subtract).then_inc(q["d_ef"], 1)
            norm(0)
            dve.wait_ge(q["a_e4"], 1)
            L(v.tensor_tensor(lbt[:, 5], lbt[:, 3], lbt[:, 4], ALU.add))
            L(v.reciprocal(lbt[:, 5], lbt[:, 5]))
            L(v.tensor_tensor(lbt[:, 0], lbt[:, 3], lbt[:, 5], ALU.mult))
            L(v.tensor_tensor(lbt[:, 1], lbt[:, 4], lbt[:, 5], ALU.mult))
            def gates(d):
                dve.wait_ge(q["a_proj"], d + 1)
                L(v.tensor_scalar(E[d], E[d], 1.0, None, ALU.add))
                L(v.reciprocal(E[d], E[d]))
                for h in range(HA):
                    sl = slice(h * 256, h * 256 + 256)
                    ins = v.tensor_scalar(E[d][:, sl], E[d][:, sl], lbt[:, 1, 4 * d + h:4 * d + h + 1],
                                          lbt[:, 0, 4 * d + h:4 * d + h + 1], ALU.mult, ALU.add)
                L(ins)
                v.tensor_scalar(K[d], E[d], -1.0, 1.0, ALU.mult, ALU.add).then_inc(q["d_kk"], 1)

            def decays(d):
                mid, last = [(CHUNK // 2, CHUNK - 1), (CHUNK - 1 - CHUNK // 2, 0)][d]
                dve.wait_ge(q["a_lf"], d + 1)
                if d == 0:
                    dve.wait_ge(q["g_const"], 8)
                    L(v.tensor_tensor_scan(B[d], seg[:], E[d], 0.0, ALU.mult, ALU.add))
                else:
                    L(v.tensor_tensor_scan(B[d][:, ::-1], seg[:], E[d][:, ::-1], 0.0, ALU.mult, ALU.add))
                b3 = B[d].rearrange("p (c t) -> p c t", t=CHUNK)
                x3 = X[d].rearrange("p (c t) -> p c t", t=CHUNK)
                t3 = A["tmp"].rearrange("p (c t) -> p c t", t=CHUNK)
                v.tensor_tensor(x3, b3, b3[:, :, mid:mid + 1].broadcast_to([P, 16, CHUNK]), ALU.subtract).then_inc(q["d_x1"], 1)
                if d == 1:
                    dve.wait_ge(q["d_kc"], 1)
                v.tensor_tensor(t3, b3[:, :, last:last + 1].broadcast_to([P, 16, CHUNK]), b3, ALU.subtract).then_inc(q["d_x2"], 1)
                dve.wait_ge(q["a_eb"], d + 1)
                v.tensor_tensor(X[d], X[d], K[d], ALU.mult).then_inc(q["d_kd"], 1)
                dve.wait_ge(q["a_e3"], d + 1)
                dve.wait_ge(q["d_kd"], d + 1)
                L(v.tensor_copy(decs[:, d, :], B[d].rearrange("p (c t) -> p c t", t=CHUNK)[:, :, last]))
                v.tensor_tensor(K[d], K[d], A["tmp"], ALU.mult).then_inc(q["d_kc"], 1)

            for d in range(2):
                gates(d)
                decays(d)
            dve.wait_ge(q["a_qksq"], 1)
            v.tensor_reduce(small[:, 0:20], sqk.rearrange("p (n c) -> p n c", c=HD), AX.X, ALU.add).then_inc(q["d_var"], 1)
            dve.wait_ge(q["a_qksd"], 1)
            dve.wait_ge(q["small_in"], 16 * 7)
            L(v.reciprocal(small[:, 20:40], small[:, 20:40]))
            qk4 = A["qk"].rearrange("p (s n c) -> p s n c", s=NS, c=HD)
            rs = small[:, 20:40].rearrange("p (s n o) -> p s n o", s=NS, o=1)
            for s in range(NS):
                L(v.tensor_tensor(qn[:, s].rearrange("p (c g) d -> p g c d", g=KV),
                                  qk4[:, s, 0:8].rearrange("p (g c) d -> p g c d", g=KV),
                                  rs[:, s, 0:8].rearrange("p (g c) o -> p g c o", g=KV).broadcast_to([P, KV, 4, HD]), ALU.mult))
                L(v.tensor_tensor(qk4[:, s, 8:10], qk4[:, s, 8:10], rs[:, s, 8:10].broadcast_to([P, KV, HD]), ALU.mult))
                L(v.tensor_tensor(qn[:, s], qn[:, s], gqk[:, 0:1].broadcast_to([P, 8, HD]), ALU.mult))
                L(v.tensor_tensor(qk4[:, s, 8:10], qk4[:, s, 8:10], gqk[:, 1:2].broadcast_to([P, 2, HD]), ALU.mult))
            s4 = C("sin").rearrange("p (o r h c) -> p o r h c", o=1, r=2, h=2)
            for xs, t2, n in [(qn[:, 1], A["qk"][:, 0:512], 8), (qk4[:, 1, 8:10], A["qk"][:, 640:768], 2)]:
                t24 = t2.rearrange("p (n r h c) -> p n r h c", r=2, h=2, c=16)
                x4 = xs.rearrange("p n (r h c) -> p n r h c", r=2, h=2)
                for hh in range(2):
                    L(v.tensor_tensor(t24[:, :, :, hh], x4[:, :, :, 1 - hh], s4[:, :, :, hh].broadcast_to([P, n, 2, 16]), ALU.mult))
                L(v.tensor_tensor(xs, xs, C("cos").rearrange("p (o c) -> p o c", o=1).broadcast_to([P, n, HD]), ALU.mult))
                ins = v.tensor_tensor(xs, xs, t2.rearrange("p (n c) -> p n c", c=HD), ALU.add)
                if n == 8:
                    L(ins)
            ins.then_inc(q["d_qk"], 1)
            dve.wait_ge(q["a_proj"], QA + 1)
            for d in range(2):
                v.tensor_tensor(E[d], E[d], A["q"], ALU.mult).then_inc(q["d_aq"], 1)
            for d in range(2):
                v.tensor_tensor(B[d], B[d], A["q"], ALU.mult).then_inc(q["d_q2"], 1)
            for d in range(2):
                dve.wait_ge(q["t_att"], d + 1)
                a4 = att[d].rearrange("p (n t) -> p n t", t=T)
                src = bank(4 + d).rearrange("p (n t) -> p n t", t=CHUNK)
                m = C("mask_r" if d else "mask_f").bitcast(U32)
                for c in range(2):
                    rows = slice(c * 64, c * 64 + 64)
                    mb = m[rows].rearrange("p (o t) -> p o t", o=1).broadcast_to([64, 8, CHUNK])
                    ins = v.copy_predicated(a4[rows, :, c * 64:c * 64 + 64], mb, src[rows])
                ins.then_inc(q["d_att"], 1)
            dve.wait_ge(q["state_in"], 32)
            for d in range(2):
                first, second = (0, 1) if d == 0 else (1, 0)
                dec = decs[:, d, :].rearrange("p (h s c) -> p h s c", h=HA, s=NS)
                Uf, Us = (bank(b).rearrange("p (h c) -> p h c", h=HA) for b in (4, 5))
                dve.wait_ge(q["t_U"], 2 * d + 1)
                L(v.tensor_copy(S1[:, d, 0], Uf))
                for h in range(HA):
                    ins = v.scalar_tensor_tensor(out=Sfin[:, d, h], in0=S1[:, d, 0, h],
                                                 scalar=dec[:, h, 0, second:second + 1],
                                                 in1=Us[:, h], op0=ALU.mult, op1=ALU.add)
                ins.then_inc(q["d_state"], 1)
                dve.wait_ge(q["t_U"], 2 * d + 2)
                for h in range(HA):
                    ins = v.scalar_tensor_tensor(out=S1[:, d, 1, h], in0=S0[:, d, h], scalar=dec[:, h, 1, first:first + 1],
                                                 in1=Uf[:, h], op0=ALU.mult, op1=ALU.add)
                ins.then_inc(q["d_state"], 1)

            def score_max(s, b, nb, keys, at):
                dve.wait_ge(q["t_sc"], 2 - s)
                L(v.tensor_reduce(small[:, at:at + 8], bank(b, nb).rearrange("p (h c) -> p h c", c=keys), AX.X, ALU.max))
                v.tensor_scalar(small[:, at:at + 8], small[:, at:at + 8], -HD ** -0.5, None, ALU.mult).then_inc(q["d_max"], 1)

            score_max(1, 0, 4, 256, 48)
            for half in range(2):
                dve.wait_ge(q["a_osqrt"], half + 1)
                r = osd[:, half * 512:half * 512 + 512]
                L(v.reciprocal(r, r))
                L(v.tensor_tensor(r, bank(4 + half), r, ALU.mult))
            dve.wait_ge(q["a_proj"], 7)
            for h in range(HA):
                r4 = osd.rearrange("p (s h t) -> p s h t", s=NS, h=HA)
                ins = v.scalar_tensor_tensor(out=catT[:, h], in0=r4[:, :, h], scalar=V("onorm")[:, h:h + 1],
                                             in1=sga[:, h], op0=ALU.mult, op1=ALU.mult)
            ins.then_inc(q["d_oA"], 1)
            dve.wait_ge(q["t_pT"], 1)
            v.tensor_copy(pT_s[:, 1024:2048], bank(2, 2)).then_inc(q["d_pT"], 1)
            score_max(0, 4, 2, 128, 56)
            for s, b, sums in [(1, 7, 64), (0, 0, 72)]:
                dve.wait_ge(q["t_pv"], 2 - s)
                L(v.reciprocal(small[:, sums:sums + 8], small[:, sums:sums + 8]))
                v.tensor_tensor(otm[:, s * 512:s * 512 + 512].rearrange("p (h c) -> p h c", c=HD),
                                bank(b).rearrange("p (h c) -> p h c", c=HD),
                                small[:, sums:sums + 8].rearrange("p (h o) -> p h o", o=1).broadcast_to([P, 8, HD]),
                                ALU.mult).then_inc(q["d_o"], 1)
            mod(1)
            mod(2)

            def residual(l, g, banks, units=None):
                for k in range(KD):
                    if units is not None and k % 4 == 0:
                        products_of(dve, units + k // 4)
                    for s in range(NS):
                        src = bank(banks[k // 2])[:, (k % 2) * 256 + s * 128:(k % 2) * 256 + s * 128 + 128]
                        ins = v.scalar_tensor_tensor(out=xT[:, k, s, :], in0=src, scalar=modT[:, l, g * 8 + k, s:s + 1],
                                                     in1=xT[:, k, s, :], op0=ALU.mult, op1=ALU.add)
                    if units is not None and k % 4 == 3:
                        ins.then_inc(q["d_x"], 1)
                if units is None:
                    L(ins)

            dve.wait_ge(q["decay_in"], 16)
            for i in range(2):
                dve.wait_ge(q["hy_f"], i + 1)
                v.tensor_tensor(filt[:, i * 1024:i * 1024 + 1024], bank([1, 6][i], 2), decay, ALU.mult).then_inc(q["hy_fd"], 1)
            residual(0, 2, [0, 3, 4, 5], OUT0_AT)
            L(v.tensor_copy(tri16[:, 0], C("tri")))

            def rank(bi, n, gt, eq, out):
                bj = bi.rearrange("p (n o j) -> p n o j", o=1, j=4).broadcast_to([P, n, 4, 4])
                b_i = bi.rearrange("p (n i o) -> p n i o", i=4, o=1).broadcast_to([P, n, 4, 4])
                g4 = gt.rearrange("p (n i j) -> p n i j", i=4, j=4)
                e4 = eq.rearrange("p (n i j) -> p n i j", i=4, j=4)
                L(v.tensor_tensor(g4, bj, b_i, ALU.is_gt))
                L(v.tensor_tensor(e4, bj, b_i, ALU.is_equal))
                e3 = eq.rearrange("p (n i) -> p n i", i=16)
                L(v.tensor_tensor(e3, e3, C("tie").rearrange("p (o c) -> p o c", o=1).broadcast_to([P, n, 16]), ALU.mult))
                L(v.tensor_tensor(gt, gt, eq, ALU.add))
                L(v.tensor_reduce(out, gt.rearrange("p (n j) -> p n j", j=4), AX.X, ALU.add))

            def moe(l):
                if l == 0:
                    dve.wait_ge(q["cache_out"], 16 * 6)
                norm(2 * l + 1)

                def col(a, n):
                    return a.rearrange("p (s o) -> p s o", o=1).broadcast_to([P, NS, n])

                def g3(a):
                    return a.rearrange("p (s e) -> p s e", s=NS)

                dve.wait_ge(q["t_log"], l + 1)
                lg = g3(bank(7)[:, 256:288])
                L(v.tensor_reduce(R["c1"], lg, AX.X, ALU.max))
                v.tensor_tensor(g3(R["lg"]), lg, col(R["c1"], NE), ALU.subtract).then_inc(q["d_lg"], 1)
                dve.wait_ge(q["a_re"], l + 1)
                L(v.tensor_reduce(R["c2"], g3(R["e"]), AX.X, ALU.add))
                L(v.reciprocal(R["c2"], R["c2"]))
                L(v.tensor_tensor(g3(R["score"]), g3(R["e"]), col(R["c2"], NE), ALU.mult))
                L(v.tensor_tensor(g3(R["bi"]), g3(R["score"]),
                                  rb[:].rearrange("p (o e) -> p o e", o=1).broadcast_to([P, NS, NE]), ALU.add))
                rank(R["bi"], 8, R["gt"], R["eq"], R["rank"])
                L(v.tensor_scalar(R["selE"], R["rank"], 1.5, None, ALU.is_lt))
                L(v.tensor_tensor(R["bs"], R["bi"], R["selE"], ALU.mult))
                L(v.tensor_reduce(R["gs"], R["bs"].rearrange("p (n j) -> p n j", j=4), AX.X, ALU.add))
                rank(R["gs"], 2, R["gt"][:, 0:32], R["eq"][:, 0:32], R["grank"])
                L(v.tensor_scalar(R["selG"], R["grank"], 0.5, None, ALU.is_lt))
                L(v.tensor_tensor(R["mask"].rearrange("p (n j) -> p n j", j=4), R["selE"].rearrange("p (n j) -> p n j", j=4),
                                  R["selG"].rearrange("p (n o) -> p n o", o=1).broadcast_to([P, 8, 4]), ALU.mult))
                v.tensor_copy(mask16[:, 0:32], R["mask"]).then_inc(q["d_mask"], 1)
                L(v.tensor_tensor(R["w"], R["score"], R["mask"], ALU.mult))
                L(v.tensor_reduce(R["c3"], g3(R["w"]), AX.X, ALU.add))
                L(v.reciprocal(R["c3"], R["c3"]))
                L(v.tensor_tensor(g3(R["gate"]), g3(R["w"]), col(R["c3"], NE), ALU.mult))
                dve.wait_ge(q["t_pos"], l + 1)
                pos = bank(7)[:, 288:320]
                L(v.tensor_scalar(R["over"], pos, CAP - 0.5, None, ALU.is_gt))
                L(v.tensor_tensor(R["over"], R["over"], R["gate"], ALU.mult))
                L(v.tensor_scalar(R["pos"], pos, 1.0, None, ALU.add))
                L(v.tensor_tensor(R["pos"], R["pos"], R["mask"], ALU.mult))
                L(v.tensor_scalar(R["pos"], R["pos"], -1.0, None, ALU.add))
                L(v.tensor_reduce(R["mxc"], bank(7)[:, 320:336], AX.X, ALU.max))
                v.tensor_scalar(flag[:, l:l + 1], R["mxc"], CAP + 0.5, None, ALU.is_gt).then_inc(q["d_flag"], 1)
                for s in range(NS):
                    s3 = S[:, s].rearrange("p (e c) -> p e c", e=NE)
                    v.tensor_tensor(s3, C("slot").rearrange("p (o c) -> p o c", o=1).broadcast_to([P, NE, CAP]),
                                    R["pos"][:, s * NE:s * NE + NE].rearrange("p (e o) -> p e o", o=1).broadcast_to([P, NE, CAP]),
                                    ALU.is_equal).then_inc(q["d_S"], 1)
                n0, n2 = l * NPAIR, 2 * l * NPAIR

                def pair(i):
                    dve.wait_ge(q["m_xg"], i + (n0 + 1))
                    v.tensor_copy(xg[:, 4:8, :].rearrange("p k c -> p (k c)"), bank(5)).then_inc(q["d_xg"], 1)
                    dve.wait_ge(q["a_sg"], i + (n0 + 1))
                    products_of(dve, MOE_AT[l] + 3, i)
                    for half in range(2):
                        c = half * 256
                        v.tensor_tensor(M["hid"][:, c:c + 256], bank(5)[:, c:c + 256], M["sg"][:, c:c + 256],
                                        ALU.mult).then_inc(q["d_hid"], 1)
                    dve.wait_ge(q["m_hT"], i + (n0 + 1))
                    v.tensor_copy(M["hidT"][:, 256:512], bank(7)[:, 0:256]).then_inc(q["d_hT"], 1)
                    products_of(dve, MOE_AT[l] + 5, i)
                    v.tensor_copy(y[:, 512:1024], bank(7)).then_inc(q["d_y"], 1)

                pair(0)
                with dve.Fori(1, NPAIR - 1) as i:
                    pair(i)
                pair(NPAIR - 1)
                dve.wait_ge(q["m_sc"], (l + 1) * NPAIR)
                residual(l, 5, [0, 1, 2, 3])
                dve.wait_ge(q["d_flag"], l + 1)
                more = dve.value_load(flag[0:1, l:l + 1])
                with dve.If(more > 0):
                    v.tensor_copy(small[:, 91:92], xT[:, 0, 0, 0:1]).then_inc(fb["fb_done"][l], 1)
                    with dve.Fori(0, NE) as e:
                        for s in range(NS):
                            v.tensor_copy(R["gcol"][:, s:s + 1], R["over"][:, bass.ds(e + s * NE, 1)]).then_inc(fb["fb_col"][l], 1)
                            dve.wait_ge(fb["fb_col"][l], e * 2 + (s + 1))
                            dve.wait_ge(fb["fb_silu"][l], e * 2 + (s + 1))
                            v.scalar_tensor_tensor(out=M["fh"], in0=bank(5), scalar=R["gcol"][:, s:s + 1], in1=M["fh"],
                                                   op0=ALU.mult, op1=ALU.mult).then_inc(fb["fb_hid"][l], 1)
                            dve.wait_ge(fb["fb_tr"][l], e * 2 + (s + 1))
                            v.tensor_copy(M["fhT"], bank(6)).then_inc(fb["fb_hidT"][l], 1)
                            dve.wait_ge(fb["fb_down"][l], e * 2 + (s + 1))
                            for k in range(KD):
                                ins = v.scalar_tensor_tensor(
                                    out=xT[:, k, s, :], in0=bank(0, 2)[:, k * 128:k * 128 + 128],
                                    scalar=modT[:, l, 40 + k, s:s + 1], in1=xT[:, k, s, :], op0=ALU.mult, op1=ALU.add)
                            ins.then_inc(fb["fb_done"][l], 1)
                            dve.wait_ge(fb["fb_done"][l], e * 2 + (s + 2))
                for half in range(2):
                    v.tensor_copy(small[:, 90 + half:91 + half], xT[:, 0, 0, 0:1]).then_inc(q["d_x"], 1)

            moe(0)
            norm(2)
            ub4 = H["ub"].rearrange("p (b s t) -> p b s t", b=4, s=NS)
            uc4 = H["uc"].rearrange("p (b s t) -> p b s t", b=4, s=NS)
            L(v.memset(ub4[:, :, :, 0:1], 0.0))
            L(v.memset(ub4[:, :, :, T + 1:T + 2], 0.0))
            cw, cb = V("hy_conv_w"), V("hy_conv_b")

            def spectral(s, part):
                dve.wait_ge(q["t_spec"], s + 1)
                Ua, Ub = bank(0, 2), bank(2, 2)
                ya, yb = YS[s]
                if part == 0:
                    L(v.tensor_tensor(ya, Ua, H["KA"], ALU.mult))
                    L(v.tensor_tensor(t1, Ub, H["KB"], ALU.mult))
                    L(v.tensor_tensor(ya, ya, t1, ALU.subtract))
                else:
                    L(v.tensor_tensor(yb, Ua, H["KB"], ALU.mult))
                    L(v.tensor_tensor(t1, Ub, H["KC"], ALU.mult))
                    v.tensor_tensor(yb, yb, t1, ALU.add).then_inc(q["d_spec"], 1)
                    dve.wait_ge(q["d_spec"], s + 1)

            for j in range(24):
                ch = HY_ORDER[j]
                u, o = ub4[:, j % 4], uc4[:, j % 4]
                dst = {1: H["x1"], 2: o, 0: H["x0"]}[ch // 8]
                if ch // 8 != 2:
                    dst = dst.rearrange("p (k s t) -> p k s t", k=KD, s=NS)[:, ch % 8]
                dve.wait_ge(q["a_u"], j + 1)
                L(v.tensor_scalar(o, u[:, :, 1:T + 1], cw[:, 24 + ch:25 + ch], cb[:, ch:ch + 1], ALU.mult, ALU.add))
                L(v.scalar_tensor_tensor(out=o, in0=u[:, :, 0:T], scalar=cw[:, ch:ch + 1], in1=o, op0=ALU.mult, op1=ALU.add))
                v.scalar_tensor_tensor(out=dst, in0=u[:, :, 2:T + 2], scalar=cw[:, 48 + ch:49 + ch], in1=o,
                                       op0=ALU.mult, op1=ALU.add).then_inc(q["d_uc"], 1)
                dve.wait_ge(q["d_uc"], j + 1)
                if ch // 8 == 2:
                    k = ch % 8
                    v.tensor_tensor(H["zz"].rearrange("p (k s t) -> p k s t", k=KD, s=NS)[:, k], dst,
                                    H["x1"].rearrange("p (k s t) -> p k s t", k=KD, s=NS)[:, k],
                                    ALU.mult).then_inc(q["d_zz"], 1)
                if 19 <= j <= 22:
                    spectral((j - 19) // 2, (j - 19) % 2)
            for s in range(NS):
                dve.wait_ge(q["t_y"], s + 1)
                dve.wait_ge(q["a_zd"], 1)
                z4 = H["zz"].rearrange("p (k s t) -> p k s t", k=KD, s=NS)[:, :, s]
                x04 = H["x0"].rearrange("p (k s t) -> p k s t", k=KD, s=NS)[:, :, s]
                L(v.tensor_tensor(z4, z4, bank(4 + 2 * s, 2).rearrange("p (k t) -> p k t", k=KD), ALU.add))
                v.tensor_tensor(x04, x04, z4, ALU.mult).then_inc(q["d_r"], 1)
            residual(1, 2, [0, 1, 2, 3], OUT1_AT)
            moe(1)

        @block.tensor
        def _(pe):
            mm = nc.tensor.matmul
            tr = nc.tensor.transpose

            rows = ring[:, RING - 1, 0:384].rearrange("p (t c) -> p t c", t=3)
            pe.wait_ge(q["rows_in"], 160)
            pe.wait_ge(q["cst_in"], 16)
            for t in range(3):
                n = ROWS_IN_TILE[t]
                ins = tr(bank(7)[:, t * 128:t * 128 + n], rows[0:n, t, :], ident[0:n, 0:n])
            ins.then_inc(q["t_rows"], 1)
            xin = arena[:, 0:2048].rearrange("p (s d) -> p s d", s=NS)
            pe.wait_ge(q["x_in"], 32)
            for k in range(KD):
                for s in range(NS):
                    c = k * 256 + s * 128
                    ins = tr(bank(0, 4)[:, c:c + 128], xin[:, s, k * 128:k * 128 + 128], ident)
            ins.then_inc(q["t_xT"], 1)

            def norm(n):
                if n == 0:
                    pe.wait_ge(q["g_const"], 8)
                    pe.wait_ge(q["d_rows"], 1)
                for k in range(KD):
                    if k % 4 == 0:
                        pe.wait_ge(q["a_sq"], 2 * n + k // 4 + 1)
                    ins = mm(bank(7)[:, 0:256], ones[:], sq[:, k].rearrange("p s t -> p (s t)"),
                             start=(k == 0), stop=(k == KD - 1))
                ins.then_inc(q["t_ss"], 1)

            def used(ins, n):
                ins.then_inc(ring_free[n % RING], 1)

            def mod_row(m):
                n = MOD_AT[m]
                arrived(pe, n)
                if m == 0:
                    pe.wait_ge(q["a_cs"], 1)
                else:
                    pe.wait_ge(q["a_mod"], m)
                for k in range(KD):
                    for g in range(4):
                        ins = mm(bank(6)[32 * g:32 * g + 32, 0:128], csil[:, k, :], unit(n)[:, k, g * 128:g * 128 + 128],
                                 start=(k == 0), stop=(k == KD - 1))
                used(ins, n)

            def mod_col(m):
                pe.wait_ge(q["a_row"], m + 1)
                tr(bank(6)[:, 0:128], A["mrow"], ident).then_inc(q["t_sel"], 1)

            norm(0)
            for m in range(4):
                mod_row(m)
                mod_col(m)

            def hk(k):
                return hT[:, k].rearrange("p s t -> p (s t)")

            def projection(j, part):
                n = AB_AT[j]
                b = 2 * (j % 2)
                if part == 0:
                    arrived(pe, n)
                    if j >= 2:
                        pe.wait_ge(q["a_proj"], j - 1)
                    if j == 0:
                        pe.wait_ge(q["a_xT"], 1)
                        pe.wait_ge(q["d_xT"], 1)
                        pe.wait_ge(q["d_h"], 4)
                        pe.wait_ge(q["a_h"], 1)
                if j in (ZF, ZB, QA, GA):
                    for k in range(KD):
                        ins = mm(bank(b, 2)[:, part * 256:part * 256 + 256], unit(n)[:, k, part * 128:part * 128 + 128],
                                 hk(k), start=(k == 0), stop=(k == KD - 1))
                else:
                    w = 256 if j == KVB else 512
                    s = part // 2
                    for k in range(4 * (part % 2), 4 * (part % 2) + 4):
                        ins = mm(bank(b + s)[:, 0:w], hT[:, k, s, :], unit(n)[:, k, 0:w],
                                 start=(k == 0), stop=(k == KD - 1))
                if part == 3:
                    used(ins, n)

            def at(d):
                pe.wait_ge(q["d_kd"], d + 1)
                pe.wait_ge(q["d_aq"], d + 1)
                Aq = E[d].rearrange("p (h s t) -> p h s t", h=HA, s=NS)
                Kd = X[d].rearrange("p (h s t) -> p h s t", h=HA, s=NS)
                for c in range(2):
                    for s in range(NS):
                        for h in range(HA):
                            col = (s * HA + h) * 64
                            ins = mm(bank(4 + d)[c * 64:c * 64 + 64, col:col + 64], Kd[:, h, s, c * 64:c * 64 + 64],
                                     Aq[:, h, s, c * 64:c * 64 + 64], start=True, stop=True)
                ins.then_inc(q["t_att"], 1)

            def kc(d, s):
                pe.wait_ge(q["d_kc"], d + 1)
                Kc = K[d].rearrange("p (h s t) -> p h s t", h=HA, s=NS)
                for h in range(HA):
                    ins = tr(bank(7)[:, h * 128:h * 128 + 128], Kc[:, h, s, :], ident)
                ins.then_inc(q["t_kcT"], 1)

            vtm = A["v"].rearrange("p (s h c) -> p s h c", s=NS, h=HA)

            def chunk_states(d, s):
                n = 2 * d + s
                pe.wait_ge(q["a_kcT"], n + 1)
                pe.wait_ge(q["d_att"], 2)
                if n:
                    pe.wait_ge(q["d_state"], n)
                kT3 = A["kcT"].rearrange("p (h c) -> p h c", h=HA)
                first, second = (0, 1) if d == 0 else (1, 0)
                for c, b in [(first, 4), (second, 5)][:2 - s]:
                    rows = slice(c * 64, c * 64 + 64)
                    for h in range(HA):
                        ins = mm(bank(b)[:, h * 128:h * 128 + 128], kT3[rows, h, :], vtm[rows, s, h, :],
                                 start=True, stop=True)
                ins.then_inc(q["t_U"], 1)

            def turn_qk():
                pe.wait_ge(q["d_qk"], 1)
                pe.wait_ge(q["cache_in"], 64)
                qkt = A["qk"].rearrange("p (s c) -> p s c", s=NS)
                for s in range(NS):
                    for c in range(4):
                        src = qn[:, s, 2 * c:2 * c + 2].rearrange("p g d -> p (g d)")
                        tr(bank(4 + s)[:, c * 128:c * 128 + 128], src, ident)
                    tr(bank(7)[:, s * 128:s * 128 + 128], qkt[:, s, 512:640], ident)
                tr(bank(7)[:, 256:384], ckv[:, 0], ident).then_inc(q["t_qkT"], 1)

            def recurrence_out():
                pe.wait_ge(q["d_state"], 4)
                pe.wait_ge(q["d_q2"], 2)
                for s in range(NS):
                    for h in range(HA):
                        o = bank(4 + s)[:, h * 128:h * 128 + 128]
                        for d in range(2):
                            mm(o, vtm[:, s, h, :], att[d].rearrange("p (s h t) -> p s h t", s=NS, h=HA)[:, s, h, :],
                               start=(d == 0), stop=False)
                        for d in range(2):
                            Q2 = B[d].rearrange("p (h s t) -> p h s t", h=HA, s=NS)
                            first, second = (0, 1) if d == 0 else (1, 0)
                            for c, st in ([(second, S1[:, d, s, h, :])] + ([(first, S0[:, d, h, :])] if s == 1 else [])):
                                last = d == 1 and (s == 0 or c == first)
                                ins = mm(o[:, c * 64:c * 64 + 64], st, Q2[:, h, s, c * 64:c * 64 + 64], start=False, stop=last)
                ins.then_inc(q["t_o"], 1)

            def scores(s, banks, keys, nk):
                for h in range(HB):
                    g, c = h // 4, h % 4
                    rows = slice(64 * g, 64 * g + 64)
                    out = bank(banks, 4)[:, h * nk:h * nk + nk] if nk == 256 else bank(banks, 2)[:, h * nk:h * nk + nk]
                    ins = mm(out, qT[rows, s, c, :], keys[rows], start=True, stop=True)
                ins.then_inc(q["t_sc"], 1)

            def squares(half):
                pe.wait_ge(q["a_osq"], half + 1)
                if half:
                    pe.wait_ge(q["a_osqrt"], 1)
                mm(bank(7), ones[:], sqs[:, half * 512:half * 512 + 512], start=True, stop=True).then_inc(q["t_oss"], 1)

            def turn_probs(s, b, src, nk):
                pe.wait_ge(q["a_exp"], 2 - s)
                nkb = nk // 128
                for h in range(HB):
                    for kb in range(nkb):
                        c = (h * nkb + kb) * 128
                        ins = tr(bank(b, 4 if s else 2)[:, c:c + 128], src[:, c:c + 128], ident)
                ins.then_inc(q["t_pT"], 1)

            def attend(s, b, pT, nkb):
                pe.wait_ge(q["a_pT"], 2 - s)
                pe.wait_ge(q["d_pT"], 1)
                pe.wait_ge(q["a_osqrt"], 2)
                for h in range(HB):
                    g = h // 4
                    for kb in range(nkb):
                        c = (h * nkb + kb) * 128
                        vals = ckv[:, 1, g * 64:g * 64 + 64] if kb else A["vb"][:, s * 128 + g * 64:s * 128 + g * 64 + 64]
                        ins = mm(bank(b)[:, h * 64:h * 64 + 64], pT[:, c:c + 128], vals, start=(kb == 0), stop=(kb == nkb - 1))
                ins.then_inc(q["t_pv"], 1)

            def turn_out(s, b):
                pe.wait_ge(q["d_o"], 2 - s)
                for c in range(4):
                    ins = tr(bank(b)[:, c * 128:c * 128 + 128], otm[:, s * 512 + c * 128:s * 512 + c * 128 + 128], ident)
                ins.then_inc(q["t_oT"], 1)

            for step in SCHED:
                what, a = step[0], step[1:]
                if what == "proj":
                    projection(*a)
                elif what == "R":
                    mod_row(*a)
                elif what == "S":
                    mod_col(*a)
                elif what == "at":
                    if a[0] == 0:
                        pe.wait_ge(q["a_qkT"], 1)
                    at(*a)
                elif what == "qkT":
                    turn_qk()
                elif what == "kc":
                    kc(*a)
                elif what == "U":
                    chunk_states(*a)
                elif what == "o":
                    recurrence_out()
                elif what == "sc" and a[0] == 1:
                    pe.wait_ge(q["a_proj"], 7)
                    scores(1, 0, kT[:, 1:3].rearrange("p c t -> p (c t)"), 256)
                elif what == "sc":
                    pe.wait_ge(q["d_oA"], 1)
                    scores(0, 4, kT[:, 0], 128)
                elif what == "oss":
                    squares(*a)
                elif what == "pT" and a[0] == 1:
                    turn_probs(1, 0, probs_s, 256)
                elif what == "pT":
                    turn_probs(0, 4, probs_p, 128)
                elif what == "pv" and a[0] == 1:
                    attend(1, 7, pT_s, 2)
                elif what == "pv":
                    attend(0, 0, pT_p, 1)
                elif what == "oT":
                    turn_out(a[0], 1 if a[0] else 2)
            pe.wait_ge(q["a_cat"], 2)

            def out_projection(at_unit, banks, src, between=lambda c: None):
                for half in range(2):
                    n = at_unit + half
                    arrived(pe, n)
                    for c in range(4):
                        k8 = half * 4 + c
                        out = bank(banks[k8 // 2])[:, (k8 % 2) * 256:(k8 % 2) * 256 + 256]
                        for k in range(KD):
                            ins = mm(out, unit(n)[:, k, c * 128:c * 128 + 128], src(k), start=(k == 0), stop=(k == KD - 1))
                        if c == 3:
                            used(ins, n)
                        between(k8)

            def spectrum(i):
                pe.wait_ge(q["hy_fd"], 2)
                nm, b = ["ka", "kb", "kc"][i], [1, 3, 5][i]
                for half in range(2):
                    for j in range(2):
                        ins = mm(bank(b + half), HC(nm + str(j)), filt[:, j * 1024 + half * 512:j * 1024 + half * 512 + 512],
                                 start=(j == 0), stop=(j == 1))
                ins.then_inc(q["hy_k"], 1)

            def filter_step(k8):
                if k8 == 1:
                    pe.wait_ge(q["a_mod"], 24)
                    pe.wait_ge(q["fw_in"], 32)
                    pe.wait_ge(q["hyc_in"], 16)
                    mm(bank(6)[0:HY, 0:128], fw[0:EMB, 0], HC("zT")[0:EMB, :], start=True, stop=True).then_inc(q["hy_l1"], 1)
                if k8 == 3:
                    pe.wait_ge(q["hy_s1"], 1)
                    mm(bank(6)[0:HY, 256:384], fw[0:HY, 1], hid1[:, 1, :], start=True, stop=True).then_inc(q["hy_l2"], 1)
                if k8 == 5:
                    pe.wait_ge(q["hy_s2"], 1)
                    pe.wait_ge(q["w3_in"], 16)
                    for i, b in enumerate([1, 2, 6, 7]):
                        ins = mm(bank(b), hid1[:, 3, :], w3s[0:HY, i * 512:i * 512 + 512], start=True, stop=True)
                        if i % 2:
                            ins.then_inc(q["hy_f"], 1)
                if k8 == 7:
                    spectrum(0)

            out_projection(OUT0_AT, [0, 3, 4, 5], hk, filter_step)

            def moe(l):
                norm(2 * l + 1)
                if l == 0:
                    pe.wait_ge(q["d_x"], 2)
                    spectrum(1)
                    spectrum(2)
                pe.wait_ge(q["d_h"], 4 * (2 * l + 2))
                pe.wait_ge(q["a_h"], 2 * l + 2)
                pe.wait_ge(q["small_in"], 16 * 7)
                for k in range(KD):
                    g = 32 * (k % 4)
                    ins = mm(bank(0)[g:g + 32, 0:256], rw[:, k, :], hk(k), start=(k < 4), stop=(k >= 4))
                ins.then_inc(q["t_lrow"], 1)
                pe.wait_ge(q["a_lrow"], l + 1)
                for s in range(NS):
                    ins = mm(bank(7)[:, 256 + s * 16:272 + s * 16], lrow[:, s * 128:s * 128 + 128], C("sel"),
                             start=True, stop=True)
                ins.then_inc(q["t_log"], 1)
                if l == 0:
                    pe.wait_ge(q["a_k"], 3)
                for s in range(NS):
                    for k in range(KD):
                        c = s * 1024 + k * 128
                        ins = tr(bank(0, 4)[:, c:c + 128], hT[:, k, s, :], ident)
                ins.then_inc(q["t_htm"], 1)
                pe.wait_ge(q["d_mask"], l + 1)
                b7 = bank(7)
                tri, one, m0, m1 = tri16[:, 0], tri16[:, 1], mask16[:, 0:16], mask16[:, 16:32]
                mm(b7[:, 288:320], tri, mask16[:, 0:32], start=True, stop=False)
                mm(b7[:, 304:320], one, m0, start=False, stop=True)
                mm(b7[:, 320:336], one, m0, start=True, stop=False)
                mm(b7[:, 320:336], one, m1, start=False, stop=True).then_inc(q["t_pos"], 1)
                n = MOE_AT[l]
                n0, n2 = l * NPAIR, 2 * l * NPAIR

                def turn_gates():
                    sgt = sqs[:, 0:2048].rearrange("p (s g c) -> p s g c", s=NS, g=NPAIR)
                    for s in range(NS):
                        pe.wait_ge(q["g_sg"], 2 * l + s + 1)
                        for g in range(NPAIR):
                            c = g * 256 + s * 128
                            ins = tr(bank(0, 4)[:, c:c + 128], sgt[:, s, g, :], ident)
                    ins.then_inc(q["t_ST"], 1)

                def pack(i):
                    for k in range(KD):
                        for s in range(NS):
                            ins = mm(bank(4, 2)[:, k * 128:k * 128 + 128], htm[:, s, k * 128:k * 128 + 128],
                                     S[:, s, bass.ds(i * 128, 128)], start=(s == 0), stop=(s == 1))
                    ins.then_inc(q["m_xg"], 1)

                def pair(i, first=False, last=False):
                    pe.wait_ge(q["a_xg"], i + (n0 + 1))
                    pe.wait_ge(q["d_xg"], i + (n0 + 1))
                    for w in range(2):
                        for e in range(2):
                            arrived(pe, n + 2 * w + e, i)
                        for k in range(KD):
                            for e in range(2):
                                ins = mm(bank(4 + w)[e * 64:e * 64 + 64, :], xg[:, k, e * 64:e * 64 + 64],
                                         unit(n + 2 * w + e)[:, k, :], start=(k == 0), stop=(k == KD - 1))
                                if k == KD - 1:
                                    used(ins, n + 2 * w + e)
                    if first:
                        turn_gates()
                    for f in range(KF):
                        if f % 2 == 0:
                            pe.wait_ge(q["d_hid"], i * 2 + (n2 + f // 2 + 1))
                        c = (f % 2) * 128
                        ins = tr(bank(6 + f // 2)[:, c:c + 128], M["hid"][:, f * 128:f * 128 + 128], ident)
                    ins.then_inc(q["m_hT"], 1)
                    pe.wait_ge(q["a_hT"], i + (n0 + 1))
                    pe.wait_ge(q["d_hT"], i + (n0 + 1))
                    for e in range(2):
                        arrived(pe, n + 4 + e, i)
                    for half in range(2):
                        for f in range(KF):
                            for e in range(2):
                                ins = mm(bank(6 + half)[e * 64:e * 64 + 64, :], hidT[:, f, e * 64:e * 64 + 64],
                                         down_unit(n + 4 + e)[:, f, half * 512:half * 512 + 512],
                                         start=(f == 0), stop=(f == KF - 1))
                                if half and f == KF - 1:
                                    used(ins, n + 4 + e)
                    if not last:
                        pack(i + 1)
                    if first:
                        pe.wait_ge(q["a_ST"], l + 1)
                        for b in range(4):
                            mm(bank(b), zero16[:], zero16[:].rearrange("p (o c) -> p o c", o=1).broadcast_to([P, 4, 128]),
                               start=True, stop=False, skip_group_check=True)
                    pe.wait_ge(q["a_y"], i + (n0 + 1))
                    pe.wait_ge(q["d_y"], i + (n0 + 1))
                    for k in range(KD):
                        ins = mm(bank(0, 4)[:, k * 256:k * 256 + 256], y[:, k * 128:k * 128 + 128],
                                 ST[:, bass.ds(i, 1), :].rearrange("p o c -> p (o c)"), start=False, stop=False,
                                 skip_group_check=True)
                    ins.then_inc(q["m_sc"], 1)

                pe.wait_ge(q["d_S"], 2 * l + 2)
                pe.wait_ge(q["a_htm"], l + 1)
                pack(0)
                pair(0, first=True)
                with pe.Fori(1, NPAIR - 1) as i:
                    pair(i)
                pair(NPAIR - 1, last=True)
                pe.wait_ge(q["d_flag"], l + 1)
                more = pe.value_load(flag[0:1, l:l + 1])
                u0 = n + 6 * NPAIR
                with pe.If(more > 0):
                    pe.wait_ge(q["m_sc"], (l + 1) * NPAIR)
                    with pe.Fori(0, NE) as e:
                        pe.wait_ge(fb["fb_in"][l], e * 48 + 48)
                        for s in range(NS):
                            for w in range(2):
                                for k in range(KD):
                                    ins = mm(bank(4 + w), hT[:, k, s, :], unit(u0 + w)[:, k, :], start=(k == 0), stop=(k == KD - 1))
                            ins.then_inc(fb["fb_gate"][l], 1)
                            pe.wait_ge(fb["fb_hid"][l], e * 2 + (s + 1))
                            for f in range(KF):
                                ins = tr(bank(6)[:, f * 128:f * 128 + 128], M["fh"][:, f * 128:f * 128 + 128], ident)
                            ins.then_inc(fb["fb_tr"][l], 1)
                            pe.wait_ge(fb["fb_hidT"][l], e * 2 + (s + 1))
                            for k in range(KD):
                                for f in range(KF):
                                    ins = mm(bank(0, 2)[:, k * 128:k * 128 + 128],
                                             down_unit(u0 + 2)[:, f, k * 128:k * 128 + 128],
                                             M["fhT"][:, f * 128:f * 128 + 128], start=(f == 0), stop=(f == KF - 1))
                            ins.then_inc(fb["fb_down"][l], 1)
                            pe.wait_ge(fb["fb_done"][l], e * 2 + (s + 2))

            moe(0)
            norm(2)
            z4 = H["zz"].rearrange("p (k s t) -> p k s t", k=KD, s=NS)
            for j in range(24):
                n = HYIN_AT + j // 4
                if j % 4 == 0:
                    arrived(pe, n)
                if j == 0:
                    pe.wait_ge(q["d_h"], 4 * 3)
                    pe.wait_ge(q["a_h"], 3)
                if j == 3:
                    pe.wait_ge(q["a_sqrt"], 3)
                if j >= 4:
                    pe.wait_ge(q["a_u"], j - 3)
                for k in range(KD):
                    ins = mm(bank(4 + j % 4)[:, 0:256], unit(n)[:, k, (j % 4) * 128:(j % 4) * 128 + 128], hk(k),
                             start=(k == 0), stop=(k == KD - 1))
                if j % 4 == 3:
                    used(ins, n)
                else:
                    ins.then_inc(q["t_u"], 1)
                if j in (16, 17):
                    s = j - 16
                    pe.wait_ge(q["d_zz"], KD)
                    for k in range(KD):
                        ins = tr(bank(2 * s, 2)[:, k * 128:k * 128 + 128], z4[:, k, s, :], ident)
                    ins.then_inc(q["t_zt"], 1)
                if j in (18, 21):
                    s = (j - 18) // 3
                    pe.wait_ge(q["a_zt"], 2)
                    if s:
                        pe.wait_ge(q["d_spec"], s)
                    for part, nm in enumerate(["fa", "fb"]):
                        for half in range(2):
                            ins = mm(bank(2 * part + half), HC(nm), H["zt"][:, s * 1024 + half * 512:s * 1024 + half * 512 + 512],
                                     start=True, stop=True)
                    ins.then_inc(q["t_spec"], 1)
            for s in range(NS):
                pe.wait_ge(q["d_spec"], s + 1)
                if s == 0:
                    pe.wait_ge(q["a_u"], 22)
                else:
                    pe.wait_ge(q["a_u"], 24)
                for k in range(KD):
                    o = bank(4 + 2 * s, 2)[:, k * 128:k * 128 + 128]
                    mm(o, YS[s][0][:, k * 128:k * 128 + 128], HC("ga"), start=True, stop=False)
                    ins = mm(o, YS[s][1][:, k * 128:k * 128 + 128], HC("gb"), start=False, stop=True)
                ins.then_inc(q["t_y"], 1)
            pe.wait_ge(q["d_r"], 2)
            out_projection(OUT1_AT, [0, 1, 2, 3], lambda k: H["x0"][:, k * 256:k * 256 + 256])
            moe(1)
            pe.wait_ge(q["d_x"], 8)
            for s in range(NS):
                for k in range(KD):
                    c = s * 1024 + k * 128
                    ins = tr(bank(0, 4)[:, c:c + 128], xT[:, k, s, :], ident)
            ins.then_inc(q["t_fin"], 1)


_INS = ['x_prompt', 'x_sample', 'cache_k', 'cache_v', 'state_hgrn', 'c', 'c_ctx', 'norm_g', 'mod_w', 'mod_b',
        'ab_in_w', 'hgrn_lb', 'hgrn_onorm_g', 'attn_qnorm_g', 'attn_knorm_g', 'ab_out_w',
        'hy_in_w', 'hy_in_b', 'hy_conv_w', 'hy_conv_b', 'hy_f_w1', 'hy_f_b1', 'hy_f_w2', 'hy_f_b2',
        'hy_f_w3', 'hy_f_freq', 'hy_dskip', 'hy_out_w', 'router_w', 'router_b',
        'moe_w_gate', 'moe_w_up', 'moe_w_down']
_OUTS = [("y_prompt", (1, T, D)), ("y_sample", (1, T, D)), ("new_cache_k", (1, 1, KV, T, HD)),
         ("new_cache_v", (1, 1, KV, T, HD)), ("new_state", (1, 1, 2, HA, 128, 128))]


def kernel(**inputs):
    import concourse.bacc as _bacc
    from concourse.bass_utils import run_bass_kernel_spmd as _run

    nc = _bacc.Bacc("TRN2", target_bir_lowering=False, num_devices=1)
    arrays, ins, outs = {}, {}, {}
    for name in _INS:
        a = np.ascontiguousarray(inputs[name])
        arrays[f"in_{name}"] = a
        ins[name] = nc.dram_tensor(f"in_{name}", a.shape, F32, kind="ExternalInput").ap()
    for name, a in zip(["cst", "hyc"], shape_constants()):
        arrays[f"in_{name}"] = a
        ins[name] = nc.dram_tensor(f"in_{name}", a.shape, F32, kind="ExternalInput").ap()
    for name, shape in _OUTS:
        outs[name] = nc.dram_tensor(f"out_{name}", shape, F32, kind="ExternalOutput").ap()
    build(nc, ins, outs)
    r = _run(nc, [arrays], core_ids=[0])
    return tuple(r.results[0][f"out_{name}"] for name, _ in _OUTS)
```

```python
from contextlib import ExitStack

import numpy as np

import concourse.bass as bass
from concourse import mybir

F32 = mybir.dt.float32
BF16 = mybir.dt.bfloat16
U32 = mybir.dt.uint32
I32 = mybir.dt.int32
ALU = mybir.AluOpType
ACT = mybir.ActivationFunctionType
AX = mybir.AxisListType

P = 128
D = 1024
KD = D // P
T = 128
NS = 2
CHUNK = 64
HA = 4
HB = 8
KV = 2
HD = 64
NE = 16
NG = 4
F = 512
KF = F // P
CAP = 64
NPAIR = NE // 2
RING = 6
UNIT = KD * 512
EPS = 1e-6
HY = 64
EMB = 33
ARENA = 17920

_GAPS = {(1, 0): [("lf", 0)], (1, 2): [("ex", 0)], (2, 0): [("lf", 1)], (2, 2): [("ex", 1)],
         (5, 1): [("qkT",)], (5, 3): [("at", 0), ("at", 1)],
         (6, 0): [("kc", 0, 0)], (6, 1): [("U", 0, 0), ("kc", 0, 1)], (6, 2): [("U", 0, 1), ("kc", 1, 0)],
         (6, 3): [("U", 1, 0), ("kc", 1, 1)]}
SCHED = []
for _j in range(7):
    for _c in range(4):
        SCHED += [("proj", _j, _c)] + _GAPS.get((_j, _c), [])
        if _j >= 3 and _c < 2:
            SCHED += [("RS"[_c], _j + 1)]
SCHED += [("U", 1, 1), ("R", 8), ("sc", 1), ("o",), ("S", 8), ("oss", 0), ("R", 9), ("oss", 1), ("S", 9), ("ex1",),
          ("R", 12), ("pT", 1), ("S", 12), ("R", 13), ("sc", 0), ("op", 0), ("ex0",), ("pv", 1), ("S", 13), ("op", 1),
          ("pT", 0), ("op", 2), ("oT", 1), ("hy", 0), ("op", 3), ("pv", 0), ("R", 14), ("sin",), ("op", 4), ("oT", 0),
          ("op", 5), ("S", 14), ("hy", 1), ("op", 6), ("R", 15), ("op", 7), ("S", 15)]

CST = {}
CST_N = 0
for _name, _n in [("ident", 128), ("tri", 128), ("mask_f", 64), ("mask_r", 64), ("cos", 64), ("sin", 64),
                  ("slot", CAP), ("tie", 16), ("sel", 16)]:
    CST[_name] = (CST_N, _n)
    CST_N += _n
HYC = {}
HYC_N = 0
for _name, _n in [("zT", 128), ("fa", 128), ("fb", 128), ("ka0", 128), ("kb0", 128), ("kc0", 128), ("ka1", 128),
                  ("kb1", 128), ("kc1", 128), ("ga", 128), ("gb", 128), ("decay", D)]:
    HYC[_name] = (HYC_N, _n)
    HYC_N += _n


def shape_constants():
    f32 = np.float32
    a = np.zeros((P, CST_N), f32)

    def put(arr, table, name, val):
        o, n = table[name]
        arr[:val.shape[0], o:o + n] = val

    i = np.arange(P)
    put(a, CST, "ident", np.eye(P, dtype=f32))
    put(a, CST, "tri", (i[:, None] < i[None, :]).astype(f32))
    j = i[:, None] % CHUNK
    put(a, CST, "mask_f", (j <= np.arange(CHUNK)[None]).astype(f32))
    put(a, CST, "mask_r", (j >= np.arange(CHUNK)[None]).astype(f32))
    inv = (f32(10000.0) ** (-np.arange(16, dtype=f32) / f32(16))).astype(f32)
    row, col = (i // 64).astype(f32), (i % 64).astype(f32)
    ang = np.stack([row[:, None] * inv, col[:, None] * inv], 1).astype(f32)
    cos, sin = np.cos(ang.astype(np.float64)), np.sin(ang.astype(np.float64))
    put(a, CST, "cos", np.stack([cos, cos], 2).reshape(P, 64).astype(f32))
    put(a, CST, "sin", np.stack([-sin, sin], 2).reshape(P, 64).astype(f32))
    put(a, CST, "slot", np.tile(np.arange(CAP, dtype=f32), (P, 1)))
    put(a, CST, "sel", (i[:, None] % 32 == np.arange(NE)[None]).astype(f32))
    tie = (np.arange(4)[None] < np.arange(4)[:, None]).astype(f32).reshape(1, 16)
    put(a, CST, "tie", np.tile(tie, (P, 1)))

    b = np.zeros((P, HYC_N), f32)
    L, N = T, 2 * T
    t = np.linspace(0.0, 1.0, L, dtype=f32)
    w = (2.0 * np.pi * np.arange(L) / L)
    fb = np.linspace(1e-4, 15, 16, dtype=f32).astype(np.float64)
    z = np.concatenate([t[:, None], np.cos(w[:, None] * fb), -np.sin(w[:, None] * fb)], 1)
    put(b, HYC, "zT", z.T.astype(f32))
    n = np.arange(L)[:, None]
    f = np.arange(L)[None]
    ang = 2 * np.pi * n * f / N
    alt = (-1.0) ** n
    fa, fbm = np.cos(ang), np.sin(ang)
    fbm = np.where(f == 0, alt, fbm)
    late = n >= 1
    put(b, HYC, "fa", fa)
    put(b, HYC, "fb", fbm)
    put(b, HYC, "ka0", fa)
    put(b, HYC, "kb0", np.sin(ang))
    put(b, HYC, "kc0", np.where(f == 0, alt, fa))
    put(b, HYC, "ka1", fa * late)
    put(b, HYC, "kb1", -np.sin(ang) * late)
    put(b, HYC, "kc1", np.where(f == 0, alt, fa) * late)
    wgt = np.where(np.arange(L) == 0, 1.0, 2.0)[:, None] / N
    ang = ang.T
    put(b, HYC, "ga", np.cos(ang) * wgt)
    put(b, HYC, "gb", np.where(np.arange(L)[:, None] == 0, alt.T / N, np.sin(ang) * wgt))
    lo, hi = np.log(1e-2) / 1.5, np.log(1e-2) / 0.3
    deltas = np.abs(np.linspace(lo, hi, D, dtype=f32)).astype(np.float64)
    put(b, HYC, "decay", np.exp(-t.astype(np.float64)[:, None] * deltas).astype(f32))
    return a, b


ROWS = {"norm_g": (0, 0, 32), "hgrn_lb": (0, 32, 16), "onorm": (0, 48, 4), "c": (0, 52, 8), "c_ctx": (0, 60, 8),
        "dskip": (0, 68, 8), "hy_in_b": (0, 76, 24), "hy_conv_b": (0, 100, 24), "mod_b": (1, 0, 96),
        "hy_conv_w": (2, 0, 72)}
ROWS_IN_TILE = [124, 96, 72]

AB_UNITS = [("ab", 512), ("ab", 1024), ("ab", 2560), ("ab", 3072), ("ab", 0), ("ab", 1536), ("ab", 2048)]
ZF, ZB, QB, KVB, QA, IA, GA = range(7)
MODS = [("mod", n // 12, n % 12) for n in range(24)]
UNITS = list(MODS[0:4])
AB_AT = []
for _j, _u in enumerate(AB_UNITS):
    AB_AT.append(len(UNITS))
    UNITS.append(_u)
    UNITS += MODS[_j + 1:_j + 2] if _j >= 3 else []
UNITS += MODS[8:10] + MODS[12:14]
OUT0_AT = len(UNITS)
UNITS += [("about", 0), ("about", 1)] + MODS[14:16]
UNITS += MODS[10:12]
MOE_AT = [len(UNITS)]
UNITS += [("moe", 0)] * 48
UNITS += MODS[16:19]
HYIN_AT = len(UNITS)
UNITS += [("hyin", c) for c in (2, 3, 4, 5)] + MODS[19:20] + [("hyin", c) for c in (0, 1)] + MODS[20:21]
OUT1_AT = len(UNITS)
UNITS += [("hyout", 0), ("hyout", 1)]
UNITS += MODS[21:24]
MOE_AT.append(len(UNITS))
UNITS += [("moe", 1)] * 48
MOD_AT = {u[1] * 12 + u[2]: n for n, u in enumerate(UNITS) if u[0] == "mod"}
MOD_TURN = {m: i for i, m in enumerate(sorted(MOD_AT, key=MOD_AT.get))}


def build(nc, I, O):
    ctx = ExitStack()
    with ctx:
        def sb(name, shape, dt=F32):
            return ctx.enter_context(nc.sbuf_tensor(name, shape, dt))

        def sem(name):
            return ctx.enter_context(nc.semaphore(name))

        ps = ctx.enter_context(nc.psum_tensor("ps", [P, 8, 512], F32))

        def bank(b, n=1):
            return ps[:, b:b + n, :].rearrange("p b c -> p (b c)")

        ring = sb("ring", [P, RING, UNIT])
        xT = sb("xT", [P, KD, NS, T])
        hT = sb("hT", [P, KD, NS, T])
        sqs = sb("sqs", [P, 2304])
        sq = sqs[:, 0:2048].rearrange("p (k s t) -> p k s t", k=KD, s=NS)
        rstd = sb("rstd", [P, NS, T])
        cst = sb("cst", [P, CST_N])
        ones = sb("ones", [P, P])
        VT = sb("VT", [P, 3, 128])
        modT = sb("modT", [P, 2, 48, NS])
        scl = sb("scl", [P, 4, KD, NS])
        csil = sb("csil", [P, KD, 32])
        eps = sb("eps", [P, 1])
        rw = sb("rw", [P, KD, 32])
        tri16 = sb("tri16", [P, 2, P], BF16)
        rb = sb("rb", [P, NE])
        fcol = sb("fcol", [P, 8])
        zero16 = sb("zero16", [P, 128], BF16)
        arena = sb("arena", [P, ARENA])

        def carve(sizes):
            out, at = {}, 0
            for name, n in sizes:
                out[name] = arena[:, at:at + n]
                at += n
            assert at <= ARENA, at
            return out

        def C(name):
            o, n = CST[name]
            return cst[:, o:o + n]

        ident = C("ident")

        def V(name):
            t, r, n = ROWS[name]
            return VT[:, t, r:r + n]

        A = carve([("E0", 1024), ("E1", 1024), ("K0", 1024), ("K1", 1024), ("B0", 1024), ("B1", 1024),
                   ("X0", 1024), ("X1", 1024), ("tmp", 1024),
                   ("kcT", 512), ("mrow", 128), ("att0", 1024), ("att1", 1024), ("q", 1024), ("v", 1024), ("S1", 2048),
                   ("qk", 1280), ("vb", 256), ("gqk", 2 * HD)])
        E, K, B, X = ([A[n + d] for d in "01"] for n in "EKBX")
        att = [A["att0"], A["att1"]]
        probs_s = arena[:, 0:2048]
        probs_p = arena[:, 3072:4096]
        pT_s = arena[:, 4096:6144]
        pT_p = arena[:, 6144:7168]
        otm = arena[:, 7168:8192]
        sqk = sqs[:, 0:1280]
        S0 = sqs[:, 1280:2304].rearrange("p (d h c) -> p d h c", d=2, h=HA)
        qn = sqs[:, 0:1024].rearrange("p (s n c) -> p s n c", s=NS, c=HD)
        osd = sqs[:, 1280:2304]
        seg = sb("seg", [P, 1024])
        qT = seg[:].rearrange("p (s c t) -> p s c t", s=NS, c=4)
        Sfin = A["tmp"].rearrange("p (d h c) -> p d h c", d=2, h=HA)
        S1 = A["S1"].rearrange("p (d s h c) -> p d s h c", d=2, s=NS, h=HA)
        decs = sb("decs", [P, 2, 16])
        kT = sb("kT", [P, 3, 128])
        ckv = sb("ckv", [P, 2, 128])
        gqk = A["gqk"].rearrange("p (n c) -> p n c", n=2)
        sga = A["K0"].rearrange("p (h s t) -> p h s t", h=HA, s=NS)
        lbt = sb("lbt", [P, 6, 8])
        small = sb("small", [P, 96])
        catT = hT

        M_SIZES = [("htm", 2048), ("S", 2048), ("ST", 2048), ("xg", 1024), ("sg", 512), ("hid", 512), ("hidT", 512),
                   ("y", 1024), ("r", 1024), ("fhT", 512), ("fh", 512)]
        M = carve(M_SIZES)
        lrow = M["fhT"][:, 0:256]
        mask16 = M["fhT"][:, 256:272].bitcast(BF16)
        htm = M["htm"].rearrange("p (s d) -> p s d", s=NS)
        S = M["S"].rearrange("p (s c) -> p s c", s=NS)
        ST = M["ST"].rearrange("p (g c) -> p g c", g=NPAIR)
        xg = M["xg"].rearrange("p (k c) -> p k c", k=KD)
        hidT = M["hidT"].rearrange("p (f c) -> p f c", f=KF)
        y = M["y"]
        R = {}
        _at = 0
        for name, n in [("lg", 32), ("e", 32), ("score", 32), ("bi", 32), ("gt", 128), ("eq", 128), ("rank", 32),
                        ("selE", 32), ("bs", 32), ("gs", 8), ("grank", 8), ("selG", 8), ("mask", 32), ("w", 32),
                        ("gate", 32), ("pos", 32), ("over", 32), ("c1", 2), ("c2", 2), ("c3", 2), ("cnt", 16),
                        ("mxc", 1), ("gcol", 2)]:
            R[name] = M["r"][:, _at:_at + n]
            _at += n
        flag = sb("flag", [P, 2], I32)

        H = carve([("zz", 2048), ("x1", 2048), ("x0", 2048), ("zt", 2048), ("ub", 4 * 264), ("uc", 4 * 256), ("ya", 1024),
                   ("gap", 480), ("KA", 1024), ("KB", 1024), ("KC", 1024), ("hyc", HYC_N - D), ("yb", 1024)])
        t1 = sqs[:, 0:1024]
        w3s = arena[:, 2048:4096]
        filt = arena[:, 4096:6144]
        decay = arena[:, 16256:17280]
        fw = arena[:, 11776:11904].rearrange("p (n c) -> p n c", n=2)
        hid1 = arena[0:HY, 17408:17920].rearrange("p (n c) -> p n c", n=4)
        assert sum(n for _, n in M_SIZES) <= 11776

        U0 = [H["zt"][:, 0:1024], sqs[:, 1024:2048]]
        YS = [(H["ya"], H["yb"]), (H["x1"][:, 0:1024], H["x1"][:, 1024:2048])]
        HY_ORDER = list(range(8, 16)) + list(range(16, 24)) + list(range(0, 8))

        fscr = arena[:, 9856:9984]
        PI = float(np.pi)

        def HC(name):
            o, n = HYC[name]
            return H["hyc"][:, o:o + n]

        fin = arena[:, 0:2048].rearrange("p (h s c) -> p h s c", h=2, s=NS)

        ring_full = [sem(f"ring_full{i}") for i in range(RING)]
        ring_free = [sem(f"ring_free{i}") for i in range(RING)]
        names = """fw_in rows_in more_rows_in cst_in x_in small_in state_in cache_in hyc_in w3_in decay_in out_done cache_out
            g_const g_rw g_fb t_rows d_rows t_xT a_xT d_xT a_cs a_sq t_ss a_sqrt d_h t_sel a_row a_mod
            a_proj d_ef d_kk a_lf d_x1 a_ea a_eb d_kd d_x2 a_e2 d_aq d_q2 d_kc a_e3 a_e4
            d_xn a_h t_lrow a_lrow d_S g_sg t_att d_att t_kcT a_kcT t_U d_state t_o a_osq t_oss a_osqrt d_oA
            a_qksq d_var a_qksd d_qk t_qkT a_qkT t_sc d_max a_exp t_pT a_pT d_pT t_pv d_o t_oT a_cat d_x
            t_log a_htm d_lg a_re d_mask t_pos t_ST a_ST t_htm
            m_add m_half m_xg a_xg d_xg a_sg d_hid m_hT a_hT d_hT a_y d_y m_sc
            d_flag hy_l hy_a hy_r hy_s hy_f hy_fd hy_k a_k t_u a_u d_uc d_zz t_zt a_zt a_zd t_spec a_spec
            d_spec t_y d_r t_fin a_fin d_fin d_chain a_chain g_chain""".split()
        q = {n: sem(n) for n in names}
        fb = {n: [sem(f"{n}{l}") for l in range(2)] for n in
              ["fb_in", "fb_gate", "fb_silu", "fb_hid", "fb_tr", "fb_hidT", "fb_down", "fb_done", "fb_col"]}

        chain = {"d_chain": 0, "a_chain": 0, "g_chain": 0}

        def link(eng, name, ins):
            chain[name] += 1
            ins.then_inc(q[name], 1)
            eng.wait_ge(q[name], chain[name])

        def mrow(m):
            return A["mrow"] if m < 10 or 12 <= m < 16 else arena[:, 11648:11776]

        def mod_bank(m):
            return bank(3 if m in (19, 20) else 6)

        def unit(n):
            return ring[:, n % RING, :].rearrange("p (k c) -> p k c", k=KD)

        def down_unit(n):
            return ring[:, n % RING, :].rearrange("p (k c) -> p k c", k=KF)

        def arrived(eng, n, more=0):
            eng.wait_ge(ring_full[n % RING], (more + (n // RING + 1)) * 16)

        def products_of(eng, n, more=0):
            eng.wait_ge(ring_free[n % RING], more + (n // RING + 1))

        rows = ring[:, RING - 1, 0:384].rearrange("p (t c) -> p t c", t=3)
        row_src = {
            "norm_g": I["norm_g"].rearrange("l i (k p) -> (l i k) p", p=P),
            "hgrn_lb": I["hgrn_lb"].rearrange("n d (k p) -> (n d k) p", p=P),
            "onorm": I["hgrn_onorm_g"].rearrange("n (k p) -> (n k) p", p=P),
            "c": I["c"].rearrange("n (k p) -> (n k) p", p=P),
            "c_ctx": I["c_ctx"].rearrange("(k p) -> k p", p=P),
            "dskip": I["hy_dskip"].rearrange("n (k p) -> (n k) p", p=P),
            "hy_in_b": I["hy_in_b"].rearrange("n (k p) -> (n k) p", p=P),
            "hy_conv_b": I["hy_conv_b"].rearrange("n (k p) -> (n k) p", p=P),
            "mod_b": I["mod_b"].rearrange("l (k p) -> (l k) p", p=P),
            "hy_conv_w": I["hy_conv_w"].rearrange("n w (k p) -> (n w k) p", p=P),
        }

        def rows_of(eng, names, landed="rows_in"):
            for name in names:
                t, r, n = ROWS[name]
                eng.dma_start(rows[r:r + n, t, :], row_src[name]).then_inc(q[landed], 16)

        block = ctx.enter_context(nc.Block())

        @block.sync
        def _(sp):
            w_dram = {
                "mod": lambda u: I["mod_w"][u[1]].rearrange("(k p) c -> p k c", p=P)[:, :, u[2] * 512:u[2] * 512 + 512],
                "ab": lambda u: I["ab_in_w"][0].rearrange("(k p) c -> p k c", p=P)[:, :, u[1]:min(u[1] + 512, 3328)],
                "about": lambda u: I["ab_out_w"][0].rearrange("(k p) c -> p k c", p=P)[:, :, u[1] * 512:u[1] * 512 + 512],
                "hyin": lambda u: I["hy_in_w"][0].rearrange("(k p) c -> p k c", p=P)[:, :, u[1] * 512:u[1] * 512 + 512],
                "hyout": lambda u: I["hy_out_w"][0].rearrange("(k p) c -> p k c", p=P)[:, :, u[1] * 512:u[1] * 512 + 512],
            }
            xin = arena[:, 0:2048].rearrange("p (s d) -> p s d", s=NS)
            sp.dma_start(cst[:], I["cst"]).then_inc(q["cst_in"], 16)
            sp.dma_start(xin[:, 0], I["x_prompt"][0]).then_inc(q["x_in"], 16)
            sp.dma_start(xin[:, 1], I["x_sample"][0]).then_inc(q["x_in"], 16)
            rows_of(sp, ["onorm", "dskip"])
            n = 0
            while n < len(UNITS):
                u = UNITS[n]
                if u[0] != "moe":
                    if n == OUT0_AT + 3:
                        sp.wait_ge(q["t_o"], 1)
                        sp.wait_ge(q["cache_out"], 16 * 6)
                        sp.dma_start(fw[0:EMB, 0], I["hy_f_w1"][0]).then_inc(q["fw_in"], 16)
                        sp.dma_start(fw[0:HY, 1], I["hy_f_w2"][0]).then_inc(q["fw_in"], 16)
                        sp.dma_start(H["hyc"], I["hyc"][:, 0:HYC_N - D]).then_inc(q["hyc_in"], 16)
                        sp.dma_start(decay, I["hyc"][:, HYC_N - D:]).then_inc(q["decay_in"], 16)
                    src = w_dram[u[0]](u)
                    if n == 1:
                        sp.wait_ge(q["rows_in"], 16 * 6)
                        sp.wait_ge(q["more_rows_in"], 16 * 4)
                    if n == RING - 1:
                        sp.wait_ge(q["t_rows"], 1)
                    if n >= RING:
                        sp.wait_ge(ring_free[n % RING], n // RING)
                    sp.dma_start(unit(n)[:, :, 0:src.shape[2]], src).then_inc(ring_full[n % RING], 16)
                    n += 1
                    continue
                l = u[1]
                with sp.Fori(0, NPAIR) as i:
                    for j, (e, w) in enumerate([(0, "gate"), (1, "gate"), (0, "up"), (1, "up"), (0, "down"), (1, "down")]):
                        m = n + j
                        sp.wait_ge(ring_free[m % RING], i + m // RING)
                        src = I["moe_w_" + w][l, bass.ds(i * 2 + e, 1)].rearrange("o (k p) c -> p (o k) c", p=P)
                        dst = down_unit(m) if w == "down" else unit(m)
                        sp.dma_start(dst, src).then_inc(ring_full[m % RING], 16)
                n += 6 * NPAIR
                sp.wait_ge(q["d_flag"], l + 1)
                more = sp.value_load(flag[0:1, l:l + 1])
                with sp.If(more > 0):
                    for m in range(n - 6, n):
                        sp.wait_ge(ring_free[m % RING], m // RING + 1)
                    with sp.Fori(0, NE) as e:
                        sp.wait_ge(fb["fb_done"][l], e * 2 + 1)
                        for j, w in enumerate(["gate", "up", "down"]):
                            src = I["moe_w_" + w][l, bass.ds(e, 1)].rearrange("o (k p) c -> p (o k) c", p=P)
                            dst = down_unit(n + j) if w == "down" else unit(n + j)
                            sp.dma_start(dst, src).then_inc(fb["fb_in"][l], 16)
                    sp.wait_ge(fb["fb_done"][l], 2 * NE + 1)
            sp.wait_ge(q["cache_out"], 16 * 6)
            for h in range(2):
                for s, o in enumerate(["y_prompt", "y_sample"]):
                    if h and s:
                        sp.wait_ge(q["d_fin"], 1)
                    else:
                        sp.wait_ge(q["a_fin"], h + 1)
                    sp.dma_start(O[o][0, :, h * 512:h * 512 + 512], fin[:, h, s]).then_inc(q["out_done"], 16)
            sp.wait_ge(q["out_done"], 16 * 4)

        @block.gpsimd
        def _(pool):
            rows_of(pool, ["mod_b", "hy_in_b", "hy_conv_b", "hy_conv_w"], "more_rows_in")
            nc.gpsimd.memset(ones[:], 1.0).then_inc(q["g_const"], 1)
            nc.gpsimd.memset(eps[:], EPS).then_inc(q["g_const"], 1)
            nc.gpsimd.memset(zero16[:], 0.0).then_inc(q["g_const"], 1)
            link(pool, "g_chain", nc.gpsimd.memset(seg[:], 1.0))
            nc.gpsimd.memset(seg[:].rearrange("p (c t) -> p c t", t=CHUNK)[:, :, 0:1], 0.0).then_inc(q["g_const"], 1)
            nc.gpsimd.memset(csil[:], 0.0).then_inc(q["g_const"], 1)
            nc.gpsimd.memset(rw[:], 0.0).then_inc(q["g_rw"], 1)
            nc.gpsimd.memset(tri16[:, 1], 1.0).then_inc(q["g_const"], 1)
            nc.gpsimd.memset(att[0], 0.0).then_inc(q["g_const"], 1)
            nc.gpsimd.memset(att[1], 0.0).then_inc(q["g_const"], 1)

            def dma(dst, src, landed):
                pool.dma_start(dst, src).then_inc(q[landed], 16)

            pool.wait_ge(q["g_rw"], 1)
            dma(rw[:, :, 0:NE], I["router_w"].rearrange("(k p) e -> p k e", p=P), "small_in")
            dma(rb[:], I["router_b"].rearrange("(a e) -> a e", a=1).broadcast_to([P, NE]), "small_in")
            dma(gqk[:, 0], I["attn_qnorm_g"].broadcast_to([P, HD]), "small_in")
            dma(gqk[:, 1], I["attn_knorm_g"].broadcast_to([P, HD]), "small_in")
            for c, n in enumerate(["hy_f_b1", "hy_f_b2", "hy_f_freq"]):
                dma(fcol[0:HY, c:c + 1], I[n].rearrange("n (c a) -> (n c) a", a=1), "small_in")
            for g in range(KV):
                dma(ckv[:, 0, 64 * g:64 * g + 64], I["cache_k"][0, 0, g], "cache_in")
                dma(ckv[:, 1, 64 * g:64 * g + 64], I["cache_v"][0, 0, g], "cache_in")
            pool.wait_ge(q["d_qk"], 1)
            qkt = A["qk"].rearrange("p (s c) -> p s c", s=NS)
            for g in range(KV):
                pool.dma_start(O["new_cache_k"][0, 0, g], qkt[:, 0, 512 + 64 * g:576 + 64 * g]).then_inc(q["cache_out"], 16)
                pool.dma_start(O["new_cache_v"][0, 0, g], A["vb"][:, 64 * g:64 * g + 64]).then_inc(q["cache_out"], 16)
            pool.wait_ge(q["d_state"], 4)
            for d in range(2):
                pool.dma_start(O["new_state"][0, 0, d].rearrange("h k v -> k h v"), Sfin[:, d]).then_inc(q["cache_out"], 16)
            g = nc.gpsimd
            pool.wait_ge(q["small_in"], 16 * 7)
            link(pool, "g_chain", g.tensor_tensor(fcol[0:HY, 3:5], fcol[0:HY, 0:2], fcol[0:HY, 2:3].broadcast_to([HY, 2]), ALU.mult))
            g.tensor_copy(fcol[0:HY, 5:6], fcol[0:HY, 2:3]).then_inc(q["g_fb"], 1)
            C1 = 6.28125
            C2 = 2 * PI - 6.28125
            MAGIC = 12582912.0
            for i in range(2):
                pool.wait_ge(q["hy_a"], i + 1)
                a, b, c = hid1[:, 2 * i, :], hid1[:, 2 * i + 1, :], fscr[0:HY, :]
                link(pool, "g_chain", g.tensor_scalar(b, a, 1.0 / (2 * PI), MAGIC, ALU.mult, ALU.add))
                link(pool, "g_chain", g.tensor_scalar(b, b, -MAGIC, None, ALU.add))
                for part in (C1, C2):
                    link(pool, "g_chain", g.tensor_scalar(c, b, -part, None, ALU.mult))
                    link(pool, "g_chain", g.tensor_tensor(a, a, c, ALU.add))
                g.tensor_scalar(a, a, PI, -PI, ALU.min, ALU.max).then_inc(q["hy_r"], 1)
            sgt = sqs[:, 0:2048].rearrange("p (s e c) -> p s e c", s=NS, e=NE)
            for l in range(2):
                for s in range(NS):
                    pool.wait_ge(q["d_S"], 3 * l + s + 2)
                    g.tensor_tensor(sgt[:, s], S[:, s].rearrange("p (e c) -> p e c", e=NE),
                                    R["gate"][:, s * NE:s * NE + NE].rearrange("p (e o) -> p e o", o=1).broadcast_to([P, NE, CAP]),
                                    ALU.mult).then_inc(q["g_sg"], 1)

        @block.scalar
        def _(act):
            rows_of(act, ["c", "c_ctx", "norm_g", "hgrn_lb"])

            def act_fn(out, in_, f, **k):
                return nc.scalar.activation(out, in_, f, **k)

            xf = xT[:].rearrange("p k s t -> p (k s t)")
            sqf = sqs[:, 0:2048]
            act.wait_ge(q["t_xT"], 1)
            nc.scalar.copy(xf[:, 1024:2048], bank(2, 2)).then_inc(q["a_xT"], 1)
            act.wait_ge(q["d_rows"], 1)
            act.wait_ge(q["g_const"], 8)
            for s, c in enumerate(["c_ctx", "c"]):
                ins = act_fn(csil[:, :, s], V(c), ACT.Silu)
            ins.then_inc(q["a_cs"], 1)

            def norm(n, *mods):
                for half in range(2):
                    sl = slice(half * 1024, half * 1024 + 1024)
                    if n:
                        act.wait_ge(q["d_x"], 2 * n - 1 + half)
                    elif half:
                        act.wait_ge(q["a_xT"], 1)
                    else:
                        act.wait_ge(q["d_xT"], 1)
                    act_fn(sqf[:, sl], xf[:, sl], ACT.Square).then_inc(q["a_sq"], 1)
                if mods:
                    mod_row(mods[0])
                act.wait_ge(q["t_ss"], n + 1)
                act.wait_ge(q["g_const"], 8)
                act_fn(rstd[:].rearrange("p s t -> p (s t)"), bank(7)[:, 0:256], ACT.Sqrt, bias=eps[:],
                       scale=1.0 / D).then_inc(q["a_sqrt"], 1)
                if mods:
                    mod_col(mods[0])
                for m in mods[1:]:
                    mod_row(m)
                    mod_col(m)

            def scaled(n):
                l, i = n // 2, n % 2
                act.wait_ge(q["d_xn"], n + 1)
                for k in range(4, KD):
                    for s in range(NS):
                        ins = act_fn(hT[:, k, s, :], sq[:, k, s, :], ACT.Identity, bias=modT[:, l, 24 * i + k, s:s + 1],
                                     scale=scl[:, n, k, s:s + 1])
                    ins.then_inc(q["a_h"], 1)

            def mod_row(m):
                products_of(act, MOD_AT[m])
                nc.scalar.copy(mrow(m), mod_bank(m)[:, 0:128]).then_inc(q["a_row"], 1)

            def mod_col(m):
                act.wait_ge(q["t_sel"], MOD_TURN[m] + 1)
                j = m % 12 * 4
                nc.scalar.copy(modT[:, m // 12, j:j + 4], mod_bank(m)[:, 0:128].rearrange("p (g c) -> p g c", g=4)[:, :, 0:NS]
                               ).then_inc(q["a_mod"], 1)

            norm(0, 0)
            act.wait_ge(q["d_ef"], 1)
            act_fn(lbt[:, 3:5], lbt[:, 1:3], ACT.Exp).then_inc(q["a_e4"], 1)
            for m in range(1, 4):
                mod_row(m)
                mod_col(m)
            scaled(0)
            act.wait_ge(q["a_h"], 4)
            act.wait_ge(q["d_h"], 4)
            for d in range(2):
                act.dma_start(S0[:, d], I["state_hgrn"][0, 0, d].rearrange("h k v -> k h v")).then_inc(q["state_in"], 16)
            qkt = A["qk"].rearrange("p (s c) -> p s c", s=NS)

            def proj_out(j):
                products_of(act, AB_AT[j])
                src = bank(2 * (j % 2), 2)
                sv = src.rearrange("p (s c) -> p s c", s=NS)
                if j in (ZF, ZB):
                    ins = act_fn(E[j], src, ACT.Sigmoid)
                elif j in (QA, IA):
                    ins = nc.scalar.copy(A["q" if j == QA else "v"], src)
                elif j == QB:
                    ins = nc.scalar.copy(qkt[:, :, 0:512], sv)
                elif j == KVB:
                    link(act, "a_chain", nc.scalar.copy(qkt[:, :, 512:640], sv[:, :, 0:128]))
                    ins = nc.scalar.copy(A["vb"].rearrange("p (s c) -> p s c", s=NS), sv[:, :, 128:256])
                else:
                    act.wait_ge(q["t_kcT"], 2)
                    ins = act_fn(A["K0"], src, ACT.Silu)
                ins.then_inc(q["a_proj"], 1)
                if j == KVB:
                    act.wait_ge(q["a_proj"], KVB + 1)
                    act_fn(sqk, A["qk"], ACT.Square).then_inc(q["a_qksq"], 1)
                    act.wait_ge(q["d_var"], 1)
                    act_fn(small[:, 20:40], small[:, 0:20], ACT.Sqrt, bias=eps[:], scale=1.0 / HD).then_inc(q["a_qksd"], 1)

            def exponentials(s):
                act.wait_ge(q["d_max"], 2 - s)
                n, probs, b = (256, probs_s, bank(0, 4)) if s else (128, probs_p, bank(4, 2))
                c = 0 if s else 8
                for h in range(HB):
                    ins = act_fn(probs[:, h * n:h * n + n], b[:, h * n:h * n + n], ACT.Exp, bias=small[:, 48 + c + h:49 + c + h],
                                 scale=HD ** -0.5, accum_out=small[:, 64 + c + h:65 + c + h])
                ins.then_inc(q["a_exp"], 1)

            def network_angle(i):
                act.wait_ge(q["g_fb"], 1)
                act.wait_ge(q["hy_l"], i + 1)
                act_fn(hid1[:, 2 * i, :], bank(6)[0:HY, 0:128], ACT.Identity, bias=fcol[0:HY, 3 + i:4 + i],
                       scale=fcol[0:HY, 5:6]).then_inc(q["hy_a"], 1)

            def network_sine(i):
                act.wait_ge(q["hy_r"], i + 1)
                act_fn(hid1[:, 1 + 2 * i, :], hid1[:, 2 * i, :], ACT.Sin).then_inc(q["hy_s"], 1)

            for step in SCHED:
                what, a = step[0], step[1:]
                if what == "R":
                    mod_row(*a)
                elif what == "S":
                    mod_col(*a)
                elif what == "hy":
                    network_angle(*a)
                elif what == "sin":
                    network_sine(0)
                elif what == "proj" and a[1] == 3:
                    proj_out(a[0])
                elif what == "lf":
                    act.wait_ge(q["d_kk"], a[0] + 1)
                    act_fn(E[a[0]], E[a[0]], ACT.Ln).then_inc(q["a_lf"], 1)
                elif what == "ex":
                    d = a[0]
                    act.wait_ge(q["d_x1"], d + 1)
                    act_fn(E[d], X[d], ACT.Exp).then_inc(q["a_ea"], 1)
                    act.wait_ge(q["a_ea"], d + 1)
                    act_fn(X[d], X[d], ACT.Exp, scale=-1.0).then_inc(q["a_eb"], 1)
                    act.wait_ge(q["d_x2"], d + 1)
                    act_fn(A["tmp"], A["tmp"], ACT.Exp).then_inc(q["a_e2"], 1)
                    act_fn(B[d], B[d], ACT.Exp).then_inc(q["a_e3"], 1)
                elif what == "qkT":
                    act.wait_ge(q["t_qkT"], 1)
                    nc.scalar.copy(qT[:, 0].rearrange("p c t -> p (c t)"), bank(4))
                    nc.scalar.copy(qT[:, 1].rearrange("p c t -> p (c t)"), bank(5))
                    nc.scalar.copy(kT[:].rearrange("p c t -> p (c t)"), bank(7)[:, 0:384]).then_inc(q["a_qkT"], 1)
                elif what == "kc":
                    act.wait_ge(q["t_kcT"], a[0] * 2 + a[1] + 1)
                    nc.scalar.copy(A["kcT"], bank(7)).then_inc(q["a_kcT"], 1)
                elif what == "o":
                    act.wait_ge(q["t_o"], 1)
                    for half in range(2):
                        act_fn(sqs[:, half * 512:half * 512 + 512], bank(4 + half), ACT.Square).then_inc(q["a_osq"], 1)
                elif what in ("ex1", "ex0"):
                    exponentials(int(what[2]))
                elif what == "oss":
                    act.wait_ge(q["t_oss"], a[0] + 1)
                    act_fn(osd[:, a[0] * 512:a[0] * 512 + 512], bank(7), ACT.Sqrt, bias=eps[:],
                           scale=1.0 / 128).then_inc(q["a_osqrt"], 1)
                elif what == "pT":
                    act.wait_ge(q["t_pT"], 2 - a[0])
                    if a[0]:
                        nc.scalar.copy(pT_s[:, 0:1024], bank(0, 2)).then_inc(q["a_pT"], 1)
                    else:
                        nc.scalar.copy(pT_p, bank(4, 2)).then_inc(q["a_pT"], 1)
                elif what == "oT":
                    s = a[0]
                    act.wait_ge(q["t_oT"], 2 - s)
                    nc.scalar.copy(catT[:, 4:8, s, :], bank(7).rearrange("p (c t) -> p c t", c=4)).then_inc(q["a_cat"], 1)

            def moe(l):
                norm(2 * l + 1, [10, 21][l])
                scaled(2 * l + 1)
                if l:
                    mod_row(22)
                act.wait_ge(q["t_lrow"], l + 1)
                nc.scalar.copy(lrow, bank(0)[:, 0:256]).then_inc(q["a_lrow"], 1)
                if l:
                    mod_col(22)
                act.wait_ge(q["d_lg"], l + 1)
                act_fn(R["e"], R["lg"], ACT.Exp).then_inc(q["a_re"], 1)
                if l == 0:
                    spectrum(1)
                    spectrum(2)
                mod_row([11, 23][l])
                act.wait_ge(q["t_htm"], l + 1)
                nc.scalar.copy(M["htm"], bank(0, 4)).then_inc(q["a_htm"], 1)
                mod_col([11, 23][l])
                n0 = l * NPAIR

                def pair(i, first=False, last=False):
                    act.wait_ge(q["m_xg"], i + (n0 + 1))
                    nc.scalar.copy(xg[:, 0:4, :].rearrange("p k c -> p (k c)"), bank(4)).then_inc(q["a_xg"], 1)
                    products_of(act, MOE_AT[l] + 1, i)
                    act_fn(M["sg"], bank(4), ACT.Silu).then_inc(q["a_sg"], 1)
                    if first:
                        act.wait_ge(q["t_ST"], l + 1)
                        nc.scalar.copy(M["ST"], bank(0, 4)).then_inc(q["a_ST"], 1)
                    act.wait_ge(q["m_hT"], i + (n0 + 1))
                    nc.scalar.copy(M["hidT"][:, 0:256], bank(6)[:, 0:256]).then_inc(q["a_hT"], 1)
                    if last:
                        act.wait_ge(q["m_half"], l + 1)
                    else:
                        products_of(act, MOE_AT[l] + 5, i)
                    nc.scalar.copy(y[:, 0:512], bank(6)).then_inc(q["a_y"], 1)

                pair(0, True)
                with act.Fori(1, NPAIR - 1) as i:
                    pair(i)
                pair(NPAIR - 1, last=True)
                act.wait_ge(q["d_flag"], l + 1)
                more = act.value_load(flag[0:1, l:l + 1])
                with act.If(more > 0):
                    with act.Fori(0, NE) as e:
                        for s in range(NS):
                            act.wait_ge(fb["fb_gate"][l], e * 2 + (s + 1))
                            act_fn(M["fh"], bank(4), ACT.Silu).then_inc(fb["fb_silu"][l], 1)
                    act.wait_ge(fb["fb_done"][l], 2 * NE + 1)

            def spectrum(i):
                act.wait_ge(q["hy_k"], i + 1)
                nc.scalar.copy(H[["KA", "KB", "KC"][i]], bank([4, 1, 3][i], 2)).then_inc(q["a_k"], 1)

            act.wait_ge(q["cache_out"], 16 * 6)
            act.dma_start(w3s[0:HY, :], I["hy_f_w3"][0]).then_inc(q["w3_in"], 16)
            network_sine(1)
            spectrum(0)
            moe(0)
            norm(2, 16, 17)
            scaled(2)
            mod_row(18)
            mod_col(18)
            for j in range(24):
                if j % 4 == 3:
                    products_of(act, HYIN_AT + j // 4 + (j >= 16))
                else:
                    act.wait_ge(q["t_u"], j // 4 * 3 + j % 4 + 1)
                ch = HY_ORDER[j]
                b = j % 4
                if j >= 4:
                    act.wait_ge(q["d_uc"], j - 3)
                ub = H["ub"].rearrange("p (b s t) -> p b s t", b=4, s=NS)[:, b, :, 1:T + 1]
                act_fn(ub, bank(4 + b)[:, 0:256].rearrange("p (s t) -> p s t", s=NS), ACT.Identity,
                       bias=V("hy_in_b")[:, ch:ch + 1]).then_inc(q["a_u"], 1)
                if j == 16:
                    mod_row(19)
                if j in (16, 17):
                    s = j - 16
                    act.wait_ge(q["t_zt"], s + 1)
                    nc.scalar.copy(H["zt"][:, s * 1024:s * 1024 + 1024], bank(2 * s, 2)).then_inc(q["a_zt"], 1)
                if j == 16:
                    mod_col(19)
                if j == 19:
                    act.wait_ge(q["t_spec"], 1)
                    nc.scalar.copy(U0[0], bank(0, 2)).then_inc(q["a_spec"], 1)
                    nc.scalar.copy(U0[1], bank(2, 2)).then_inc(q["a_spec"], 1)
                if j == 18:
                    z3 = H["zz"].rearrange("p (k c) -> p k c", k=KD)
                    for k in range(KD):
                        ins = act_fn(z3[:, k], z3[:, k], ACT.Identity, scale=V("dskip")[:, k:k + 1])
                    ins.then_inc(q["a_zd"], 1)
            mod_row(20)
            mod_col(20)
            moe(1)
            act.wait_ge(q["t_fin"], 1)
            nc.scalar.copy(fin[:, 0, :, :], bank(4, 2).rearrange("p (s c) -> p s c", s=NS)).then_inc(q["a_fin"], 1)
            act.wait_ge(q["t_fin"], 2)
            nc.scalar.copy(fin[:, 1, 0], bank(6)).then_inc(q["a_fin"], 1)

        @block.vector
        def _(dve):
            v = nc.vector

            def L(ins):
                link(dve, "d_chain", ins)

            dve.wait_ge(q["t_xT"], 1)
            xf = xT[:].rearrange("p k s t -> p (k s t)")
            v.tensor_copy(xf[:, 0:1024], bank(0, 2)).then_inc(q["d_xT"], 1)
            dve.wait_ge(q["t_rows"], 1)
            L(v.tensor_copy(VT[:, 0, 0:124], bank(4)[:, 0:124]))
            L(v.tensor_copy(VT[:, 1, 0:96], bank(4)[:, 128:224]))
            v.tensor_copy(VT[:, 2, 0:72], bank(4)[:, 256:328]).then_inc(q["d_rows"], 1)

            def norm(n):
                l, i = n // 2, n % 2
                dve.wait_ge(q["a_sqrt"], n + 1)
                L(v.reciprocal(rstd[:], rstd[:]))
                if n in (0, 3):
                    mod([0, 5][n // 3])
                for s in range(NS):
                    L(v.scalar_tensor_tensor(out=scl[:, n, :, s], in0=modT[:, l, 24 * i + 8:24 * i + 16, s], scalar=1.0,
                                             in1=V("norm_g")[:, 8 * n:8 * n + 8], op0=ALU.add, op1=ALU.mult))
                for half in (1, 0):
                    ks = slice(4 * half, 4 * half + 4)
                    ins = v.tensor_tensor(sq[:, ks], xT[:, ks], rstd[:].rearrange("p (o s) t -> p o s t", o=1).broadcast_to([P, 4, NS, T]), ALU.mult)
                    if half:
                        ins.then_inc(q["d_xn"], 1)
                L(ins)
                for k in range(4):
                    for s in range(NS):
                        ins = v.tensor_scalar(hT[:, k, s, :], sq[:, k, s, :], scl[:, n, k, s:s + 1],
                                              modT[:, l, 24 * i + k, s:s + 1], ALU.mult, ALU.add)
                    ins.then_inc(q["d_h"], 1)

            MODS_DONE = [(4, 0, 0, 16), (14, 0, 16, 40), (14, 1, 0, 16), (16, 0, 40, 48), (18, 1, 16, 24), (22, 1, 24, 40),
                         (24, 1, 40, 48)]

            def mod(g):
                units, l, a, b = MODS_DONE[g]
                dve.wait_ge(q["a_mod"], units)
                bias = V("mod_b")[:, 48 * l + a:48 * l + b].rearrange("p (j o) -> p j o", o=1).broadcast_to([P, b - a, NS])
                L(v.tensor_tensor(modT[:, l, a:b], modT[:, l, a:b], bias, ALU.add))

            lb = V("hgrn_lb")
            L(v.tensor_tensor(lbt[:, 0], lb[:, 0:8], lb[:, 8:16], ALU.max))
            L(v.tensor_tensor(lbt[:, 1], lb[:, 0:8], lbt[:, 0], ALU.subtract))
            v.tensor_tensor(lbt[:, 2], lb[:, 8:16], lbt[:, 0], ALU.subtract).then_inc(q["d_ef"], 1)
            norm(0)
            dve.wait_ge(q["a_e4"], 1)
            L(v.tensor_tensor(lbt[:, 5], lbt[:, 3], lbt[:, 4], ALU.add))
            L(v.reciprocal(lbt[:, 5], lbt[:, 5]))
            L(v.tensor_tensor(lbt[:, 0], lbt[:, 3], lbt[:, 5], ALU.mult))
            L(v.tensor_tensor(lbt[:, 1], lbt[:, 4], lbt[:, 5], ALU.mult))
            def gates(d):
                dve.wait_ge(q["a_proj"], d + 1)
                for h in range(HA):
                    sl = slice(h * 256, h * 256 + 256)
                    ins = v.tensor_scalar(E[d][:, sl], E[d][:, sl], lbt[:, 1, 4 * d + h:4 * d + h + 1],
                                          lbt[:, 0, 4 * d + h:4 * d + h + 1], ALU.mult, ALU.add)
                L(ins)
                v.tensor_scalar(K[d], E[d], -1.0, 1.0, ALU.mult, ALU.add).then_inc(q["d_kk"], 1)

            def decays(d):
                mid, last = [(CHUNK // 2, CHUNK - 1), (CHUNK - 1 - CHUNK // 2, 0)][d]
                dve.wait_ge(q["a_lf"], d + 1)
                if d == 0:
                    dve.wait_ge(q["g_const"], 8)
                    L(v.tensor_tensor_scan(B[d], seg[:], E[d], 0.0, ALU.mult, ALU.add))
                else:
                    L(v.tensor_tensor_scan(B[d][:, ::-1], seg[:], E[d][:, ::-1], 0.0, ALU.mult, ALU.add))
                b3 = B[d].rearrange("p (c t) -> p c t", t=CHUNK)
                x3 = X[d].rearrange("p (c t) -> p c t", t=CHUNK)
                t3 = A["tmp"].rearrange("p (c t) -> p c t", t=CHUNK)
                v.tensor_tensor(x3, b3, b3[:, :, mid:mid + 1].broadcast_to([P, 16, CHUNK]), ALU.subtract).then_inc(q["d_x1"], 1)
                if d == 1:
                    dve.wait_ge(q["d_kc"], 1)
                v.tensor_tensor(t3, b3[:, :, last:last + 1].broadcast_to([P, 16, CHUNK]), b3, ALU.subtract).then_inc(q["d_x2"], 1)
                dve.wait_ge(q["a_eb"], d + 1)
                v.tensor_tensor(X[d], X[d], K[d], ALU.mult).then_inc(q["d_kd"], 1)
                dve.wait_ge(q["a_e3"], d + 1)
                dve.wait_ge(q["d_kd"], d + 1)
                L(v.tensor_copy(decs[:, d, :], B[d].rearrange("p (c t) -> p c t", t=CHUNK)[:, :, last]))
                v.tensor_tensor(K[d], K[d], A["tmp"], ALU.mult).then_inc(q["d_kc"], 1)

            for d in range(2):
                gates(d)
                decays(d)
            dve.wait_ge(q["a_qksq"], 1)
            v.tensor_reduce(small[:, 0:20], sqk.rearrange("p (n c) -> p n c", c=HD), AX.X, ALU.add).then_inc(q["d_var"], 1)
            dve.wait_ge(q["a_qksd"], 1)
            dve.wait_ge(q["small_in"], 16 * 7)
            L(v.reciprocal(small[:, 20:40], small[:, 20:40]))
            qk4 = A["qk"].rearrange("p (s n c) -> p s n c", s=NS, c=HD)
            rs = small[:, 20:40].rearrange("p (s n o) -> p s n o", s=NS, o=1)
            for s in range(NS):
                L(v.tensor_tensor(qn[:, s].rearrange("p (c g) d -> p g c d", g=KV),
                                  qk4[:, s, 0:8].rearrange("p (g c) d -> p g c d", g=KV),
                                  rs[:, s, 0:8].rearrange("p (g c) o -> p g c o", g=KV).broadcast_to([P, KV, 4, HD]), ALU.mult))
                L(v.tensor_tensor(qk4[:, s, 8:10], qk4[:, s, 8:10], rs[:, s, 8:10].broadcast_to([P, KV, HD]), ALU.mult))
                L(v.tensor_tensor(qn[:, s], qn[:, s], gqk[:, 0:1].broadcast_to([P, 8, HD]), ALU.mult))
                L(v.tensor_tensor(qk4[:, s, 8:10], qk4[:, s, 8:10], gqk[:, 1:2].broadcast_to([P, 2, HD]), ALU.mult))
            s4 = C("sin").rearrange("p (o r h c) -> p o r h c", o=1, r=2, h=2)
            for xs, t2, n in [(qn[:, 1], A["qk"][:, 0:512], 8), (qk4[:, 1, 8:10], A["qk"][:, 640:768], 2)]:
                t24 = t2.rearrange("p (n r h c) -> p n r h c", r=2, h=2, c=16)
                x4 = xs.rearrange("p n (r h c) -> p n r h c", r=2, h=2)
                for hh in range(2):
                    L(v.tensor_tensor(t24[:, :, :, hh], x4[:, :, :, 1 - hh], s4[:, :, :, hh].broadcast_to([P, n, 2, 16]), ALU.mult))
                L(v.tensor_tensor(xs, xs, C("cos").rearrange("p (o c) -> p o c", o=1).broadcast_to([P, n, HD]), ALU.mult))
                ins = v.tensor_tensor(xs, xs, t2.rearrange("p (n c) -> p n c", c=HD), ALU.add)
                if n == 8:
                    L(ins)
            ins.then_inc(q["d_qk"], 1)
            dve.wait_ge(q["a_proj"], QA + 1)
            for d in range(2):
                v.tensor_tensor(E[d], E[d], A["q"], ALU.mult).then_inc(q["d_aq"], 1)
            for d in range(2):
                v.tensor_tensor(B[d], B[d], A["q"], ALU.mult).then_inc(q["d_q2"], 1)
            for d in range(2):
                dve.wait_ge(q["t_att"], d + 1)
                a4 = att[d].rearrange("p (n t) -> p n t", t=T)
                src = bank(4 + d).rearrange("p (n t) -> p n t", t=CHUNK)
                m = C("mask_r" if d else "mask_f").bitcast(U32)
                for c in range(2):
                    rows = slice(c * 64, c * 64 + 64)
                    mb = m[rows].rearrange("p (o t) -> p o t", o=1).broadcast_to([64, 8, CHUNK])
                    ins = v.copy_predicated(a4[rows, :, c * 64:c * 64 + 64], mb, src[rows])
                ins.then_inc(q["d_att"], 1)
            dve.wait_ge(q["state_in"], 32)
            for d in range(2):
                first, second = (0, 1) if d == 0 else (1, 0)
                dec = decs[:, d, :].rearrange("p (h s c) -> p h s c", h=HA, s=NS)
                Uf, Us = (bank(b).rearrange("p (h c) -> p h c", h=HA) for b in (4, 5))
                dve.wait_ge(q["t_U"], 2 * d + 1)
                L(v.tensor_copy(S1[:, d, 0], Uf))
                for h in range(HA):
                    ins = v.scalar_tensor_tensor(out=Sfin[:, d, h], in0=S1[:, d, 0, h],
                                                 scalar=dec[:, h, 0, second:second + 1],
                                                 in1=Us[:, h], op0=ALU.mult, op1=ALU.add)
                ins.then_inc(q["d_state"], 1)
                dve.wait_ge(q["t_U"], 2 * d + 2)
                for h in range(HA):
                    ins = v.scalar_tensor_tensor(out=S1[:, d, 1, h], in0=S0[:, d, h], scalar=dec[:, h, 1, first:first + 1],
                                                 in1=Uf[:, h], op0=ALU.mult, op1=ALU.add)
                ins.then_inc(q["d_state"], 1)

            def score_max(s, b, nb, keys, at):
                dve.wait_ge(q["t_sc"], 2 - s)
                L(v.tensor_reduce(small[:, at:at + 8], bank(b, nb).rearrange("p (h c) -> p h c", c=keys), AX.X, ALU.max))
                v.tensor_scalar(small[:, at:at + 8], small[:, at:at + 8], -HD ** -0.5, None, ALU.mult).then_inc(q["d_max"], 1)

            score_max(1, 0, 4, 256, 48)
            for half in range(2):
                dve.wait_ge(q["a_osqrt"], half + 1)
                r = osd[:, half * 512:half * 512 + 512]
                L(v.reciprocal(r, r))
                L(v.tensor_tensor(r, bank(4 + half), r, ALU.mult))
            dve.wait_ge(q["a_proj"], 7)
            for h in range(HA):
                r4 = osd.rearrange("p (s h t) -> p s h t", s=NS, h=HA)
                ins = v.scalar_tensor_tensor(out=catT[:, h], in0=r4[:, :, h], scalar=V("onorm")[:, h:h + 1],
                                             in1=sga[:, h], op0=ALU.mult, op1=ALU.mult)
            ins.then_inc(q["d_oA"], 1)
            dve.wait_ge(q["t_pT"], 1)
            v.tensor_copy(pT_s[:, 1024:2048], bank(2, 2)).then_inc(q["d_pT"], 1)
            score_max(0, 4, 2, 128, 56)
            for s, b, sums in [(1, 7, 64), (0, 7, 72)]:
                dve.wait_ge(q["t_pv"], 2 - s)
                L(v.reciprocal(small[:, sums:sums + 8], small[:, sums:sums + 8]))
                v.tensor_tensor(otm[:, s * 512:s * 512 + 512].rearrange("p (h c) -> p h c", c=HD),
                                bank(b).rearrange("p (h c) -> p h c", c=HD),
                                small[:, sums:sums + 8].rearrange("p (h o) -> p h o", o=1).broadcast_to([P, 8, HD]),
                                ALU.mult).then_inc(q["d_o"], 1)
            mod(1)
            mod(2)

            def residual(l, g, banks, units=None):
                for k in range(KD):
                    if k % 4 == 0:
                        if units is None:
                            dve.wait_ge(q["m_add"], 2 * l + k // 4 + 1)
                        else:
                            products_of(dve, units + k // 4)
                    for s in range(NS):
                        src = bank(banks[k // 2])[:, (k % 2) * 256 + s * 128:(k % 2) * 256 + s * 128 + 128]
                        ins = v.scalar_tensor_tensor(out=xT[:, k, s, :], in0=src, scalar=modT[:, l, g * 8 + k, s:s + 1],
                                                     in1=xT[:, k, s, :], op0=ALU.mult, op1=ALU.add)
                    if k % 4 == 3:
                        ins.then_inc(q["d_x"], 1)

            dve.wait_ge(q["decay_in"], 16)
            for i in range(2):
                dve.wait_ge(q["hy_f"], i + 1)
                v.tensor_tensor(filt[:, i * 1024:i * 1024 + 1024], bank([4, 6][i], 2), decay, ALU.mult).then_inc(q["hy_fd"], 1)
            residual(0, 2, [0, 1, 2, 3], OUT0_AT)
            L(v.tensor_copy(tri16[:, 0], C("tri")))

            def rank(bi, n, gt, eq, out):
                bj = bi.rearrange("p (n o j) -> p n o j", o=1, j=4).broadcast_to([P, n, 4, 4])
                b_i = bi.rearrange("p (n i o) -> p n i o", i=4, o=1).broadcast_to([P, n, 4, 4])
                g4 = gt.rearrange("p (n i j) -> p n i j", i=4, j=4)
                e4 = eq.rearrange("p (n i j) -> p n i j", i=4, j=4)
                L(v.tensor_tensor(g4, bj, b_i, ALU.is_gt))
                L(v.tensor_tensor(e4, bj, b_i, ALU.is_equal))
                e3 = eq.rearrange("p (n i) -> p n i", i=16)
                L(v.tensor_tensor(e3, e3, C("tie").rearrange("p (o c) -> p o c", o=1).broadcast_to([P, n, 16]), ALU.mult))
                L(v.tensor_tensor(gt, gt, eq, ALU.add))
                L(v.tensor_reduce(out, gt.rearrange("p (n j) -> p n j", j=4), AX.X, ALU.add))

            def moe(l):
                if l == 0:
                    dve.wait_ge(q["cache_out"], 16 * 6)
                norm(2 * l + 1)

                def col(a, n):
                    return a.rearrange("p (s o) -> p s o", o=1).broadcast_to([P, NS, n])

                def g3(a):
                    return a.rearrange("p (s e) -> p s e", s=NS)

                dve.wait_ge(q["t_log"], l + 1)
                lg = g3(bank(7)[:, 256:288])
                L(v.tensor_reduce(R["c1"], lg, AX.X, ALU.max))
                v.tensor_tensor(g3(R["lg"]), lg, col(R["c1"], NE), ALU.subtract).then_inc(q["d_lg"], 1)
                dve.wait_ge(q["a_re"], l + 1)
                L(v.tensor_reduce(R["c2"], g3(R["e"]), AX.X, ALU.add))
                L(v.reciprocal(R["c2"], R["c2"]))
                L(v.tensor_tensor(g3(R["score"]), g3(R["e"]), col(R["c2"], NE), ALU.mult))
                L(v.tensor_tensor(g3(R["bi"]), g3(R["score"]),
                                  rb[:].rearrange("p (o e) -> p o e", o=1).broadcast_to([P, NS, NE]), ALU.add))
                rank(R["bi"], 8, R["gt"], R["eq"], R["rank"])
                L(v.tensor_scalar(R["selE"], R["rank"], 1.5, None, ALU.is_lt))
                L(v.tensor_tensor(R["bs"], R["bi"], R["selE"], ALU.mult))
                L(v.tensor_reduce(R["gs"], R["bs"].rearrange("p (n j) -> p n j", j=4), AX.X, ALU.add))
                rank(R["gs"], 2, R["gt"][:, 0:32], R["eq"][:, 0:32], R["grank"])
                L(v.tensor_scalar(R["selG"], R["grank"], 0.5, None, ALU.is_lt))
                L(v.tensor_tensor(R["mask"].rearrange("p (n j) -> p n j", j=4), R["selE"].rearrange("p (n j) -> p n j", j=4),
                                  R["selG"].rearrange("p (n o) -> p n o", o=1).broadcast_to([P, 8, 4]), ALU.mult))
                v.tensor_copy(mask16[:, 0:32], R["mask"]).then_inc(q["d_mask"], 1)
                L(v.tensor_tensor(R["w"], R["score"], R["mask"], ALU.mult))
                L(v.tensor_reduce(R["c3"], g3(R["w"]), AX.X, ALU.add))
                L(v.reciprocal(R["c3"], R["c3"]))
                L(v.tensor_tensor(g3(R["gate"]), g3(R["w"]), col(R["c3"], NE), ALU.mult))
                dve.wait_ge(q["t_pos"], l + 1)
                pos = bank(7)[:, 288:320]
                L(v.tensor_scalar(R["over"], pos, CAP - 0.5, None, ALU.is_gt))
                L(v.tensor_tensor(R["over"], R["over"], R["gate"], ALU.mult))
                L(v.tensor_scalar(R["pos"], pos, 1.0, None, ALU.add))
                L(v.tensor_tensor(R["pos"], R["pos"], R["mask"], ALU.mult))
                L(v.tensor_scalar(R["pos"], R["pos"], -1.0, None, ALU.add))
                L(v.tensor_reduce(R["mxc"], bank(7)[:, 320:336], AX.X, ALU.max))
                v.tensor_scalar(flag[:, l:l + 1], R["mxc"], CAP + 0.5, None, ALU.is_gt).then_inc(q["d_flag"], 1)
                S4 = M["S"].rearrange("p (s e c) -> p s e c", s=NS, e=NE)
                pos3 = R["pos"].rearrange("p (s e o) -> p s e o", s=NS, o=1)
                for s, a, b in [(slice(0, 2), 0, 2), (slice(0, 1), 2, NE), (slice(1, 2), 2, NE)]:
                    ns = s.stop - s.start
                    v.tensor_tensor(S4[:, s, a:b], C("slot").rearrange("p (u o c) -> p u o c", u=1, o=1).broadcast_to([P, ns, b - a, CAP]),
                                    pos3[:, s, a:b].broadcast_to([P, ns, b - a, CAP]), ALU.is_equal).then_inc(q["d_S"], 1)
                if l == 0:
                    mod(3)
                n0, n2 = l * NPAIR, 2 * l * NPAIR

                def pair(i):
                    dve.wait_ge(q["m_xg"], i + (n0 + 1))
                    v.tensor_copy(xg[:, 4:8, :].rearrange("p k c -> p (k c)"), bank(5)).then_inc(q["d_xg"], 1)
                    dve.wait_ge(q["a_sg"], i + (n0 + 1))
                    products_of(dve, MOE_AT[l] + 3, i)
                    for half in range(2):
                        c = half * 256
                        v.tensor_tensor(M["hid"][:, c:c + 256], bank(5)[:, c:c + 256], M["sg"][:, c:c + 256],
                                        ALU.mult).then_inc(q["d_hid"], 1)
                    dve.wait_ge(q["m_hT"], i + (n0 + 1))
                    v.tensor_copy(M["hidT"][:, 256:512], bank(7)[:, 0:256]).then_inc(q["d_hT"], 1)
                    products_of(dve, MOE_AT[l] + 5, i)
                    v.tensor_copy(y[:, 512:1024], bank(7)).then_inc(q["d_y"], 1)

                pair(0)
                with dve.Fori(1, NPAIR - 1) as i:
                    pair(i)
                pair(NPAIR - 1)
                if l:
                    mod(6)
                residual(l, 5, [0, 1, 2, 3])
                dve.wait_ge(q["d_flag"], l + 1)
                more = dve.value_load(flag[0:1, l:l + 1])
                with dve.If(more > 0):
                    dve.wait_ge(q["d_x"], 4 * l + 4)
                    v.tensor_copy(small[:, 91:92], xT[:, 0, 0, 0:1]).then_inc(fb["fb_done"][l], 1)
                    with dve.Fori(0, NE) as e:
                        for s in range(NS):
                            v.tensor_copy(R["gcol"][:, s:s + 1], R["over"][:, bass.ds(e + s * NE, 1)]).then_inc(fb["fb_col"][l], 1)
                            dve.wait_ge(fb["fb_col"][l], e * 2 + (s + 1))
                            dve.wait_ge(fb["fb_silu"][l], e * 2 + (s + 1))
                            v.scalar_tensor_tensor(out=M["fh"], in0=bank(5), scalar=R["gcol"][:, s:s + 1], in1=M["fh"],
                                                   op0=ALU.mult, op1=ALU.mult).then_inc(fb["fb_hid"][l], 1)
                            dve.wait_ge(fb["fb_tr"][l], e * 2 + (s + 1))
                            v.tensor_copy(M["fhT"], bank(6)).then_inc(fb["fb_hidT"][l], 1)
                            dve.wait_ge(fb["fb_down"][l], e * 2 + (s + 1))
                            for k in range(KD):
                                ins = v.scalar_tensor_tensor(
                                    out=xT[:, k, s, :], in0=bank(0, 2)[:, k * 128:k * 128 + 128],
                                    scalar=modT[:, l, 40 + k, s:s + 1], in1=xT[:, k, s, :], op0=ALU.mult, op1=ALU.add)
                            ins.then_inc(fb["fb_done"][l], 1)
                            dve.wait_ge(fb["fb_done"][l], e * 2 + (s + 2))
            moe(0)
            norm(2)
            ub4 = H["ub"].rearrange("p (b s t) -> p b s t", b=4, s=NS)
            uc4 = H["uc"].rearrange("p (b s t) -> p b s t", b=4, s=NS)
            L(v.memset(ub4[:, :, :, 0:1], 0.0))
            L(v.memset(ub4[:, :, :, T + 1:T + 2], 0.0))
            cw, cb = V("hy_conv_w"), V("hy_conv_b")

            def spectral(s, part):
                if s:
                    dve.wait_ge(q["t_spec"], 2)
                    Ua, Ub = bank(0, 2), bank(2, 2)
                else:
                    dve.wait_ge(q["a_spec"], 2)
                    Ua, Ub = U0
                ya, yb = YS[s]
                if part == 0:
                    L(v.tensor_tensor(ya, Ua, H["KA"], ALU.mult))
                    L(v.tensor_tensor(t1, Ub, H["KB"], ALU.mult))
                    L(v.tensor_tensor(ya, ya, t1, ALU.subtract))
                else:
                    L(v.tensor_tensor(yb, Ua, H["KB"], ALU.mult))
                    L(v.tensor_tensor(t1, Ub, H["KC"], ALU.mult))
                    v.tensor_tensor(yb, yb, t1, ALU.add).then_inc(q["d_spec"], 1)
                    dve.wait_ge(q["d_spec"], s + 1)

            for j in range(24):
                ch = HY_ORDER[j]
                u, o = ub4[:, j % 4], uc4[:, j % 4]
                dst = {1: H["x1"], 2: o, 0: H["x0"]}[ch // 8]
                if ch // 8 != 2:
                    dst = dst.rearrange("p (k s t) -> p k s t", k=KD, s=NS)[:, ch % 8]
                dve.wait_ge(q["a_u"], j + 1)
                L(v.tensor_scalar(o, u[:, :, 1:T + 1], cw[:, 24 + ch:25 + ch], cb[:, ch:ch + 1], ALU.mult, ALU.add))
                L(v.scalar_tensor_tensor(out=o, in0=u[:, :, 0:T], scalar=cw[:, ch:ch + 1], in1=o, op0=ALU.mult, op1=ALU.add))
                v.scalar_tensor_tensor(out=dst, in0=u[:, :, 2:T + 2], scalar=cw[:, 48 + ch:49 + ch], in1=o,
                                       op0=ALU.mult, op1=ALU.add).then_inc(q["d_uc"], 1)
                dve.wait_ge(q["d_uc"], j + 1)
                if ch // 8 == 2:
                    k = ch % 8
                    v.tensor_tensor(H["zz"].rearrange("p (k s t) -> p k s t", k=KD, s=NS)[:, k], dst,
                                    H["x1"].rearrange("p (k s t) -> p k s t", k=KD, s=NS)[:, k],
                                    ALU.mult).then_inc(q["d_zz"], 1)
                if 19 <= j <= 22:
                    spectral((j - 19) // 2, (j - 19) % 2)
            for s in range(NS):
                dve.wait_ge(q["t_y"], s + 1)
                dve.wait_ge(q["a_zd"], 1)
                z4 = H["zz"].rearrange("p (k s t) -> p k s t", k=KD, s=NS)[:, :, s]
                x04 = H["x0"].rearrange("p (k s t) -> p k s t", k=KD, s=NS)[:, :, s]
                L(v.tensor_tensor(z4, z4, bank(4 + 2 * s, 2).rearrange("p (k t) -> p k t", k=KD), ALU.add))
                v.tensor_tensor(x04, x04, z4, ALU.mult).then_inc(q["d_r"], 1)
            mod(4)
            residual(1, 2, [0, 1, 2, 3], OUT1_AT)
            moe(1)
            dve.wait_ge(q["t_fin"], 2)
            v.tensor_copy(fin[:, 1, 1], bank(7)).then_inc(q["d_fin"], 1)

        @block.tensor
        def _(pe):
            mm = nc.tensor.matmul
            tr = nc.tensor.transpose

            xin = arena[:, 0:2048].rearrange("p (s d) -> p s d", s=NS)
            pe.wait_ge(q["cst_in"], 16)
            pe.wait_ge(q["x_in"], 32)
            for k in range(KD):
                for s in range(NS):
                    c = k * 256 + s * 128
                    ins = tr(bank(0, 4)[:, c:c + 128], xin[:, s, k * 128:k * 128 + 128], ident)
            ins.then_inc(q["t_xT"], 1)
            pe.wait_ge(q["rows_in"], 16 * 6)
            pe.wait_ge(q["more_rows_in"], 16 * 4)
            for t in range(3):
                n = ROWS_IN_TILE[t]
                ins = tr(bank(4)[:, t * 128:t * 128 + n], rows[0:n, t, :], ident[0:n, 0:n])
            ins.then_inc(q["t_rows"], 1)

            def norm(n):
                if n == 0:
                    pe.wait_ge(q["g_const"], 8)
                for k in range(KD):
                    if k % 4 == 0:
                        pe.wait_ge(q["a_sq"], 2 * n + k // 4 + 1)
                    ins = mm(bank(7)[:, 0:256], ones[:], sq[:, k].rearrange("p s t -> p (s t)"),
                             start=(k == 0), stop=(k == KD - 1))
                ins.then_inc(q["t_ss"], 1)

            def used(ins, n):
                ins.then_inc(ring_free[n % RING], 1)

            def mod_row(m):
                n = MOD_AT[m]
                arrived(pe, n)
                if m == 0:
                    pe.wait_ge(q["a_cs"], 1)
                else:
                    pe.wait_ge(q["a_mod"], MOD_TURN[m])
                if m in (14, 15):
                    pe.wait_ge(q["hy_a"], m - 13)
                for k in range(KD):
                    for g in range(4):
                        ins = mm(mod_bank(m)[32 * g:32 * g + 32, 0:128], csil[:, k, :], unit(n)[:, k, g * 128:g * 128 + 128],
                                 start=(k == 0), stop=(k == KD - 1))
                used(ins, n)

            def mod_col(m):
                pe.wait_ge(q["a_row"], MOD_TURN[m] + 1)
                tr(mod_bank(m)[:, 0:128], mrow(m), ident).then_inc(q["t_sel"], 1)

            mod_row(0)
            norm(0)
            mod_col(0)
            for m in range(1, 4):
                mod_row(m)
                mod_col(m)

            def hk(k):
                return hT[:, k].rearrange("p s t -> p (s t)")

            KORDER = [4, 0, 5, 1, 6, 2, 7, 3]

            def h_ready(n, k):
                if k < 4:
                    pe.wait_ge(q["d_h"], 4 * n + k + 1)
                else:
                    pe.wait_ge(q["a_h"], 4 * n + k - 3)

            def projection(j, part):
                n = AB_AT[j]
                b = 2 * (j % 2)
                if part == 0:
                    arrived(pe, n)
                    if j >= 2:
                        pe.wait_ge(q["a_proj"], j - 1)
                    if j == 0:
                        pe.wait_ge(q["a_xT"], 1)
                        pe.wait_ge(q["d_xT"], 1)
                if j in (ZF, ZB, QA, GA):
                    for k in KORDER:
                        if (j, part) == (0, 0):
                            h_ready(0, k)
                        ins = mm(bank(b, 2)[:, part * 256:part * 256 + 256], unit(n)[:, k, part * 128:part * 128 + 128],
                                 hk(k), start=(k == KORDER[0]), stop=(k == KORDER[-1]))
                else:
                    w = 256 if j == KVB else 512
                    s = part // 2
                    for k in range(4 * (part % 2), 4 * (part % 2) + 4):
                        ins = mm(bank(b + s)[:, 0:w], hT[:, k, s, :], unit(n)[:, k, 0:w],
                                 start=(k == 0), stop=(k == KD - 1))
                if part == 3:
                    used(ins, n)

            def at(d):
                pe.wait_ge(q["d_kd"], d + 1)
                pe.wait_ge(q["d_aq"], d + 1)
                Aq = E[d].rearrange("p (h s t) -> p h s t", h=HA, s=NS)
                Kd = X[d].rearrange("p (h s t) -> p h s t", h=HA, s=NS)
                for c in range(2):
                    for s in range(NS):
                        for h in range(HA):
                            col = (s * HA + h) * 64
                            ins = mm(bank(4 + d)[c * 64:c * 64 + 64, col:col + 64], Kd[:, h, s, c * 64:c * 64 + 64],
                                     Aq[:, h, s, c * 64:c * 64 + 64], start=True, stop=True)
                ins.then_inc(q["t_att"], 1)

            def kc(d, s):
                pe.wait_ge(q["d_kc"], d + 1)
                Kc = K[d].rearrange("p (h s t) -> p h s t", h=HA, s=NS)
                for h in range(HA):
                    ins = tr(bank(7)[:, h * 128:h * 128 + 128], Kc[:, h, s, :], ident)
                ins.then_inc(q["t_kcT"], 1)

            vtm = A["v"].rearrange("p (s h c) -> p s h c", s=NS, h=HA)

            def chunk_states(d, s):
                n = 2 * d + s
                pe.wait_ge(q["a_kcT"], n + 1)
                pe.wait_ge(q["d_att"], 2)
                if n:
                    pe.wait_ge(q["d_state"], n)
                kT3 = A["kcT"].rearrange("p (h c) -> p h c", h=HA)
                first, second = (0, 1) if d == 0 else (1, 0)
                for c, b in [(first, 4), (second, 5)][:2 - s]:
                    rows = slice(c * 64, c * 64 + 64)
                    for h in range(HA):
                        ins = mm(bank(b)[:, h * 128:h * 128 + 128], kT3[rows, h, :], vtm[rows, s, h, :],
                                 start=True, stop=True)
                ins.then_inc(q["t_U"], 1)

            def turn_qk():
                pe.wait_ge(q["d_qk"], 1)
                pe.wait_ge(q["cache_in"], 64)
                qkt = A["qk"].rearrange("p (s c) -> p s c", s=NS)
                for s in range(NS):
                    for c in range(4):
                        src = qn[:, s, 2 * c:2 * c + 2].rearrange("p g d -> p (g d)")
                        tr(bank(4 + s)[:, c * 128:c * 128 + 128], src, ident)
                    tr(bank(7)[:, s * 128:s * 128 + 128], qkt[:, s, 512:640], ident)
                tr(bank(7)[:, 256:384], ckv[:, 0], ident).then_inc(q["t_qkT"], 1)

            def recurrence_out():
                pe.wait_ge(q["d_state"], 4)
                pe.wait_ge(q["d_q2"], 2)
                for s in range(NS):
                    for h in range(HA):
                        o = bank(4 + s)[:, h * 128:h * 128 + 128]
                        for d in range(2):
                            mm(o, vtm[:, s, h, :], att[d].rearrange("p (s h t) -> p s h t", s=NS, h=HA)[:, s, h, :],
                               start=(d == 0), stop=False)
                        for d in range(2):
                            Q2 = B[d].rearrange("p (h s t) -> p h s t", h=HA, s=NS)
                            first, second = (0, 1) if d == 0 else (1, 0)
                            for c, st in ([(second, S1[:, d, s, h, :])] + ([(first, S0[:, d, h, :])] if s == 1 else [])):
                                last = d == 1 and (s == 0 or c == first)
                                ins = mm(o[:, c * 64:c * 64 + 64], st, Q2[:, h, s, c * 64:c * 64 + 64], start=False, stop=last)
                ins.then_inc(q["t_o"], 1)

            def scores(s, banks, keys, nk):
                for h in range(HB):
                    g, c = h // 4, h % 4
                    rows = slice(64 * g, 64 * g + 64)
                    out = bank(banks, 4)[:, h * nk:h * nk + nk] if nk == 256 else bank(banks, 2)[:, h * nk:h * nk + nk]
                    ins = mm(out, qT[rows, s, c, :], keys[rows], start=True, stop=True)
                ins.then_inc(q["t_sc"], 1)

            def squares(half):
                pe.wait_ge(q["a_osq"], half + 1)
                if half:
                    pe.wait_ge(q["a_osqrt"], 1)
                mm(bank(7), ones[:], sqs[:, half * 512:half * 512 + 512], start=True, stop=True).then_inc(q["t_oss"], 1)

            def turn_probs(s, b, src, nk):
                pe.wait_ge(q["a_exp"], 2 - s)
                nkb = nk // 128
                for h in range(HB):
                    for kb in range(nkb):
                        c = (h * nkb + kb) * 128
                        ins = tr(bank(b, 4 if s else 2)[:, c:c + 128], src[:, c:c + 128], ident)
                ins.then_inc(q["t_pT"], 1)

            def attend(s, b, pT, nkb):
                pe.wait_ge(q["a_pT"], 2 - s)
                pe.wait_ge(q["d_pT"], 1)
                pe.wait_ge(q["a_osqrt"], 2)
                for h in range(HB):
                    g = h // 4
                    for kb in range(nkb):
                        c = (h * nkb + kb) * 128
                        vals = ckv[:, 1, g * 64:g * 64 + 64] if kb else A["vb"][:, s * 128 + g * 64:s * 128 + g * 64 + 64]
                        ins = mm(bank(b)[:, h * 64:h * 64 + 64], pT[:, c:c + 128], vals, start=(kb == 0), stop=(kb == nkb - 1))
                ins.then_inc(q["t_pv"], 1)

            def turn_out(s, b):
                pe.wait_ge(q["d_o"], 2 - s)
                for c in range(4):
                    ins = tr(bank(b)[:, c * 128:c * 128 + 128], otm[:, s * 512 + c * 128:s * 512 + c * 128 + 128], ident)
                ins.then_inc(q["t_oT"], 1)

            def open_accumulators():
                for b in range(4):
                    mm(bank(b), zero16[:], zero16[:].rearrange("p (o c) -> p o c", o=1).broadcast_to([P, 4, 128]),
                       start=True, stop=False, skip_group_check=True)

            def out_chunk(k8, ks):
                n = OUT0_AT + k8 // 4
                for k in ks:
                    ins = mm(bank(k8 // 2)[:, (k8 % 2) * 256:(k8 % 2) * 256 + 256],
                             unit(n)[:, k, (k8 % 4) * 128:(k8 % 4) * 128 + 128], hk(k),
                             start=False, stop=(k == KD - 1), skip_group_check=True)
                return ins

            def out_part(k8):
                if k8 == 0:
                    pe.wait_ge(q["d_oA"], 1)
                    pe.wait_ge(q["a_pT"], 1)
                    pe.wait_ge(q["d_pT"], 1)
                    open_accumulators()
                if k8 % 4 == 0:
                    arrived(pe, OUT0_AT + k8 // 4)
                out_chunk(k8, range(0, 4))

            def network_layer(i):
                pe.wait_ge(q["a_mod"], 12 + i)
                if i == 0:
                    pe.wait_ge(q["fw_in"], 32)
                    pe.wait_ge(q["hyc_in"], 16)
                    mm(bank(6)[0:HY, 0:128], fw[0:EMB, 0], HC("zT")[0:EMB, :], start=True, stop=True).then_inc(q["hy_l"], 1)
                else:
                    pe.wait_ge(q["hy_s"], 1)
                    mm(bank(6)[0:HY, 0:128], fw[0:HY, 1], hid1[:, 1, :], start=True, stop=True).then_inc(q["hy_l"], 1)

            for step in SCHED:
                what, a = step[0], step[1:]
                if what == "proj":
                    projection(*a)
                elif what == "R":
                    mod_row(*a)
                elif what == "S":
                    mod_col(*a)
                elif what == "at":
                    if a[0] == 0:
                        pe.wait_ge(q["a_qkT"], 1)
                    at(*a)
                elif what == "qkT":
                    turn_qk()
                elif what == "kc":
                    kc(*a)
                elif what == "U":
                    chunk_states(*a)
                elif what == "o":
                    recurrence_out()
                elif what == "sc" and a[0] == 1:
                    pe.wait_ge(q["a_proj"], 7)
                    scores(1, 0, kT[:, 1:3].rearrange("p c t -> p (c t)"), 256)
                elif what == "sc":
                    pe.wait_ge(q["d_oA"], 1)
                    scores(0, 4, kT[:, 0], 128)
                elif what == "oss":
                    squares(*a)
                elif what == "pT" and a[0] == 1:
                    turn_probs(1, 0, probs_s, 256)
                elif what == "pT":
                    turn_probs(0, 4, probs_p, 128)
                elif what == "pv" and a[0] == 1:
                    attend(1, 7, pT_s, 2)
                elif what == "pv":
                    pe.wait_ge(q["a_cat"], 1)
                    attend(0, 7, pT_p, 1)
                elif what == "oT":
                    turn_out(a[0], 7)
                elif what == "op":
                    out_part(*a)
                elif what == "hy":
                    network_layer(*a)
            pe.wait_ge(q["a_cat"], 2)

            def out_projection(at_unit, banks, src, between):
                for half in range(2):
                    n = at_unit + half
                    arrived(pe, n)
                    for c in range(4):
                        k8 = half * 4 + c
                        out = bank(banks[k8 // 2])[:, (k8 % 2) * 256:(k8 % 2) * 256 + 256]
                        for k in range(KD):
                            ins = mm(out, unit(n)[:, k, c * 128:c * 128 + 128], src(k), start=(k == 0), stop=(k == KD - 1))
                        if c == 3:
                            used(ins, n)
                        between(k8)

            def spectrum(i):
                pe.wait_ge(q["hy_fd"], 2)
                nm, b = ["ka", "kb", "kc"][i], [4, 1, 3][i]
                for half in range(2):
                    for j in range(2):
                        ins = mm(bank(b + half), HC(nm + str(j)), filt[:, j * 1024 + half * 512:j * 1024 + half * 512 + 512],
                                 start=(j == 0), stop=(j == 1))
                ins.then_inc(q["hy_k"], 1)

            def filter_step(k8):
                if k8 == 4:
                    pe.wait_ge(q["hy_s"], 2)
                    pe.wait_ge(q["w3_in"], 16)
                    pe.wait_ge(q["a_mod"], 14)
                    for i, b in enumerate([4, 5, 6, 7]):
                        ins = mm(bank(b), hid1[:, 3, :], w3s[0:HY, i * 512:i * 512 + 512], start=True, stop=True)
                        if i % 2:
                            ins.then_inc(q["hy_f"], 1)
                if k8 == 7:
                    spectrum(0)

            for k8 in range(8):
                ins = out_chunk(k8, range(4, KD))
                if k8 % 4 == 3:
                    used(ins, OUT0_AT + k8 // 4)
                filter_step(k8)

            def moe(l):
                mod_row([10, 21][l])
                norm(2 * l + 1)
                mod_col([10, 21][l])
                if l == 0:
                    pe.wait_ge(q["d_x"], 2)
                    spectrum(1)
                    pe.wait_ge(q["a_k"], 1)
                    spectrum(2)
                else:
                    mod_row(22)
                pe.wait_ge(q["small_in"], 16 * 7)
                for k in KORDER:
                    h_ready(2 * l + 1, k)
                    g = 32 * (k % 4)
                    ins = mm(bank(0)[g:g + 32, 0:256], rw[:, k, :], hk(k), start=(k >= 4), stop=(k < 4))
                ins.then_inc(q["t_lrow"], 1)
                if l:
                    mod_col(22)
                pe.wait_ge(q["a_lrow"], l + 1)
                for s in range(NS):
                    ins = mm(bank(7)[:, 256 + s * 16:272 + s * 16], lrow[:, s * 128:s * 128 + 128], C("sel"),
                             start=True, stop=True)
                ins.then_inc(q["t_log"], 1)
                mod_row([11, 23][l])
                if l == 0:
                    pe.wait_ge(q["a_k"], 3)
                for s in range(NS):
                    for k in range(KD):
                        c = s * 1024 + k * 128
                        ins = tr(bank(0, 4)[:, c:c + 128], hT[:, k, s, :], ident)
                ins.then_inc(q["t_htm"], 1)
                mod_col([11, 23][l])
                pe.wait_ge(q["d_mask"], l + 1)
                b7 = bank(7)
                tri, one, m0, m1 = tri16[:, 0], tri16[:, 1], mask16[:, 0:16], mask16[:, 16:32]
                mm(b7[:, 288:320], tri, mask16[:, 0:32], start=True, stop=False)
                mm(b7[:, 304:320], one, m0, start=False, stop=True)
                mm(b7[:, 320:336], one, m0, start=True, stop=False)
                mm(b7[:, 320:336], one, m1, start=False, stop=True).then_inc(q["t_pos"], 1)
                n = MOE_AT[l]
                n0, n2 = l * NPAIR, 2 * l * NPAIR

                def turn_gates():
                    sgt = sqs[:, 0:2048].rearrange("p (s g c) -> p s g c", s=NS, g=NPAIR)
                    for s in range(NS):
                        pe.wait_ge(q["g_sg"], 2 * l + s + 1)
                        for g in range(NPAIR):
                            c = g * 256 + s * 128
                            ins = tr(bank(0, 4)[:, c:c + 128], sgt[:, s, g, :], ident)
                    ins.then_inc(q["t_ST"], 1)

                def pack(i):
                    for k in range(KD):
                        for s in range(NS):
                            ins = mm(bank(4, 2)[:, k * 128:k * 128 + 128], htm[:, s, k * 128:k * 128 + 128],
                                     S[:, s, bass.ds(i * 128, 128)], start=(s == 0), stop=(s == 1))
                    ins.then_inc(q["m_xg"], 1)

                def pair(i, first=False, last=False):
                    pe.wait_ge(q["a_xg"], i + (n0 + 1))
                    pe.wait_ge(q["d_xg"], i + (n0 + 1))
                    for w in range(2):
                        for e in range(2):
                            arrived(pe, n + 2 * w + e, i)
                        for k in range(KD):
                            for e in range(2):
                                ins = mm(bank(4 + w)[e * 64:e * 64 + 64, :], xg[:, k, e * 64:e * 64 + 64],
                                         unit(n + 2 * w + e)[:, k, :], start=(k == 0), stop=(k == KD - 1))
                                if k == KD - 1:
                                    used(ins, n + 2 * w + e)
                    if first:
                        turn_gates()
                        pe.wait_ge(q["a_mod"], [16, 24][l])
                    for f in range(KF):
                        if f % 2 == 0:
                            pe.wait_ge(q["d_hid"], i * 2 + (n2 + f // 2 + 1))
                        c = (f % 2) * 128
                        ins = tr(bank(6 + f // 2)[:, c:c + 128], M["hid"][:, f * 128:f * 128 + 128], ident)
                    ins.then_inc(q["m_hT"], 1)
                    pe.wait_ge(q["a_hT"], i + (n0 + 1))
                    pe.wait_ge(q["d_hT"], i + (n0 + 1))
                    for e in range(2):
                        arrived(pe, n + 4 + e, i)
                    for half in range(2):
                        for f in range(KF):
                            for e in range(2):
                                ins = mm(bank(6 + half)[e * 64:e * 64 + 64, :], hidT[:, f, e * 64:e * 64 + 64],
                                         down_unit(n + 4 + e)[:, f, half * 512:half * 512 + 512],
                                         start=(f == 0), stop=(f == KF - 1))
                                if half and f == KF - 1:
                                    used(ins, n + 4 + e)
                        if last and half == 0:
                            ins.then_inc(q["m_half"], 1)
                    if first:
                        pe.wait_ge(q["d_S"], 3 * l + 3)
                    if not last:
                        pack(i + 1)
                    if first:
                        pe.wait_ge(q["a_ST"], l + 1)
                        open_accumulators()
                    pe.wait_ge(q["a_y"], i + (n0 + 1))
                    if not last:
                        pe.wait_ge(q["d_y"], i + (n0 + 1))
                    for k in range(KD):
                        if last and k == 4:
                            ins.then_inc(q["m_add"], 1)
                            pe.wait_ge(q["d_y"], i + (n0 + 1))
                        ins = mm(bank(0, 4)[:, k * 256:k * 256 + 256], y[:, k * 128:k * 128 + 128],
                                 ST[:, bass.ds(i, 1), :].rearrange("p o c -> p (o c)"), start=False, stop=False,
                                 skip_group_check=True)
                    ins.then_inc(q["m_add" if last else "m_sc"], 1)

                pe.wait_ge(q["d_S"], 3 * l + 1)
                pe.wait_ge(q["a_htm"], l + 1)
                pack(0)
                pair(0, first=True)
                with pe.Fori(1, NPAIR - 1) as i:
                    pair(i)
                pair(NPAIR - 1, last=True)
                pe.wait_ge(q["d_flag"], l + 1)
                more = pe.value_load(flag[0:1, l:l + 1])
                u0 = n + 6 * NPAIR
                with pe.If(more > 0):
                    pe.wait_ge(q["m_add"], 2 * l + 2)
                    with pe.Fori(0, NE) as e:
                        pe.wait_ge(fb["fb_in"][l], e * 48 + 48)
                        for s in range(NS):
                            for w in range(2):
                                for k in range(KD):
                                    ins = mm(bank(4 + w), hT[:, k, s, :], unit(u0 + w)[:, k, :], start=(k == 0), stop=(k == KD - 1))
                            ins.then_inc(fb["fb_gate"][l], 1)
                            pe.wait_ge(fb["fb_hid"][l], e * 2 + (s + 1))
                            for f in range(KF):
                                ins = tr(bank(6)[:, f * 128:f * 128 + 128], M["fh"][:, f * 128:f * 128 + 128], ident)
                            ins.then_inc(fb["fb_tr"][l], 1)
                            pe.wait_ge(fb["fb_hidT"][l], e * 2 + (s + 1))
                            for k in range(KD):
                                for f in range(KF):
                                    ins = mm(bank(0, 2)[:, k * 128:k * 128 + 128],
                                             down_unit(u0 + 2)[:, f, k * 128:k * 128 + 128],
                                             M["fhT"][:, f * 128:f * 128 + 128], start=(f == 0), stop=(f == KF - 1))
                            ins.then_inc(fb["fb_down"][l], 1)
                            pe.wait_ge(fb["fb_done"][l], e * 2 + (s + 2))

            moe(0)
            mod_row(16)
            norm(2)
            mod_col(16)
            mod_row(17)
            mod_col(17)
            mod_row(18)
            z4 = H["zz"].rearrange("p (k s t) -> p k s t", k=KD, s=NS)
            for j in range(24):
                n = HYIN_AT + j // 4 + (j >= 16)
                if j % 4 == 0:
                    arrived(pe, n)
                if j == 3:
                    pe.wait_ge(q["a_sqrt"], 3)
                if j >= 4:
                    pe.wait_ge(q["a_u"], j - 3)
                if j == 2:
                    mod_col(18)
                    pe.wait_ge(q["a_mod"], 19)
                for k in KORDER:
                    if j == 0:
                        h_ready(2, k)
                    ins = mm(bank(4 + j % 4)[:, 0:256], unit(n)[:, k, (j % 4) * 128:(j % 4) * 128 + 128], hk(k),
                             start=(k == KORDER[0]), stop=(k == KORDER[-1]))
                if j % 4 == 3:
                    used(ins, n)
                else:
                    ins.then_inc(q["t_u"], 1)
                if j in (16, 17):
                    s = j - 16
                    if s:
                        pe.wait_ge(q["a_mod"], 20)
                    else:
                        mod_row(19)
                    pe.wait_ge(q["d_zz"], KD)
                    for k in range(KD):
                        ins = tr(bank(2 * s, 2)[:, k * 128:k * 128 + 128], z4[:, k, s, :], ident)
                    ins.then_inc(q["t_zt"], 1)
                    if s == 0:
                        mod_col(19)
                if j in (18, 21):
                    s = (j - 18) // 3
                    pe.wait_ge(q["a_zt"], 2)
                    if s:
                        pe.wait_ge(q["a_spec"], 2)
                    for part, nm in enumerate(["fa", "fb"]):
                        for half in range(2):
                            ins = mm(bank(2 * part + half), HC(nm), H["zt"][:, s * 1024 + half * 512:s * 1024 + half * 512 + 512],
                                     start=True, stop=True)
                    ins.then_inc(q["t_spec"], 1)
            for s in range(NS):
                pe.wait_ge(q["d_spec"], s + 1)
                if s == 0:
                    pe.wait_ge(q["a_u"], 22)
                else:
                    pe.wait_ge(q["a_u"], 24)
                for k in range(KD):
                    o = bank(4 + 2 * s, 2)[:, k * 128:k * 128 + 128]
                    mm(o, YS[s][0][:, k * 128:k * 128 + 128], HC("ga"), start=True, stop=False)
                    ins = mm(o, YS[s][1][:, k * 128:k * 128 + 128], HC("gb"), start=False, stop=True)
                ins.then_inc(q["t_y"], 1)
            mod_row(20)

            def mod_step(k8):
                if k8 == 0:
                    mod_col(20)
                if k8 == 5:
                    pe.wait_ge(q["a_mod"], 21)

            pe.wait_ge(q["d_r"], 2)
            out_projection(OUT1_AT, [0, 1, 2, 3], lambda k: H["x0"][:, k * 256:k * 256 + 256], mod_step)
            moe(1)
            for half in range(2):
                pe.wait_ge(q["d_x"], 7 + half)
                for s in range(NS):
                    for k in range(4):
                        ins = tr(bank(4 + 2 * half + s)[:, k * 128:k * 128 + 128], xT[:, 4 * half + k, s, :], ident)
                ins.then_inc(q["t_fin"], 1)


_INS = ['x_prompt', 'x_sample', 'cache_k', 'cache_v', 'state_hgrn', 'c', 'c_ctx', 'norm_g', 'mod_w', 'mod_b',
        'ab_in_w', 'hgrn_lb', 'hgrn_onorm_g', 'attn_qnorm_g', 'attn_knorm_g', 'ab_out_w',
        'hy_in_w', 'hy_in_b', 'hy_conv_w', 'hy_conv_b', 'hy_f_w1', 'hy_f_b1', 'hy_f_w2', 'hy_f_b2',
        'hy_f_w3', 'hy_f_freq', 'hy_dskip', 'hy_out_w', 'router_w', 'router_b',
        'moe_w_gate', 'moe_w_up', 'moe_w_down']
_OUTS = [("y_prompt", (1, T, D)), ("y_sample", (1, T, D)), ("new_cache_k", (1, 1, KV, T, HD)),
         ("new_cache_v", (1, 1, KV, T, HD)), ("new_state", (1, 1, 2, HA, 128, 128))]


def kernel(**inputs):
    import concourse.bacc as _bacc
    from concourse.bass_utils import run_bass_kernel_spmd as _run

    nc = _bacc.Bacc("TRN2", target_bir_lowering=False, num_devices=1)
    arrays, ins, outs = {}, {}, {}
    for name in _INS:
        a = np.ascontiguousarray(inputs[name])
        arrays[f"in_{name}"] = a
        ins[name] = nc.dram_tensor(f"in_{name}", a.shape, F32, kind="ExternalInput").ap()
    for name, a in zip(["cst", "hyc"], shape_constants()):
        arrays[f"in_{name}"] = a
        ins[name] = nc.dram_tensor(f"in_{name}", a.shape, F32, kind="ExternalInput").ap()
    for name, shape in _OUTS:
        outs[name] = nc.dram_tensor(f"out_{name}", shape, F32, kind="ExternalOutput").ap()
    build(nc, ins, outs)
    r = _run(nc, [arrays], core_ids=[0])
    return tuple(r.results[0][f"out_{name}"] for name, _ in _OUTS)
```
